# Optimizing a Trainium2 kernel written in Bass

```python
import jax, jax.numpy as jnp
from jax import lax
import numpy as np

D_MODEL = 1024
BATCH = 1
SEQ = 1024
DEPTH = 2
DEC_BATCH = 8
DEC_SEQ = 8
PAST_LEN = 2048
PAGE_SIZE = 128

HEAD_DIM = 64
N_HEADS_A = 8
N_KV_A = 2
N_HEADS_B = 8
N_KV_B = 8
N_ATTN_HEADS = N_HEADS_A + N_HEADS_B
WINDOW_A = 128
DILATED_BRANCHES = ((128, 1), (512, 4), (2048, 16))
WINDOW_B = 2048
BLK = 128
POOL_WINDOWS = (2, 4, 8, 16)
N_POOL_GROUPS = 4
POOL_GROUP = D_MODEL // N_POOL_GROUPS
POOL_CTX = 15
D_FF = 4 * D_MODEL
N_ATTN_LAYERS = (DEPTH + 1) // 2
N_POOL_LAYERS = DEPTH // 2
RMS_EPS = 1e-6
NEG = -1e30
Q_A = N_HEADS_A * HEAD_DIM
Q_B = N_HEADS_B * HEAD_DIM
KV_A_W = N_KV_A * HEAD_DIM
KV_B_W = N_KV_B * HEAD_DIM
D_IN = Q_A + Q_B + 2 * KV_A_W + 2 * KV_B_W
D_MIX = Q_A + Q_B

kernel_name = "hybrid_swa_sink_dilated_pool_decoder_step"

def _rms(x, g):
    xf = x.astype(jnp.float32)
    y = xf * lax.rsqrt(jnp.mean(xf * xf, axis=-1, keepdims=True) + RMS_EPS)
    return (y * g.astype(jnp.float32)).astype(x.dtype)

def _alibi_slopes():
    return jnp.exp2(-8.0 * jnp.arange(1, N_ATTN_HEADS + 1, dtype=jnp.float32) / N_ATTN_HEADS)

def _softmax_stats(s, sink):
    m = jnp.max(s, axis=-1)
    if sink is not None:
        m = jnp.maximum(m, sink)
    p = jnp.exp(s - m[..., None])
    den = jnp.sum(p, axis=-1)
    if sink is not None:
        den = den + jnp.exp(sink - m)
    return p, m, den

def _band_attend(q, k, v, slopes, dil, steps, sinks=None):
    n, L, H, hd = q.shape
    kvh = k.shape[2]
    g = H // kvh
    lp = -(-L // BLK) * BLK
    nb = lp // BLK
    pad = ((0, 0), (0, lp - L), (0, 0), (0, 0))
    qb = jnp.pad(q, pad).reshape(n, nb, BLK, kvh, g, hd)

    def blocks_with_prev(t):
        tb = jnp.pad(t, pad).reshape(n, nb, BLK, kvh, hd)
        prev = jnp.pad(tb, ((0, 0), (1, 0), (0, 0), (0, 0), (0, 0)))[:, :nb]
        return jnp.concatenate([prev, tb], axis=2)

    kc = blocks_with_prev(k)
    vc = blocks_with_prev(v)
    s = jnp.einsum('nbqcgd,nbscd->nbcgqs', qb, kc, preferred_element_type=jnp.float32) * (hd ** -0.5)
    dist = (BLK + jnp.arange(BLK))[:, None] - jnp.arange(2 * BLK)[None, :]
    kidx = jnp.arange(nb)[:, None] * BLK - BLK + jnp.arange(2 * BLK)[None, :]
    mask = ((dist >= 0) & (dist <= steps))[None] & (kidx >= 0)[:, None, :]
    bias = -slopes.reshape(kvh, g)[:, :, None, None] * (dil * dist).astype(jnp.float32)
    s = jnp.where(mask[:, None, None], s + bias, NEG)
    sink = None if sinks is None else sinks.astype(jnp.float32).reshape(kvh, g)[:, :, None]
    p, m, den = _softmax_stats(s, sink)
    o = jnp.einsum('nbcgqs,nbscd->nbqcgd', p.astype(vc.dtype), vc, preferred_element_type=jnp.float32)
    o = o / jnp.transpose(den, (0, 1, 4, 2, 3))[..., None]
    o = o.reshape(n, lp, H, hd)[:, :L].astype(q.dtype)
    lse = jnp.transpose(m + jnp.log(den), (0, 1, 4, 2, 3)).reshape(n, lp, H)[:, :L]
    return o, lse

def _gather_attend(q, kcat, vcat, base, slopes, dil, steps, sinks=None):
    n, t, H, hd = q.shape
    kvh = kcat.shape[2]
    g = H // kvh
    slot = jnp.arange(steps + 1)
    idx = base + jnp.arange(t)[:, None] - dil * slot[None, :]
    valid = idx >= 0
    idx = jnp.maximum(idx, 0)
    kg = kcat[:, idx]
    vg = vcat[:, idx]
    qg = q.reshape(n, t, kvh, g, hd)
    s = jnp.einsum('ntcgd,ntjcd->ntcgj', qg, kg, preferred_element_type=jnp.float32) * (hd ** -0.5)
    bias = -slopes.reshape(kvh, g)[:, :, None] * (dil * slot).astype(jnp.float32)
    s = jnp.where(valid[:, None, None, :], s + bias, NEG)
    sink = None if sinks is None else sinks.astype(jnp.float32).reshape(kvh, g)
    p, m, den = _softmax_stats(s, sink)
    o = jnp.einsum('ntcgj,ntjcd->ntcgd', p.astype(vg.dtype), vg, preferred_element_type=jnp.float32)
    o = (o / den[..., None]).reshape(n, t, H, hd).astype(q.dtype)
    return o, (m + jnp.log(den)).reshape(n, t, H)

def _combine_branches(outs, lses, dtype):
    w = jax.nn.softmax(jnp.stack(lses, axis=0), axis=0)
    o = jnp.einsum('rnth,rnthd->nthd', w, jnp.stack(outs, axis=0).astype(jnp.float32))
    return o.astype(dtype)

def _attn_project(h, w_in):
    n, t, _ = h.shape
    z = h @ w_in
    qa, qb, ka, va, kb, vb = jnp.split(
        z, [Q_A, Q_A + Q_B, Q_A + Q_B + KV_A_W, Q_A + Q_B + 2 * KV_A_W, Q_A + Q_B + 2 * KV_A_W + KV_B_W], axis=-1)
    qa = qa.reshape(n, t, N_HEADS_A, HEAD_DIM)
    qb = qb.reshape(n, t, N_HEADS_B, HEAD_DIM)
    ka = ka.reshape(n, t, N_KV_A, HEAD_DIM)
    va = va.reshape(n, t, N_KV_A, HEAD_DIM)
    kb = kb.reshape(n, t, N_KV_B, HEAD_DIM)
    vb = vb.reshape(n, t, N_KV_B, HEAD_DIM)
    return qa, ka, va, qb, kb, vb

def _attn_mixer_prompt(h, w_in, w_out, sinks, slopes):
    n, s_len, _ = h.shape
    qa, ka, va, qb, kb, vb = _attn_project(h, w_in)
    oa, _ = _band_attend(qa, ka, va, slopes[:N_HEADS_A], 1, WINDOW_A, sinks)
    outs, lses = [], []
    for w, d in DILATED_BRANCHES:
        L = s_len // d

        def to_res(a):
            return a.reshape(n, L, d, a.shape[2], HEAD_DIM).swapaxes(1, 2).reshape(n * d, L, a.shape[2], HEAD_DIM)

        o, lse = _band_attend(to_res(qb), to_res(kb), to_res(vb), slopes[N_HEADS_A:], d, w // d)
        outs.append(o.reshape(n, d, L, N_HEADS_B, HEAD_DIM).swapaxes(1, 2).reshape(n, s_len, N_HEADS_B, HEAD_DIM))
        lses.append(lse.reshape(n, d, L, N_HEADS_B).swapaxes(1, 2).reshape(n, s_len, N_HEADS_B))
    ob = _combine_branches(outs, lses, h.dtype)
    y = jnp.concatenate([oa.reshape(n, s_len, Q_A), ob.reshape(n, s_len, Q_B)], axis=-1) @ w_out
    return y, ka, va, kb, vb

def _attn_mixer_sample(h, ka_buf, va_buf, kb_buf, vb_buf, w_in, w_out, sinks, slopes):
    n, t, _ = h.shape
    qa, ka, va, qb, kb, vb = _attn_project(h, w_in)
    kac = jnp.concatenate([ka_buf.astype(ka.dtype), ka], axis=1)
    vac = jnp.concatenate([va_buf.astype(va.dtype), va], axis=1)
    oa, _ = _gather_attend(qa, kac, vac, ka_buf.shape[1], slopes[:N_HEADS_A], 1, WINDOW_A, sinks)
    kbc = jnp.concatenate([kb_buf.astype(kb.dtype), kb], axis=1)
    vbc = jnp.concatenate([vb_buf.astype(vb.dtype), vb], axis=1)
    outs, lses = [], []
    for w, d in DILATED_BRANCHES:
        o, lse = _gather_attend(qb, kbc, vbc, kb_buf.shape[1], slopes[N_HEADS_A:], d, w // d)
        outs.append(o)
        lses.append(lse)
    ob = _combine_branches(outs, lses, h.dtype)
    y = jnp.concatenate([oa.reshape(n, t, Q_A), ob.reshape(n, t, Q_B)], axis=-1) @ w_out
    return y, ka, va, kb, vb

def _pool_mixer(h_ctx, h, w_pool, pool_scale):
    n, t, _ = h.shape
    c = h_ctx.shape[1]
    he = jnp.concatenate([h_ctx.astype(jnp.float32), h.astype(jnp.float32)], axis=1)
    cs = jnp.pad(jnp.cumsum(he, axis=1), ((0, 0), (1, 0), (0, 0)))
    hi = c + 1 + jnp.arange(t)
    ys = []
    for gi, w in enumerate(POOL_WINDOWS):
        lo = jnp.maximum(hi - w, 0)
        csg = cs[:, :, gi * POOL_GROUP:(gi + 1) * POOL_GROUP]
        mean = (csg[:, hi] - csg[:, lo]) / (hi - lo).astype(jnp.float32)[:, None]
        ys.append(mean - h[:, :, gi * POOL_GROUP:(gi + 1) * POOL_GROUP].astype(jnp.float32))
    y = jnp.stack(ys, axis=2).astype(h.dtype)
    z = jnp.einsum('ntgc,gce->ntge', y, w_pool).reshape(n, t, D_MODEL)
    return z * pool_scale

def _sq_relu_mlp(x, w1, w2):
    return jnp.square(jax.nn.relu(x @ w1)) @ w2

def setup_inputs(seed: int = 0) -> dict:
    key = jax.random.key(seed)
    ks = jax.random.split(key, 16)
    nrm = jax.random.normal
    f32 = jnp.float32
    buf_a = min(WINDOW_A, PAST_LEN)
    buf_b = min(WINDOW_B, PAST_LEN)
    return {
        'x_prompt': nrm(ks[0], (BATCH, SEQ, D_MODEL), f32),
        'x_sample': nrm(ks[1], (DEC_BATCH, DEC_SEQ, D_MODEL), f32),
        'cache_a_k': nrm(ks[2], (N_ATTN_LAYERS, DEC_BATCH, buf_a, N_KV_A, HEAD_DIM), f32),
        'cache_a_v': nrm(ks[3], (N_ATTN_LAYERS, DEC_BATCH, buf_a, N_KV_A, HEAD_DIM), f32),
        'cache_b_k': nrm(ks[4], (N_ATTN_LAYERS, DEC_BATCH, buf_b, N_KV_B, HEAD_DIM), f32),
        'cache_b_v': nrm(ks[5], (N_ATTN_LAYERS, DEC_BATCH, buf_b, N_KV_B, HEAD_DIM), f32),
        'state_pool': nrm(ks[6], (N_POOL_LAYERS, DEC_BATCH, POOL_CTX, D_MODEL), f32),
        'norm_g': 1.0 + 0.05 * nrm(ks[7], (DEPTH, 4, D_MODEL), f32),
        'attn_w_in': nrm(ks[8], (N_ATTN_LAYERS, D_MODEL, D_IN), f32) * D_MODEL ** -0.5,
        'attn_w_out': nrm(ks[9], (N_ATTN_LAYERS, D_MIX, D_MODEL), f32) * D_MIX ** -0.5,
        'attn_sinks': 0.5 * nrm(ks[10], (N_ATTN_LAYERS, N_HEADS_A), f32),
        'pool_w': nrm(ks[11], (N_POOL_LAYERS, N_POOL_GROUPS, POOL_GROUP, POOL_GROUP), f32) * POOL_GROUP ** -0.5,
        'pool_scale': 1.0 + 0.1 * nrm(ks[12], (N_POOL_LAYERS, D_MODEL), f32),
        'mlp_w1': nrm(ks[13], (DEPTH, D_MODEL, D_FF), f32) * D_MODEL ** -0.5,
        'mlp_w2': nrm(ks[14], (DEPTH, D_FF, D_MODEL), f32) * D_FF ** -0.5,
    }

def reference(x_prompt, x_sample, cache_a_k, cache_a_v, cache_b_k, cache_b_v, state_pool,
              norm_g, attn_w_in, attn_w_out, attn_sinks, pool_w, pool_scale, mlp_w1, mlp_w2):
    slopes = _alibi_slopes()
    xp, xs = x_prompt, x_sample
    pa_k, pa_v, pb_k, pb_v, p_pool = [], [], [], [], []
    sa_k, sa_v, sb_k, sb_v, s_pool = [], [], [], [], []
    for l in range(DEPTH):
        gl = norm_g[l]
        i = l // 2
        hp = _rms(xp, gl[0])
        hs = _rms(xs, gl[0])
        if l % 2 == 0:
            mp, ka, va, kb, vb = _attn_mixer_prompt(hp, attn_w_in[i], attn_w_out[i], attn_sinks[i], slopes)
            pa_k.append(ka[:, -WINDOW_A:])
            pa_v.append(va[:, -WINDOW_A:])
            pb_k.append(kb[:, -WINDOW_B:])
            pb_v.append(vb[:, -WINDOW_B:])
            ms, ka, va, kb, vb = _attn_mixer_sample(hs, cache_a_k[i], cache_a_v[i], cache_b_k[i], cache_b_v[i],
                                                    attn_w_in[i], attn_w_out[i], attn_sinks[i], slopes)
            sa_k.append(ka)
            sa_v.append(va)
            sb_k.append(kb)
            sb_v.append(vb)
        else:
            mp = _pool_mixer(hp[:, :0], hp, pool_w[i], pool_scale[i])
            p_pool.append(hp[:, -POOL_CTX:])
            ctx = state_pool[i].astype(hs.dtype)
            ms = _pool_mixer(ctx, hs, pool_w[i], pool_scale[i])
            s_pool.append(jnp.concatenate([ctx, hs], axis=1)[:, -POOL_CTX:])
        xp = xp + _rms(mp, gl[1])
        xs = xs + _rms(ms, gl[1])
        xp = xp + _rms(_sq_relu_mlp(_rms(xp, gl[2]), mlp_w1[l], mlp_w2[l]), gl[3])
        xs = xs + _rms(_sq_relu_mlp(_rms(xs, gl[2]), mlp_w1[l], mlp_w2[l]), gl[3])
    return (xp, xs,
            jnp.stack(pa_k), jnp.stack(pa_v), jnp.stack(pb_k), jnp.stack(pb_v), jnp.stack(p_pool),
            jnp.stack(sa_k), jnp.stack(sa_v), jnp.stack(sb_k), jnp.stack(sb_v), jnp.stack(s_pool))


_drawn_inputs = setup_inputs


def setup_inputs(seed=0):
    import zlib

    import numpy as np

    out = dict(_drawn_inputs(seed))
    spreads = {}
    factors = {}
    for name, (base, spread) in spreads.items():
        noise = np.random.default_rng([zlib.crc32(name.encode()), seed]).standard_normal(out[name].shape)
        drawn = base * np.exp(spread * noise) if base else spread * noise
        out[name] = __import__('jax').numpy.asarray(drawn.astype(out[name].dtype))
    for name, factor in factors.items():
        out[name] = (out[name] * factor).astype(out[name].dtype)
    return out
```

```python
from contextlib import ExitStack

import numpy as np

import concourse.bass as bass
from concourse import mybir

F32 = mybir.dt.float32
F32R = mybir.dt.float32r
ALU = mybir.AluOpType
ACT = mybir.ActivationFunctionType
AX = mybir.AxisListType

P = 128
D = 1024
KT = D // P
SEQ = 1024
NB = 8
NQ = 8
NS = NB * NQ
TOK = SEQ + NS
PT = SEQ // P
NT = PT + 1
TOKEN_CHUNKS = ((0, 384), (384, 384), (768, 320))
HD = 64
NH = 8
WINDOW_A = 128
PAST = 2048
DFF = 4 * D
FFB = 4
NBLK = DFF // (FFB * P)
CTX = 15
POOL_W = (2, 4, 8, 16)
EPS = 1e-6
NEG = -1e30
BRANCHES = ((128, 1), (512, 4), (2048, 16))
FAR = PAST - 512
FAR_TILES = FAR // 2 // P
NEAR_TILES = 512 // P
CT = FAR_TILES + NEAR_TILES
ST = CT + 3


def tile_start(t):
    return t * P if t < PT else TOK - P


def new_columns(t):
    return (slice(t * P, (t + 1) * P), slice(0, P)) if t < PT else (slice(SEQ, TOK), slice(P - NS, P))


def slope(n):
    return 2.0 ** (-8.0 * (n + 1) / 16)


def branch_bias(dist, n):
    count = sum(((dist >= 0) & (dist <= w) & (dist % d == 0)).astype(np.float64) for w, d in BRANCHES)
    return np.where(count > 0, np.log(np.maximum(count, 1)) - slope(n) * dist, NEG)


def window_bias(dist, n):
    return np.where((dist >= 0) & (dist <= WINDOW_A), -slope(n) * dist, NEG)


def shape_constants():
    q = np.arange(P)[:, None]
    prompt_a = np.stack([window_bias(P + q - np.arange(2 * P), h) for h in range(NH)], 1)
    prompt_b = np.stack([branch_bias(SEQ - P + q - np.arange(SEQ), NH + h) for h in range(NH)], 1)
    prompt = np.concatenate([np.maximum(x * 8, NEG).reshape(P, -1) for x in (prompt_a, prompt_b)], 1)

    rows = np.empty((CT, P), np.int64)
    p = np.arange(P)
    for t in range(FAR_TILES):
        rows[t] = 16 * (16 * t + p // 8) + p % 8
    for t in range(NEAR_TILES):
        rows[FAR_TILES + t] = FAR + t * P + p
    sample = np.full((P, ST, NH, NQ), NEG, np.float32)
    own = np.full((P, NB, 2, NH, NQ), NEG, np.float32)
    for h in range(NH):
        for i in range(NQ):
            for t in range(CT):
                sample[:, t, h, i] = branch_bias(PAST + i - rows[t], NH + h)
            sample[:, CT + 1, h, i] = window_bias(P + i - p, h)
            for b in range(NB):
                for j in range(NQ):
                    r = P - NS + b * NQ + j
                    own[r, b, 0, h, i] = branch_bias(np.array(i - j), NH + h)
                    own[r, b, 1, h, i] = window_bias(np.array(i - j), h)
    pool = np.zeros((P, 4, 3, P), np.float32)
    pool_own = np.zeros((P, 4, NS), np.float32)
    pool_ctx = np.zeros((NB * CTX, 4, NS), np.float32)
    for g, w in enumerate(POOL_W):
        for j in range(P):
            for k in range(max(0, j - w + 1), j + 1):
                pool[k, g, 0, j] += 1.0 / min(w, j + 1)
            for k in range(j - w + 1, j + 1):
                if k >= 0:
                    pool[k, g, 1, j] += 1.0 / w
                else:
                    pool[P + k, g, 2, j] += 1.0 / w
            pool[j, g, 0, j] -= 1
            pool[j, g, 1, j] -= 1
        for b in range(NB):
            for i in range(NQ):
                for k in range(i - w + 1, i + 1):
                    if k >= 0:
                        pool_own[P - NS + b * NQ + k, g, b * NQ + i] += 1.0 / w
                    else:
                        pool_ctx[b * CTX + CTX + k, g, b * NQ + i] += 1.0 / w
                pool_own[P - NS + b * NQ + i, g, b * NQ + i] -= 1
    return {
        "identity": np.eye(P, dtype=np.float32),
        "prompt_bias": prompt.astype(np.float32),
        "sample_bias": sample.reshape(P, -1),
        "own_bias": own.reshape(P, -1),
        "pool_band": pool.reshape(P, -1),
        "pool_own": pool_own.reshape(P, -1),
        "pool_ctx": pool_ctx.reshape(NB * CTX, -1),
    }


class Core:

    def __init__(self, nc, ctx):
        self.nc, self.ctx = nc, ctx
        self.stage_sems = []
        self.ps = ctx.enter_context(nc.psum_tensor("ps", [P, 8, 512], F32))
        self.identity = self.sb("identity", [P, P])
        self.ones = self.sb("ones", [P, P])
        self.minus_half = self.sb("minus_half", [P, 1])
        self.sample_oT = self.sb("sample_oT", [P, KT, NS])

    def sb(self, name, shape, dt=F32, ctx=None):
        return (ctx or self.ctx).enter_context(self.nc.sbuf_tensor(name, shape, dt))

    def sem(self, name):
        self.stage_sems.append(self.nc.alloc_semaphore(name=name))
        return self.stage_sems[-1]

    def end_stage(self):
        self.nc.clear_and_free_semaphores(self.stage_sems)
        self.stage_sems = []
        self.nc.all_engine_barrier()

    def banks(self, first, n, width=512):
        return self.ps[:, first:first + n, :].rearrange("p a b -> p (a b)")[:, 0:n * 512 if width == 512 else width]


def token_rows(prompt, sample, t):
    if t < PT:
        return [(slice(0, P), prompt[t * P:(t + 1) * P, :])]
    return [(slice(0, P - NS), prompt[SEQ - (P - NS):SEQ, :]), (slice(P - NS, P), sample[0:NS, :])]


def stored_rows(prompt, sample, t):
    return token_rows(prompt, sample, t) if t < PT else token_rows(prompt, sample, t)[1:]


def start(core, constants):
    nc = core.nc
    const_in = core.sem("const_in")
    with nc.Block() as block:
        @block.sync
        def _(sp):
            sp.dma_start(core.identity[:], constants["identity"]).then_inc(const_in, 16)
            sp.wait_ge(const_in, 16)

        @block.vector
        def _(dve):
            nc.vector.memset(core.ones[:], 1.0)
            nc.vector.memset(core.minus_half[:], -0.5)


def root(core, pool, ms, rstd, shifted, ready, t):
    nc = core.nc
    col = slice(t, t + 1)
    nc.gpsimd.tensor_scalar(ms[:, col], ms[:, col], EPS, None, ALU.add).then_inc(shifted, 1)
    pool.wait_ge(shifted, t + 1)
    nc.gpsimd.tensor_tensor(rstd[:, col], ms[:, col], core.minus_half[:], ALU.pow).then_inc(ready, 1)


def prepare(core, tag, x_prompt, x_sample, gain, xT_hi, xT_lo):
    nc = core.nc
    xs = 3
    with ExitStack() as mem:
        x = core.sb(tag + "x", [P, xs, D], F32, mem)
        xn = core.sb(tag + "xn", [P, 2, D], F32, mem)
        gain_b = core.sb(tag + "gain", [P, D], F32, mem)
        junk = core.sb(tag + "junk", [P, D], F32, mem)
        ms = core.sb(tag + "ms", [P, NT], F32, mem)
        rstd = core.sb(tag + "rstd", [P, NT], F32, mem)
        x_in = [core.sem(f"{tag}x_in{s}") for s in range(xs)]
        gain_in = core.sem(tag + "gain_in")
        squared = core.sem(tag + "squared")
        ms_shifted = core.sem(tag + "ms_shifted")
        rstd_ready = core.sem(tag + "rstd_ready")
        normed = core.sem(tag + "normed")
        turned = core.sem(tag + "turned")
        hi_done = core.sem(tag + "hi_done")
        lo_done = core.sem(tag + "lo_done")
        turned_ps = [core.banks(2 * i, 2).rearrange("p (k c) -> p k c", k=KT) for i in range(2)]

        with nc.Block() as block:
            @block.sync
            def _(sp):
                sp.dma_start(gain_b[:], gain.partition_broadcast(P)).then_inc(gain_in, 16)
                for t in range(NT):
                    if t >= xs:
                        sp.wait_ge(normed, t - xs + 1)
                    for rows, src in token_rows(x_prompt, x_sample, t):
                        sp.dma_start(x[rows, t % xs, :], src).then_inc(x_in[t % xs], 16)

            @block.scalar
            def _(act):
                def take_hi(t):
                    act.wait_ge(turned, t + 1)
                    c, new = new_columns(t)
                    nc.scalar.activation(xT_hi[:, :, c], turned_ps[t % 2][:, :, new], ACT.Copy).then_inc(hi_done, 1)

                for t in range(NT):
                    act.wait_ge(x_in[t % xs], 16 * (t // xs + 1 + (t == PT)))
                    if t >= 1:
                        act.wait_ge(squared, t)
                    nc.scalar.activation(junk[:], x[:, t % xs, :], ACT.Square, scale=1.0 / 32,
                                         accum_out=ms[:, t:t + 1]).then_inc(squared, 1)
                    if t >= 1:
                        take_hi(t - 1)
                take_hi(NT - 1)

            @block.gpsimd
            def _(pool):
                for t in range(NT):
                    pool.wait_ge(squared, t + 1)
                    root(core, pool, ms, rstd, ms_shifted, rstd_ready, t)

            @block.vector
            def _(dve):
                def take_lo(t):
                    dve.wait_ge(hi_done, t + 1)
                    c, new = new_columns(t)
                    nc.vector.tensor_tensor(xT_lo[:, :, c], turned_ps[t % 2][:, :, new],
                                            xT_hi[:, :, c].bitcast(F32), ALU.subtract).then_inc(lo_done, 1)

                for t in range(NT):
                    dve.wait_ge(rstd_ready, t + 1)
                    if t == 0:
                        dve.wait_ge(gain_in, 16)
                    if t >= 2:
                        dve.wait_ge(turned, t - 1)
                    nc.vector.scalar_tensor_tensor(xn[:, t % 2, :], x[:, t % xs, :], rstd[:, t:t + 1], gain_b[:],
                                                   ALU.mult, ALU.mult).then_inc(normed, 1)
                    if t >= 1:
                        take_lo(t - 1)
                take_lo(NT - 1)

            @block.tensor
            def _(pe):
                for t in range(NT):
                    pe.wait_ge(normed, t + 1)
                    if t >= 2:
                        pe.wait_ge(lo_done, t - 1)
                    for k in range(KT):
                        last = nc.tensor.transpose(turned_ps[t % 2][:, k, :], xn[:, t % 2, k * P:(k + 1) * P],
                                                   core.identity[:])
                    last.then_inc(turned, 1)


def in_project(core, w_in, xT_hi, xT_lo, qT, kaT, kbT, v, outs):
    nc = core.nc
    W = 256
    chunks = [4, 5, 6, 7, 8, 0, 1, 2, 3]
    NKV, NK = 5, 3
    w_rows = w_in.rearrange("(k p) n -> p k n", p=P)
    with ExitStack() as mem:
        raw = core.sb("in_raw", [P, 2, KT, W], F32, mem)
        w_hi = core.sb("in_w_hi", [P, 2, KT, W], F32R, mem)
        w_lo = core.sb("in_w_lo", [P, 2, KT, W], F32R, mem)
        ks = 3
        k_rows = core.sb("k_rows", [P, ks, W], F32, mem)
        raw_in = [core.sem(f"in_raw_in{s}") for s in range(2)]
        hi_done = core.sem("in_hi_done")
        lo_done = core.sem("in_lo_done")
        kv_ready = core.sem("in_kv_ready")
        kv_taken = core.sem("in_kv_taken")
        k_stored = [core.sem(f"in_k_stored{s}") for s in range(ks)]
        k_turned = core.sem("in_k_turned")
        kT_taken = core.sem("in_kT_taken")
        q_ready = core.sem("in_q_ready")
        q_taken = core.sem("in_q_taken")
        v_stored = core.sem("in_v_stored")

        def k_store(n, t):
            rows = slice(0, P) if t < PT else slice(P - NS, P)
            if n == 0:
                if t < PT - 1:
                    return None
                return (outs["prompt_a_k"] if t < PT else outs["sample_a_k"])[:, :], rows, slice(0, P)
            c = (n - 1) * W
            dst = outs["prompt_b_k"][t * P:(t + 1) * P, c:c + W] if t < PT else outs["sample_b_k"][:, c:c + W]
            return dst, rows, slice(0, W)

        stored_before = {}
        count = [0] * ks
        for i in range(NK * NT):
            stored_before[i] = count[i % ks]
            count[i % ks] += k_store(i // NT, i % NT) is not None

        arrived = [16 * sum(4 if chunks[j] < 2 else 1 for j in range(n % 2, n + 1, 2)) for n in range(len(chunks))]

        with nc.Block() as block:
            @block.sync
            def _(sp):
                for n, c in enumerate(chunks):
                    if n >= 2:
                        sp.wait_ge(lo_done, n - 1)
                    if c >= 2:
                        sp.dma_start(raw[:, n % 2], w_rows[:, :, c * W:(c + 1) * W]).then_inc(raw_in[n % 2], 16)
                        continue
                    for j in range(2):
                        for half in range(2):
                            src = half * W + (2 * c + j) * HD
                            dst = (2 * j + half) * HD
                            sp.dma_start(raw[:, n % 2, :, dst:dst + HD],
                                         w_rows[:, :, src:src + HD]).then_inc(raw_in[n % 2], 16)

            @block.gpsimd
            def _(pool):
                for i in range(NK * NT):
                    n, t = divmod(i, NT)
                    if (piece := k_store(n, t)) is not None:
                        dst, rows, cols = piece
                        pool.wait_ge(kv_taken, i + 1)
                        pool.dma_start(dst, k_rows[rows, i % ks, cols]).then_inc(k_stored[i % ks], 16)
                pool.wait_ge(kv_taken, NKV * NT)
                pool.dma_start(outs["prompt_b_v"].rearrange("(t p) n -> p t n", p=P),
                               v[:, 0:PT, P:]).then_inc(v_stored, 16)
                pool.dma_start(outs["prompt_a_v"], v[:, PT - 1, 0:P]).then_inc(v_stored, 16)
                pool.dma_start(outs["sample_b_v"], v[P - NS:P, PT, P:]).then_inc(v_stored, 16)
                pool.dma_start(outs["sample_a_v"], v[P - NS:P, PT, 0:P]).then_inc(v_stored, 16)
                pool.wait_ge(v_stored, 64)
                for s in range(ks):
                    pool.wait_ge(k_stored[s], 16 * count[s])

            @block.scalar
            def _(act):
                def split(n):
                    act.wait_ge(raw_in[n % 2], arrived[n])
                    if 2 <= n < NKV + 2:
                        act.wait_ge(kv_ready, NT * (n - 1))
                    elif n >= NKV + 2:
                        act.wait_ge(q_ready, 2 * (n - 1 - NKV))
                    nc.scalar.activation(w_hi[:, n % 2], raw[:, n % 2], ACT.Copy).then_inc(hi_done, 1)

                split(0)
                split(1)
                for n in range(NKV):
                    for t in range(NT):
                        i = n * NT + t
                        act.wait_ge(kv_ready, i + 1)
                        got = core.ps[:, 6 + i % 2, 0:W]
                        if n < NK:
                            if i >= ks:
                                act.wait_ge(k_turned, i - ks + 1)
                                if stored_before[i]:
                                    act.wait_ge(k_stored[i % ks], 16 * stored_before[i])
                            op = nc.scalar.activation(k_rows[:, i % ks, :], got, ACT.Copy)
                            if n == 0:
                                op = nc.scalar.activation(v[:, t, 0:P], got[:, P:W], ACT.Copy)
                        else:
                            c = P + (n - NK) * W
                            op = nc.scalar.activation(v[:, t, c:c + W], got, ACT.Copy)
                        op.then_inc(kv_taken, 1)
                    if n + 2 < len(chunks):
                        split(n + 2)
                for m in range(KT):
                    act.wait_ge(q_ready, m + 1)
                    for j, (c, w) in enumerate(TOKEN_CHUNKS):
                        op = nc.scalar.activation(qT[:, m, c:c + w], core.ps[:, 3 * (m % 2) + j, 0:w], ACT.Copy)
                    op.then_inc(q_taken, 1)
                    n = NKV + m // 2 + 2
                    if m % 2 == 1 and n < len(chunks):
                        split(n)

            @block.vector
            def _(dve):
                def lo(n):
                    dve.wait_ge(hi_done, n + 1)
                    nc.vector.tensor_tensor(w_lo[:, n % 2], raw[:, n % 2], w_hi[:, n % 2].bitcast(F32),
                                            ALU.subtract).then_inc(lo_done, 1)

                lo(0)
                lo(1)
                for n in range(NK):
                    for t in range(NT):
                        i = n * NT + t
                        dve.wait_ge(k_turned, i + 1)
                        c, new = new_columns(t)
                        if n == 0:
                            op = nc.vector.tensor_copy(kaT[:, c], core.ps[:, i % 2, new])
                        else:
                            j = 2 * (n - 1)
                            op = nc.vector.tensor_copy(kbT[:, j:j + 2, c], core.ps[:, i % 2, 0:W].rearrange(
                                "p (j c) -> p j c", j=2)[:, :, new])
                        op.then_inc(kT_taken, 1)
                    lo(n + 2)
                for n in range(NK + 2, len(chunks)):
                    lo(n)

            @block.tensor
            def _(pe):
                def turn(i):
                    n = i // NT
                    pe.wait_ge(kv_taken, i + 1)
                    if i >= 2:
                        pe.wait_ge(kT_taken, i - 1)
                    for j in range(1 if n == 0 else 2):
                        last = nc.tensor.transpose(core.ps[:, i % 2, j * P:(j + 1) * P],
                                                   k_rows[:, i % ks, j * P:(j + 1) * P], core.identity[:])
                    last.then_inc(k_turned, 1)

                for n in range(NKV):
                    pe.wait_ge(lo_done, n + 1)
                    for t in range(NT):
                        i = n * NT + t
                        if i >= 2:
                            pe.wait_ge(kv_taken, i - 1)
                        c = tile_start(t)
                        for k in range(KT):
                            for a, b in ((xT_hi, w_hi), (xT_hi, w_lo), (xT_lo, w_hi)):
                                last = nc.tensor.matmul(core.ps[:, 6 + i % 2, 0:W], a[:, k, c:c + P], b[:, n % 2, k, :],
                                                        start=(k == 0 and b is w_hi and a is xT_hi),
                                                        stop=(k == KT - 1 and a is xT_lo))
                        last.then_inc(kv_ready, 1)
                        if 1 <= i <= NK * NT:
                            turn(i - 1)
                for m in range(KT):
                    n = NKV + m // 2
                    pe.wait_ge(lo_done, n + 1)
                    if m == 0:
                        pe.wait_ge(kT_taken, NK * NT)
                    if m >= 2:
                        pe.wait_ge(q_taken, m - 1)
                    for k in range(KT):
                        for a, b in ((w_hi, xT_hi), (w_hi, xT_lo), (w_lo, xT_hi)):
                            lhs = a[:, n % 2, k, (m % 2) * P:(m % 2 + 1) * P]
                            for j, (c, w) in enumerate(TOKEN_CHUNKS):
                                last = nc.tensor.matmul(core.ps[:, 3 * (m % 2) + j, 0:w], lhs, b[:, k, c:c + w],
                                                        start=(k == 0 and a is w_hi and b is xT_hi),
                                                        stop=(k == KT - 1 and a is w_lo))
                    last.then_inc(q_ready, 1)


def prompt_attention(core, qT, kaT, kbT, v, prompt_bias, sinks, o_rows):
    nc = core.nc
    SB = 4
    LAG = 3
    WA, WB = 2 * P, SEQ
    with ExitStack() as mem:
        bias = core.sb("pa_bias", [P, NH * (WA + WB)], F32, mem)
        bias_a = bias[:, 0:NH * WA].rearrange("p (h c) -> p h c", h=NH)
        bias_b = bias[:, NH * WA:].rearrange("p (h c) -> p h c", h=NH)
        sink_b = core.sb("pa_sink", [P, NH], F32, mem)
        s = core.sb("pa_s", [P, SB, SEQ], F32, mem)
        pT = core.sb("pa_pT", [P, 2, 4 * P], F32, mem)
        o = core.sb("pa_o", [P, 2, D], F32, mem)
        m = core.sb("pa_m", [P, PT, 2 * NH], F32, mem)
        neg_m = core.sb("pa_neg_m", [P, PT, 2 * NH], F32, mem)
        den = core.sb("pa_den", [P, PT, 2 * NH], F32, mem)
        e_sink = core.sb("pa_e_sink", [P, PT, NH], F32, mem)
        rden = core.sb("pa_rden", [P, PT, 2 * NH], F32, mem)
        tables_in = core.sem("pa_tables_in")
        scored = core.sem("pa_scored")
        biased = core.sem("pa_biased")
        negated = core.sem("pa_negated")
        exped = core.sem("pa_exped")
        turned = core.sem("pa_turned")
        copied = [core.sem("pa_copied_act"), core.sem("pa_copied_dve")]
        multiplied = core.sem("pa_multiplied")
        sink_shifted = core.sem("pa_sink_shifted")
        sink_exped = core.sem("pa_sink_exped")
        den_ready = core.sem("pa_den_ready")
        rden_ready = core.sem("pa_rden_ready")
        o_ready = core.sem("pa_o_ready")
        o_stored = [core.sem(f"pa_o_stored{x}") for x in range(2)]

        units = [(i, h) for i in range(PT) for h in range(2 * NH)]
        U = len(units)

        def first_tile(u):
            i, h = units[u]
            return 0 if h >= NH else max(0, i - 1)

        def n_tiles(u):
            return units[u][0] + 1 - first_tile(u)

        groups = [(u, g, min(4, n_tiles(u) - g)) for u in range(U) for g in range(0, n_tiles(u), 4)]
        first_group = {}
        for n, (u, _, _) in enumerate(groups):
            first_group.setdefault(u, n)
        last_group = {u: n for n, (u, _, _) in enumerate(groups)}

        def score_ps(u):
            return core.banks(2 * (u % 2), 2)[:, 0:n_tiles(u) * P]

        def copies_before(n, which):
            return (n - which) // 2 + 1

        with nc.Block() as block:
            @block.sync
            def _(sp):
                sp.dma_start(bias[:], prompt_bias).then_inc(tables_in, 16)
                sp.dma_start(sink_b[:], sinks.partition_broadcast(P)).then_inc(tables_in, 16)
                for i in range(PT):
                    sp.wait_ge(o_ready, 2 * (i + 1))
                    sp.dma_start(o_rows[i * P:(i + 1) * P, :], o[:, i % 2, :]).then_inc(o_stored[i % 2], 16)
                for x in range(2):
                    sp.wait_ge(o_stored[x], 16 * (PT // 2))

            @block.scalar
            def _(act):
                def copy(n):
                    u, _, k = groups[n]
                    act.wait_ge(turned, n + 1)
                    if n >= 2:
                        act.wait_ge(multiplied, n - 1)
                    nc.scalar.activation(pT[:, n % 2, 0:k * P], core.ps[:, 4 + n % 2, 0:k * P],
                                         ACT.Copy).then_inc(copied[0], 1)

                for step in range(U + LAG):
                    if step < U:
                        u = step
                        i, h = units[u]
                        act.wait_ge(negated, u + 1)
                        row = s[:, u % SB, 0:n_tiles(u) * P]
                        nc.scalar.activation(row, row, ACT.Exp, bias=neg_m[:, i, h:h + 1],
                                             accum_out=den[:, i, h:h + 1]).then_inc(exped, 1)
                        if h == 2 * NH - 1:
                            act.wait_ge(sink_shifted, i + 1)
                            nc.scalar.activation(e_sink[:, i], e_sink[:, i], ACT.Exp).then_inc(sink_exped, 1)
                    if step >= LAG:
                        for n in range(first_group[step - LAG], last_group[step - LAG] + 1):
                            if n % 2 == 0:
                                copy(n)

            @block.vector
            def _(dve):
                dve.wait_ge(tables_in, 32)
                for step in range(U + LAG + 1):
                    if step < U:
                        u = step
                        i, h = units[u]
                        w = n_tiles(u) * P
                        dve.wait_ge(scored, u + 1)
                        if u >= SB:
                            dve.wait_ge(turned, last_group[u - SB] + 1)
                        if h < NH:
                            table, least = bias_a[:, h, WA - w:WA], sink_b[:, h:h + 1]
                        else:
                            table, least = bias_b[:, h - NH, WB - w:WB], NEG
                        nc.vector.tensor_tensor_reduce(s[:, u % SB, 0:w], score_ps(u), table, 0.125, least,
                                                       ALU.add, ALU.max, m[:, i, h:h + 1]).then_inc(biased, 1)
                        dve.wait_ge(biased, u + 1)
                        nc.vector.tensor_scalar(neg_m[:, i, h:h + 1], m[:, i, h:h + 1], -1.0, None,
                                                ALU.mult).then_inc(negated, 1)
                        if h == 2 * NH - 1:
                            nc.vector.tensor_tensor(e_sink[:, i], sink_b[:], m[:, i, 0:NH],
                                                    ALU.subtract).then_inc(sink_shifted, 1)
                    if LAG <= step < U + LAG:
                        for n in range(first_group[step - LAG], last_group[step - LAG] + 1):
                            if n % 2 == 1:
                                dve.wait_ge(turned, n + 1)
                                if n >= 2:
                                    dve.wait_ge(multiplied, n - 1)
                                k = groups[n][2]
                                nc.vector.tensor_copy(pT[:, n % 2, 0:k * P],
                                                      core.ps[:, 4 + n % 2, 0:k * P]).then_inc(copied[1], 1)
                    if step >= LAG + 1 and units[step - LAG - 1][1] == 2 * NH - 1:
                        u = step - LAG - 1
                        i = units[u][0]
                        dve.wait_ge(sink_exped, i + 1)
                        dve.wait_ge(exped, u + 1)
                        nc.vector.tensor_tensor(den[:, i, 0:NH], den[:, i, 0:NH], e_sink[:, i],
                                                ALU.add).then_inc(den_ready, 1)
                        dve.wait_ge(den_ready, i + 1)
                        nc.vector.reciprocal(rden[:, i], den[:, i]).then_inc(rden_ready, 1)
                        dve.wait_ge(rden_ready, i + 1)
                        dve.wait_ge(multiplied, last_group[u] + 1)
                        if i >= 2:
                            dve.wait_ge(o_stored[i % 2], 16 * (i // 2))
                        r_a = rden[:, i, 0:NH].rearrange("p (s j) -> p j s", s=2).unsqueeze(3)
                        nc.vector.tensor_tensor(
                            o[:, i % 2, 0:NH * HD].rearrange("p (j s d) -> p j s d", j=4, s=2),
                            core.ps[:, 6, :].rearrange("p (j s d) -> p j s d", j=4, s=2),
                            r_a.to_broadcast([P, 4, 2, HD]), ALU.mult).then_inc(o_ready, 1)
                        r_b = rden[:, i, NH:].unsqueeze(2)
                        nc.vector.tensor_tensor(
                            o[:, i % 2, NH * HD:].rearrange("p (h d) -> p h d", h=NH),
                            core.ps[:, 7, :].rearrange("p (h d) -> p h d", h=NH),
                            r_b.to_broadcast([P, NH, HD]), ALU.mult).then_inc(o_ready, 1)

            @block.tensor
            def _(pe):
                def scores(u):
                    i, h = units[u]
                    if u >= 2:
                        pe.wait_ge(biased, u - 1)
                    j, half = (h % 4, h // 4) if h < NH else (h // 2, h % 2)
                    rows = slice(half * HD, (half + 1) * HD)
                    kT = kaT[rows, :] if h < NH else kbT[rows, j - 4, :]
                    w, k0 = n_tiles(u) * P, first_tile(u) * P
                    for c in range(0, w, 512):
                        e = min(w, c + 512)
                        last = nc.tensor.matmul(score_ps(u)[:, c:e], qT[rows, j, i * P:(i + 1) * P],
                                                kT[:, k0 + c:k0 + e], start=True, stop=True)
                    last.then_inc(scored, 1)

                def turn(n):
                    u, g, k = groups[n]
                    if g == 0:
                        pe.wait_ge(exped, u + 1)
                    if n >= 2:
                        pe.wait_ge(copied[n % 2], copies_before(n - 2, n % 2))
                    for t in range(k):
                        last = nc.tensor.transpose(core.ps[:, 4 + n % 2, t * P:(t + 1) * P],
                                                   s[:, u % SB, (g + t) * P:(g + t + 1) * P], core.identity[:])
                    last.then_inc(turned, 1)

                def multiply(n):
                    u, g, k = groups[n]
                    i, h = units[u]
                    if g == 0 and h % NH == 0 and i >= 1:
                        pe.wait_ge(o_ready, 2 * i)
                    pe.wait_ge(copied[n % 2], copies_before(n, n % 2))
                    col = (h % 4) * P + (h // 4) * HD if h < NH else (h - NH) * HD
                    vc = (h // 4) * HD if h < NH else P + (h - NH) * HD
                    for t in range(k):
                        kt = first_tile(u) + g + t
                        last = nc.tensor.matmul(core.ps[:, 6 + h // NH, col:col + HD], pT[:, n % 2, t * P:(t + 1) * P],
                                                v[:, kt, vc:vc + HD], start=(g + t == 0), stop=(g + t == n_tiles(u) - 1))
                    last.then_inc(multiplied, 1)

                for step in range(U + LAG):
                    if step < U:
                        scores(step)
                    if step >= LAG:
                        for n in range(first_group[step - LAG], last_group[step - LAG] + 1):
                            turn(n)
                            if n >= 1:
                                multiply(n - 1)
                multiply(len(groups) - 1)


def sample_attention(core, qT, kaT, kbT, v, cache, sinks, sample_bias, own_bias):
    nc = core.nc
    HQ = NH * NQ
    PAIRS = NH // 2
    with ExitStack() as mem:
        kb = core.sb("sa_kb", [P, 2, CT, 512], F32, mem)
        vb = core.sb("sa_vb", [P, 2, CT, 512], F32, mem)
        ka = core.sb("sa_ka", [P, 2, P], F32, mem)
        va = core.sb("sa_va", [P, 2, P], F32, mem)
        kT = core.sb("sa_kT", [P, PAIRS * CT + 1, P], F32, mem)
        q_pair = core.sb("sa_q_pair", [P, PAIRS, NB, 2 * NQ], F32, mem)
        q_all = core.sb("sa_q_all", [P, NB, HQ], F32, mem)
        bias = core.sb("sa_bias", [P, ST, HQ], F32, mem)
        own = core.sb("sa_own", [P, NB, 2, HQ], F32, mem)
        st = core.sb("sa_st", [P, ST, HQ], F32, mem)
        sink_b = core.sb("sa_sink", [P, NH], F32, mem)
        mx = core.sb("sa_mx", [P, 2 * HQ], F32, mem)
        m_col = core.sb("sa_m_col", [P, 1], F32, mem)
        m_diag = core.sb("sa_m_diag", [P, P], F32, mem)
        m_row = core.sb("sa_m_row", [P, 2 * HQ], F32, mem)
        e_sink = core.sb("sa_e_sink", [P, HQ], F32, mem)
        den = core.sb("sa_den", [P, 2 * HQ], F32, mem)
        rden = core.sb("sa_rden", [P, 2 * HQ], F32, mem)
        k_in = [core.sem(f"sa_k_in{x}") for x in range(2)]
        v_in = [core.sem(f"sa_v_in{x}") for x in range(2)]
        tables_in = core.sem("sa_tables_in")
        zeroed = core.sem("sa_zeroed")
        q_ready = core.sem("sa_q_ready")
        turned = core.sem("sa_turned")
        copied = [core.sem("sa_copied_act"), core.sem("sa_copied_dve")]
        scored = core.sem("sa_scored")
        biased = core.sem("sa_biased")
        max_tiles = core.sem("sa_max_tiles")
        max_turned = core.sem("sa_max_turned")
        max_col = core.sem("sa_max_col")
        diag_ready = core.sem("sa_diag_ready")
        max_spread = core.sem("sa_max_spread")
        row_ready = core.sem("sa_row_ready")
        shifted = core.sem("sa_shifted")
        exped = core.sem("sa_exped")
        summed = core.sem("sa_summed")
        den_ready = core.sem("sa_den_ready")
        rden_ready = core.sem("sa_rden_ready")
        multiplied = core.sem("sa_multiplied")
        o_taken = core.sem("sa_o_taken")

        KV_DMAS = FAR_TILES + 2
        turns = [(c, t) for c in range(PAIRS) for t in range(CT)] + [(None, 0)]
        groups = [turns[g:g + 4] for g in range(0, len(turns), 4)]
        G = len(groups)
        act_groups = [g for g in range(G) if g % 2 == 0]
        dve_groups = [g for g in range(G) if g % 2 == 1]

        def group_copied(b, g):
            mine = (act_groups, dve_groups)[g % 2]
            return copied[g % 2], len(mine) * b + mine.index(g) + 1

        scores_ps = core.banks(4, 2)
        far = slice(0, 8)

        def copy_group(g, op, dst_of):
            w = len(groups[g]) * P
            return w

        with nc.Block() as block:
            @block.sync
            def _(sp):
                sp.dma_start(bias[:], sample_bias.rearrange("p (t c) -> p t c", t=ST)).then_inc(tables_in, 16)
                sp.dma_start(own[:], own_bias.rearrange("p (b t c) -> p b t c", b=NB, t=2)).then_inc(tables_in, 16)
                sp.dma_start(sink_b[:], sinks.partition_broadcast(P)).then_inc(tables_in, 16)

                def load(big, small, big_src, small_src, b, arrived):
                    rows = big_src[b].rearrange("(t m s) c -> t m s c", m=16, s=16)
                    for t in range(FAR_TILES):
                        sp.dma_start(big[:, b % 2, t, :], rows[t, :, 0:8, :]).then_inc(arrived[b % 2], 16)
                    sp.dma_start(big[:, b % 2, FAR_TILES:CT, :],
                                 big_src[b, FAR:PAST, :].rearrange("(t p) c -> p t c", p=P)).then_inc(arrived[b % 2], 16)
                    sp.dma_start(small[:, b % 2, :], small_src[b]).then_inc(arrived[b % 2], 16)

                for b in range(NB):
                    if b >= 2:
                        sp.wait_ge(turned, G * (b - 1))
                    load(kb, ka, cache["b_k"], cache["a_k"], b, k_in)
                    if b >= 2:
                        sp.wait_ge(multiplied, b - 1)
                    load(vb, va, cache["b_v"], cache["a_v"], b, v_in)

            @block.scalar
            def _(act):
                def copy_keys(b):
                    for g in act_groups:
                        act.wait_ge(turned, G * b + g + 1)
                        w = len(groups[g])
                        nc.scalar.activation(kT[:, 4 * g:4 * g + w, :],
                                             core.ps[:, g % 4, 0:w * P].rearrange("p (g c) -> p g c", g=w),
                                             ACT.Copy).then_inc(copied[0], 1)

                copy_keys(0)
                for b in range(NB):
                    if b + 1 < NB:
                        act.wait_ge(scored, b + 1)
                        copy_keys(b + 1)
                    act.wait_ge(shifted, 3 * b + 1)
                    nc.scalar.activation(e_sink[:], e_sink[:], ACT.Exp).then_inc(exped, 1)
                    act.wait_ge(shifted, 3 * b + 3)
                    nc.scalar.activation(st[:], st[:], ACT.Exp).then_inc(exped, 1)

            @block.vector
            def _(dve):
                def copy_keys(b):
                    for g in dve_groups:
                        dve.wait_ge(turned, G * b + g + 1)
                        w = len(groups[g])
                        nc.vector.tensor_copy(kT[:, 4 * g:4 * g + w, :],
                                              core.ps[:, g % 4, 0:w * P].rearrange("p (g c) -> p g c", g=w)
                                              ).then_inc(copied[1], 1)

                nc.vector.memset(q_pair[:], 0.0).then_inc(zeroed, 1)
                nc.vector.memset(q_all[:], 0.0).then_inc(zeroed, 1)
                dve.wait_ge(zeroed, 2)
                for half in range(2):
                    rows = slice(half * HD, (half + 1) * HD)
                    for j in range(PAIRS):
                        c = half * HQ // 2 + j * NQ
                        nc.vector.tensor_copy(q_all[rows, :, c:c + NQ],
                                              qT[rows, j, SEQ:TOK].rearrange("p (b i) -> p b i", b=NB)
                                              ).then_inc(q_ready, 1)
                        nc.vector.tensor_copy(q_pair[rows, j, :, half * NQ:(half + 1) * NQ],
                                              qT[rows, 4 + j, SEQ:TOK].rearrange("p (b i) -> p b i", b=NB)
                                              ).then_inc(q_ready, 1)
                copy_keys(0)
                dve.wait_ge(tables_in, 48)
                s_ps = scores_ps[:, 0:ST * HQ].rearrange("p (t c) -> p t c", c=HQ)
                for b in range(NB):
                    dve.wait_ge(scored, b + 1)
                    if b >= 1:
                        dve.wait_ge(multiplied, b)
                    for tiles, table in ((slice(0, CT), bias[:, 0:CT]), (slice(CT + 1, CT + 2), bias[:, CT + 1:CT + 2]),
                                         (slice(CT, CT + 3, 2), own[:, b])):
                        nc.vector.scalar_tensor_tensor(st[:, tiles], s_ps[:, tiles], 0.125, table,
                                                       ALU.mult, ALU.add).then_inc(biased, 1)
                    if b + 1 < NB:
                        copy_keys(b + 1)
                    dve.wait_ge(biased, 3 * (b + 1))
                    nc.vector.tensor_reduce(mx[:, HQ:], st[:, 0:CT + 1].rearrange("p t c -> p c t"), AX.X,
                                            ALU.max).then_inc(max_tiles, 1)
                    nc.vector.tensor_tensor(mx[:, 0:HQ], st[:, CT + 1], st[:, CT + 2], ALU.max).then_inc(max_tiles, 1)
                    dve.wait_ge(max_turned, b + 1)
                    nc.vector.tensor_reduce(m_col[:], core.ps[:, 6, 0:P], AX.X, ALU.max).then_inc(max_col, 1)
                    dve.wait_ge(max_col, b + 1)
                    nc.vector.tensor_scalar(m_diag[:], core.identity[:], m_col[:, 0:1], None,
                                            ALU.mult).then_inc(diag_ready, 1)
                    dve.wait_ge(max_spread, b + 1)
                    sink_hq = sink_b[:].unsqueeze(2).to_broadcast([P, NH, NQ])
                    nc.vector.tensor_tensor(m_row[:, 0:HQ].rearrange("p (h i) -> p h i", h=NH),
                                            core.ps[:, 6, P:P + HQ].rearrange("p (h i) -> p h i", h=NH), sink_hq,
                                            ALU.max).then_inc(row_ready, 1)
                    nc.vector.tensor_copy(m_row[:, HQ:], core.ps[:, 6, P + HQ:2 * P]).then_inc(row_ready, 1)
                    dve.wait_ge(row_ready, 2 * (b + 1))
                    nc.vector.tensor_tensor(e_sink[:].rearrange("p (h i) -> p h i", h=NH), sink_hq,
                                            m_row[:, 0:HQ].rearrange("p (h i) -> p h i", h=NH),
                                            ALU.subtract).then_inc(shifted, 1)
                    nc.vector.tensor_tensor(st[:, 0:CT + 1], st[:, 0:CT + 1],
                                            m_row[:, HQ:].unsqueeze(1).to_broadcast([P, CT + 1, HQ]),
                                            ALU.subtract).then_inc(shifted, 1)
                    nc.vector.tensor_tensor(st[:, CT + 1:ST], st[:, CT + 1:ST],
                                            m_row[:, 0:HQ].unsqueeze(1).to_broadcast([P, 2, HQ]),
                                            ALU.subtract).then_inc(shifted, 1)
                    dve.wait_ge(summed, b + 1)
                    nc.vector.tensor_tensor(den[:, 0:HQ], core.ps[:, 6, 2 * P:2 * P + HQ], e_sink[:],
                                            ALU.add).then_inc(den_ready, 1)
                    nc.vector.tensor_copy(den[:, HQ:], core.ps[:, 6, 2 * P + HQ:3 * P]).then_inc(den_ready, 1)
                    dve.wait_ge(den_ready, 2 * (b + 1))
                    nc.vector.reciprocal(rden[:], den[:]).then_inc(rden_ready, 1)
                    dve.wait_ge(rden_ready, b + 1)
                    dve.wait_ge(multiplied, b + 1)
                    for half in range(2):
                        rows = slice(half * HD, (half + 1) * HD)
                        out = core.sample_oT[rows, :, b * NQ:(b + 1) * NQ]
                        c = half * HQ // 2
                        nc.vector.tensor_tensor(
                            out[:, 0:PAIRS, :],
                            core.ps[rows, 7, c:c + HQ // 2].rearrange("p (j i) -> p j i", j=PAIRS),
                            rden[rows, c:c + HQ // 2].rearrange("p (j i) -> p j i", j=PAIRS), ALU.mult).then_inc(o_taken, 1)
                        o_b = core.ps[rows, 7, HQ:2 * HQ].rearrange("p (j x i) -> p x j i", j=PAIRS, x=2)[:, half]
                        r_b = rden[rows, HQ:2 * HQ].rearrange("p (j x i) -> p x j i", j=PAIRS, x=2)[:, half]
                        nc.vector.tensor_tensor(out[:, PAIRS:, :], o_b, r_b, ALU.mult).then_inc(o_taken, 1)

            @block.tensor
            def _(pe):
                def turn_keys(b):
                    pe.wait_ge(k_in[b % 2], 16 * KV_DMAS * (b // 2 + 1))
                    for g, members in enumerate(groups):
                        if g >= 4:
                            pe.wait_ge(*group_copied(b, g - 4))
                        elif b >= 1:
                            last_in_bank = max(x for x in range(G) if x % 4 == g)
                            pe.wait_ge(*group_copied(b - 1, last_in_bank))
                        for x, (c, t) in enumerate(members):
                            src = ka[:, b % 2, :] if c is None else kb[:, b % 2, t, c * P:(c + 1) * P]
                            last = nc.tensor.transpose(core.ps[:, g % 4, x * P:(x + 1) * P], src, core.identity[:])
                        last.then_inc(turned, 1)

                def score(b):
                    for g in (act_groups[-1], dve_groups[-1]):
                        pe.wait_ge(*group_copied(b, g))
                    if b >= 1:
                        pe.wait_ge(biased, 3 * b)
                    for t in range(CT + 1):
                        for c in range(PAIRS):
                            lhs = kT[:, c * CT + t, :] if t < CT else kbT[:, c, TOK - P:TOK]
                            col = t * HQ + c * 2 * NQ
                            nc.tensor.matmul(scores_ps[:, col:col + 2 * NQ], lhs, q_pair[:, c, b, :],
                                             start=True, stop=True)
                    for t, lhs in ((CT + 1, kT[:, PAIRS * CT, :]), (CT + 2, kaT[:, TOK - P:TOK])):
                        last = nc.tensor.matmul(scores_ps[:, t * HQ:(t + 1) * HQ], lhs, q_all[:, b, :],
                                                start=True, stop=True)
                    last.then_inc(scored, 1)

                def sum_and_multiply(b):
                    pe.wait_ge(exped, 2 * (b + 1))
                    for col, tiles in ((0, (CT + 1, CT + 2)), (HQ, range(CT + 1))):
                        for t in tiles:
                            last = nc.tensor.matmul(core.ps[:, 6, 2 * P + col:2 * P + col + HQ], core.ones[:],
                                                    st[:, t, :], start=(t == tiles[0]), stop=(t == tiles[-1]))
                    last.then_inc(summed, 1)
                    pe.wait_ge(v_in[b % 2], 16 * KV_DMAS * (b // 2 + 1))
                    if b >= 1:
                        pe.wait_ge(o_taken, 4 * b)
                    nc.tensor.matmul(core.ps[:, 7, 0:HQ], va[:, b % 2, :], st[:, CT + 1, :], start=True, stop=False)
                    nc.tensor.matmul(core.ps[:, 7, 0:HQ], v[:, PT, 0:P], st[:, CT + 2, :], start=False, stop=True)
                    for c in range(PAIRS):
                        for t in range(CT + 1):
                            lhs = vb[:, b % 2, t, c * P:(c + 1) * P] if t < CT else v[:, PT, P + c * P:P + (c + 1) * P]
                            last = nc.tensor.matmul(core.ps[:, 7, HQ + c * 2 * NQ:HQ + (c + 1) * 2 * NQ], lhs,
                                                    st[:, t, c * 2 * NQ:(c + 1) * 2 * NQ],
                                                    start=(t == 0), stop=(t == CT))
                    last.then_inc(multiplied, 1)

                turn_keys(0)
                pe.wait_ge(q_ready, 4 * PAIRS)
                for b in range(NB):
                    score(b)
                    if b + 1 < NB:
                        turn_keys(b + 1)
                    pe.wait_ge(max_tiles, 2 * (b + 1))
                    if b >= 1:
                        pe.wait_ge(den_ready, 2 * b)
                    nc.tensor.transpose(core.ps[:, 6, 0:P], mx[:], core.identity[:]).then_inc(max_turned, 1)
                    pe.wait_ge(diag_ready, b + 1)
                    nc.tensor.matmul(core.ps[:, 6, P:2 * P], core.ones[:], m_diag[:], start=True,
                                     stop=True).then_inc(max_spread, 1)
                    sum_and_multiply(b)


class PostNorm:

    def __init__(self, core, tag, mem):
        self.x = core.sb(tag + "res", [P, 2, D], F32, mem)
        self.yn = core.sb(tag + "yn", [P, D], F32, mem)
        self.gain = core.sb(tag + "post_gain", [P, D], F32, mem)
        self.junk = core.sb(tag + "post_junk", [P, D], F32, mem)
        self.ms = core.sb(tag + "post_ms", [P, NT], F32, mem)
        self.rstd = core.sb(tag + "post_rstd", [P, NT], F32, mem)
        self.gain_in = core.sem(tag + "post_gain_in")
        self.x_in = [core.sem(f"{tag}res_in{s}") for s in range(2)]
        self.squared = core.sem(tag + "post_squared")
        self.ms_shifted = core.sem(tag + "post_ms_shifted")
        self.rstd_ready = core.sem(tag + "post_rstd_ready")
        self.scaled = core.sem(tag + "post_scaled")
        self.added = core.sem(tag + "post_added")
        self.stored = [core.sem(f"{tag}post_stored{s}") for s in range(2)]


def load_residual(sp, pn, src, t):
    if t >= 2:
        sp.wait_ge(pn.stored[t % 2], 16 * (t // 2))
    for rows, piece in token_rows(*src, t):
        sp.dma_start(pn.x[rows, t % 2, :], piece).then_inc(pn.x_in[t % 2], 16)


def store_residual(sp, pn, dst, t):
    sp.wait_ge(pn.added, t + 1)
    for rows, piece in stored_rows(*dst, t):
        sp.dma_start(piece, pn.x[rows, t % 2, :]).then_inc(pn.stored[t % 2], 16)


def square_of_y(nc, act, pn, y, t):
    if t >= 1:
        act.wait_ge(pn.squared, t)
    nc.scalar.activation(pn.junk[:], y, ACT.Square, scale=1.0 / 32,
                         accum_out=pn.ms[:, t:t + 1]).then_inc(pn.squared, 1)


def rstd_of_y(core, pool, pn, t):
    pool.wait_ge(pn.squared, t + 1)
    root(core, pool, pn.ms, pn.rstd, pn.ms_shifted, pn.rstd_ready, t)


def add_normed(nc, dve, pn, y, t):
    if t == 0:
        dve.wait_ge(pn.gain_in, 16)
    dve.wait_ge(pn.rstd_ready, t + 1)
    if t >= 1:
        dve.wait_ge(pn.added, t)
    nc.vector.scalar_tensor_tensor(pn.yn[:], y, pn.rstd[:, t:t + 1], pn.gain[:], ALU.mult, ALU.mult).then_inc(pn.scaled, 1)
    dve.wait_ge(pn.scaled, t + 1)
    dve.wait_ge(pn.x_in[t % 2], 16 * (t // 2 + 1 + (t == PT)))
    nc.vector.tensor_tensor(pn.x[:, t % 2, :], pn.x[:, t % 2, :], pn.yn[:], ALU.add).then_inc(pn.added, 1)


def wait_stored(sp, pn):
    sp.wait_ge(pn.stored[0], 16 * (PT // 2 + 1))
    sp.wait_ge(pn.stored[1], 16 * (PT // 2))


def out_project(core, o_rows, w_out, x_src, x_dst, gain):
    nc = core.nc
    with ExitStack() as mem:
        oT_hi = core.sb("oT_hi", [P, KT, TOK], F32R, mem)
        oT_lo = core.sb("oT_lo", [P, KT, TOK], F32R, mem)
        w_hi = core.sb("out_w_hi", [P, KT, D], F32R, mem)
        w_lo = core.sb("out_w_lo", [P, KT, D], F32R, mem)
        raws = 2
        raw = core.sb("out_raw", [P, raws, D], F32, mem)
        o = core.sb("out_o", [P, 2, D], F32, mem)
        pn = PostNorm(core, "out_", mem)
        raw_in = [core.sem(f"out_raw_in{s}") for s in range(raws)]
        o_in = [core.sem(f"out_o_in{s}") for s in range(2)]
        w_hi_done = core.sem("out_w_hi_done")
        w_lo_done = core.sem("out_w_lo_done")
        turned = core.sem("out_turned")
        o_hi_done = core.sem("out_o_hi_done")
        o_lo_done = core.sem("out_o_lo_done")
        y_ready = core.sem("out_y_ready")
        turned_ps = [core.banks(2 * i, 2).rearrange("p (k c) -> p k c", k=KT) for i in range(2)]

        def w_pieces(k):
            if k >= KT // 2:
                return [(slice(0, P), w_out[k * P:(k + 1) * P, :])]
            return [(slice(h * HD, (h + 1) * HD), w_out[(k + 4 * h) * HD:(k + 4 * h + 1) * HD, :]) for h in range(2)]

        raw_arrived = [16 * sum(len(w_pieces(j)) for j in range(k % raws, k + 1, raws)) for k in range(KT)]

        def y_of(t):
            return core.banks(4 + 2 * (t % 2), 2)

        with nc.Block() as block:
            @block.sync
            def _(sp):
                for t in range(PT):
                    if t >= 2:
                        sp.wait_ge(turned, t - 1)
                    sp.dma_start(o[:, t % 2, :], o_rows[t * P:(t + 1) * P, :]).then_inc(o_in[t % 2], 16)
                    if t >= raws:
                        sp.wait_ge(w_lo_done, t - raws + 1)
                    for rows, src in w_pieces(t):
                        sp.dma_start(raw[rows, t % raws, :], src).then_inc(raw_in[t % raws], 16)
                sp.dma_start(pn.gain[:], gain.partition_broadcast(P)).then_inc(pn.gain_in, 16)
                for t in range(NT):
                    load_residual(sp, pn, x_src, t)
                    if t >= 1:
                        store_residual(sp, pn, x_dst, t - 1)
                store_residual(sp, pn, x_dst, NT - 1)
                wait_stored(sp, pn)

            @block.scalar
            def _(act):
                nc.scalar.activation(oT_hi[:, :, SEQ:TOK], core.sample_oT[:], ACT.Copy).then_inc(o_hi_done, 1)
                for t in range(PT):
                    act.wait_ge(raw_in[t % raws], raw_arrived[t])
                    nc.scalar.activation(w_hi[:, t, :], raw[:, t % raws, :], ACT.Copy).then_inc(w_hi_done, 1)
                    act.wait_ge(turned, t + 1)
                    nc.scalar.activation(oT_hi[:, :, t * P:(t + 1) * P], turned_ps[t % 2],
                                         ACT.Copy).then_inc(o_hi_done, 1)
                for t in range(NT):
                    act.wait_ge(y_ready, t + 1)
                    square_of_y(nc, act, pn, y_of(t), t)

            @block.gpsimd
            def _(pool):
                for t in range(NT):
                    rstd_of_y(core, pool, pn, t)

            @block.vector
            def _(dve):
                dve.wait_ge(o_hi_done, 1)
                nc.vector.tensor_tensor(oT_lo[:, :, SEQ:TOK], core.sample_oT[:], oT_hi[:, :, SEQ:TOK].bitcast(F32),
                                        ALU.subtract).then_inc(o_lo_done, 1)
                for t in range(PT):
                    dve.wait_ge(w_hi_done, t + 1)
                    nc.vector.tensor_tensor(w_lo[:, t, :], raw[:, t % raws, :], w_hi[:, t, :].bitcast(F32),
                                            ALU.subtract).then_inc(w_lo_done, 1)
                    dve.wait_ge(o_hi_done, t + 2)
                    c = slice(t * P, (t + 1) * P)
                    nc.vector.tensor_tensor(oT_lo[:, :, c], turned_ps[t % 2], oT_hi[:, :, c].bitcast(F32),
                                            ALU.subtract).then_inc(o_lo_done, 1)
                for t in range(NT):
                    add_normed(nc, dve, pn, y_of(t), t)

            @block.tensor
            def _(pe):
                for t in range(PT):
                    pe.wait_ge(o_in[t % 2], 16 * (t // 2 + 1))
                    if t >= 2:
                        pe.wait_ge(o_lo_done, t)
                    for k in range(KT):
                        last = nc.tensor.transpose(turned_ps[t % 2][:, k, :], o[:, t % 2, k * P:(k + 1) * P],
                                                   core.identity[:])
                    last.then_inc(turned, 1)
                pe.wait_ge(w_lo_done, KT)
                pe.wait_ge(o_lo_done, NT)
                for t in range(NT):
                    if t >= 2:
                        pe.wait_ge(pn.scaled, t - 1)
                    c = tile_start(t)
                    for k in range(KT):
                        for a, b in ((oT_hi, w_hi), (oT_hi, w_lo), (oT_lo, w_hi)):
                            for n in range(2):
                                last = nc.tensor.matmul(core.ps[:, 4 + 2 * (t % 2) + n, :], a[:, k, c:c + P],
                                                        b[:, k, n * 512:(n + 1) * 512],
                                                        start=(k == 0 and a is oT_hi and b is w_hi),
                                                        stop=(k == KT - 1 and a is oT_lo))
                    last.then_inc(y_ready, 1)


def mlp(core, tag, xT_hi, xT_lo, w1, w2, y):
    nc = core.nc
    w1_rows = w1.rearrange("(k p) n -> p k n", p=P)
    with ExitStack() as mem:
        h_hi = core.sb(tag + "h_hi", [P, FFB, TOK], F32R, mem)
        h_lo = core.sb(tag + "h_lo", [P, FFB, TOK], F32R, mem)
        w2_hi = core.sb(tag + "w2_hi", [P, FFB, D], F32R, mem)
        w2_lo = core.sb(tag + "w2_lo", [P, FFB, D], F32R, mem)
        relu = core.sb(tag + "relu", [P, 2, 384], F32, mem)
        square = core.sb(tag + "square", [P, 2, 384], F32, mem)
        w1_hi = core.sb(tag + "w1_hi", [P, 2, KT, P], F32R, mem)
        w1_lo = core.sb(tag + "w1_lo", [P, 2, KT, P], F32R, mem)
        raw = core.sb(tag + "raw", [P, 2, D], F32, mem)
        raw_in = [core.sem(f"{tag}raw_in{s}") for s in range(2)]
        hi_done = core.sem(tag + "hi_done")
        lo_done = core.sem(tag + "lo_done")
        up_ready = core.sem(tag + "up_ready")
        relu_done = core.sem(tag + "relu_done")
        square_hi = core.sem(tag + "square_hi")
        squared = core.sem(tag + "squared")
        h_ready = core.sem(tag + "h_ready")
        part_ready = core.sem(tag + "part_ready")
        part_added = core.sem(tag + "part_added")
        y_zero = core.sem(tag + "y_zero")
        PARTS = 2 * NT

        def tile_source(b, n, ahead=0):
            if n in (3, 4, 5, 6):
                return w2[bass.ds((b + ahead) * (FFB * P) + (n - 3) * P, P), :]
            i = 3 if n == 7 else n
            return w1_rows[:, :, bass.ds((b + ahead) * (FFB * P) + i * P, P)]

        def raw_view(n):
            r = raw[:, n % 2, :]
            return r if n in (3, 4, 5, 6) else r.rearrange("p (k c) -> p k c", k=KT)

        def split_into(n):
            if n in (3, 4, 5, 6):
                return w2_hi[:, n - 3, :], w2_lo[:, n - 3, :]
            i = 3 if n == 7 else n
            return w1_hi[:, i % 2], w1_lo[:, i % 2]

        with nc.Block() as block:
            @block.sync
            def _(sp):
                def load(b, n, ahead=0, first=False):
                    if not first:
                        sp.wait_ge(lo_done, b * 8 + (8 * ahead + n - 1))
                    sp.dma_start(raw_view(n), tile_source(b, n, ahead)).then_inc(raw_in[n % 2], 16)

                load(0, 0, first=True)
                load(0, 1, first=True)
                for b in range(NBLK):
                    for n in range(2, 8):
                        load(b, n)
                    if b < NBLK - 1:
                        load(b, 0, 1)
                        load(b, 1, 1)

            @block.scalar
            def _(act):
                def split(b, n, ahead=0, first=False):
                    m = 8 * ahead + n
                    act.wait_ge(raw_in[n % 2], b * 64 + 16 * (m // 2 + 1))
                    if n in (3, 4, 5, 6):
                        if not first:
                            act.wait_ge(part_ready, b * PARTS)
                    elif not first:
                        i = 4 * ahead + (3 if n == 7 else n)
                        act.wait_ge(up_ready, b * 4 + (i - 1))
                    nc.scalar.activation(split_into(n)[0], raw_view(n), ACT.Copy).then_inc(hi_done, 1)

                def hidden(b, i, first=False):
                    act.wait_ge(up_ready, b * 4 + (i + 1))
                    if i == 0 and not first:
                        act.wait_ge(part_ready, b * PARTS)
                    for j, (c, w) in enumerate(TOKEN_CHUNKS):
                        n = 3 * i + j
                        if not (first and n < 2):
                            act.wait_ge(squared, b * 12 + (n - 1))
                        nc.scalar.activation(relu[:, n % 2, 0:w], core.ps[:, 3 * (i % 2) + j, 0:w],
                                             ACT.Relu).then_inc(relu_done, 1)
                        act.wait_ge(relu_done, b * 12 + (n + 1))
                        nc.scalar.activation(h_hi[:, i, c:c + w], relu[:, n % 2, 0:w], ACT.Square).then_inc(square_hi, 1)

                def steps(b, last=False, first=False):
                    hidden(b, 0, first)
                    split(b, 2)
                    for n in (3, 4, 5, 6):
                        split(b, n, first=first)
                    split(b, 7)
                    hidden(b, 1)
                    if not last:
                        split(b, 0, 1)
                    hidden(b, 2)
                    if not last:
                        split(b, 1, 1)
                    hidden(b, 3)

                split(0, 0, first=True)
                split(0, 1, first=True)
                steps(0, first=True)
                with act.Fori(1, NBLK - 1) as b:
                    steps(b)
                steps(NBLK - 1, last=True)

            @block.vector
            def _(dve):
                def split(b, n, ahead=0):
                    dve.wait_ge(hi_done, b * 8 + (8 * ahead + n + 1))
                    hi, lo = split_into(n)
                    nc.vector.tensor_tensor(lo, raw_view(n), hi.bitcast(F32), ALU.subtract).then_inc(lo_done, 1)

                def hidden(b, i):
                    for j, (c, w) in enumerate(TOKEN_CHUNKS):
                        n = 3 * i + j
                        dve.wait_ge(relu_done, b * 12 + (n + 1))
                        nc.vector.tensor_tensor(square[:, n % 2, 0:w], relu[:, n % 2, 0:w], relu[:, n % 2, 0:w],
                                                ALU.mult).then_inc(squared, 1)
                        dve.wait_ge(squared, b * 12 + (n + 1))
                        dve.wait_ge(square_hi, b * 12 + (n + 1))
                        nc.vector.tensor_tensor(h_lo[:, i, c:c + w], square[:, n % 2, 0:w],
                                                h_hi[:, i, c:c + w].bitcast(F32), ALU.subtract).then_inc(h_ready, 1)

                def steps(b, last=False):
                    hidden(b, 0)
                    for n in range(2, 8):
                        split(b, n)
                    hidden(b, 1)
                    if not last:
                        split(b, 0, 1)
                    hidden(b, 2)
                    if not last:
                        split(b, 1, 1)
                    hidden(b, 3)
                    for n in range(PARTS):
                        dve.wait_ge(part_ready, b * PARTS + (n + 1))
                        part = y[:, n // 2, (n % 2) * 512:(n % 2 + 1) * 512]
                        nc.vector.tensor_tensor(part, part, core.ps[:, 6 + n % 2, :], ALU.add).then_inc(part_added, 1)

                nc.vector.memset(y[:], 0.0).then_inc(y_zero, 1)
                split(0, 0)
                split(0, 1)
                dve.wait_ge(y_zero, 1)
                with dve.Fori(0, NBLK - 1) as b:
                    steps(b)
                steps(NBLK - 1, last=True)

            @block.tensor
            def _(pe):
                def up(b, i, ahead=0, first=False):
                    pe.wait_ge(lo_done, b * 8 + (8 * ahead + (8 if i == 3 else i + 1)))
                    if not first:
                        pe.wait_ge(relu_done, b * 12 + (3 * (4 * ahead + i) - 3))
                    for k in range(KT):
                        for a, x in ((w1_hi, xT_hi), (w1_hi, xT_lo), (w1_lo, xT_hi)):
                            for j, (c, w) in enumerate(TOKEN_CHUNKS):
                                mm = nc.tensor.matmul(core.ps[:, 3 * (i % 2) + j, 0:w], a[:, i % 2, k, :],
                                                      x[:, k, c:c + w],
                                                      start=(k == 0 and a is w1_hi and x is xT_hi),
                                                      stop=(k == KT - 1 and a is w1_lo))
                    mm.then_inc(up_ready, 1)

                def down(b, first=False):
                    pe.wait_ge(lo_done, b * 8 + 7)
                    pe.wait_ge(h_ready, b * 12 + 12)
                    for n in range(PARTS):
                        t, half = n // 2, n % 2
                        if not (first and n < 2):
                            pe.wait_ge(part_added, b * PARTS + (n - 1))
                        s = tile_start(t)
                        for k in range(FFB):
                            for a, w in ((h_hi, w2_hi), (h_hi, w2_lo), (h_lo, w2_hi)):
                                mm = nc.tensor.matmul(core.ps[:, 6 + half, :], a[:, k, s:s + P],
                                                      w[:, k, half * 512:(half + 1) * 512],
                                                      start=(k == 0 and a is h_hi and w is w2_hi),
                                                      stop=(k == FFB - 1 and a is h_lo))
                        mm.then_inc(part_ready, 1)

                up(0, 0, first=True)
                up(0, 1, first=True)
                for i in (2, 3):
                    up(0, i)
                up(0, 0, 1)
                down(0, first=True)
                with pe.Fori(1, NBLK - 1) as b:
                    for i in (1, 2, 3):
                        up(b, i)
                    up(b, 0, 1)
                    down(b)
                for i in (1, 2, 3):
                    up(NBLK - 1, i)
                down(NBLK - 1)


def finish_mlp(core, tag, y, x_src, x_dst, gain):
    nc = core.nc
    with ExitStack() as mem:
        pn = PostNorm(core, tag, mem)
        with nc.Block() as block:
            @block.sync
            def _(sp):
                sp.dma_start(pn.gain[:], gain.partition_broadcast(P)).then_inc(pn.gain_in, 16)
                for t in range(NT):
                    load_residual(sp, pn, x_src, t)
                    if t >= 1:
                        store_residual(sp, pn, x_dst, t - 1)
                store_residual(sp, pn, x_dst, NT - 1)
                wait_stored(sp, pn)

            @block.scalar
            def _(act):
                for t in range(NT):
                    square_of_y(nc, act, pn, y[:, t, :], t)

            @block.gpsimd
            def _(pool):
                for t in range(NT):
                    rstd_of_y(core, pool, pn, t)

            @block.vector
            def _(dve):
                for t in range(NT):
                    add_normed(nc, dve, pn, y[:, t, :], t)


def pool_mix(core, x_src, x_dst, state, pool_w, pool_scale, pre_gain, post_gain, tables, prompt_pool, sample_pool):
    nc = core.nc
    xs = 3
    with ExitStack() as mem:
        x = core.sb("pm_x", [P, xs, D], F32, mem)
        gain_b = core.sb("pm_gain", [P, D], F32, mem)
        junk = core.sb("pm_junk", [P, D], F32, mem)
        ms = core.sb("pm_ms", [P, NT], F32, mem)
        rstd = core.sb("pm_rstd", [P, NT], F32, mem)
        h = core.sb("pm_h", [P, NT, D], F32, mem)
        before = core.sb("pm_before", [NB * CTX, D], F32, mem)
        band = core.sb("pm_band", [P, 4, 3, P], F32, mem)
        own = core.sb("pm_own", [P, 4, NS], F32, mem)
        ctx = core.sb("pm_ctx", [NB * CTX, 4, NS], F32, mem)
        w = core.sb("pm_w", [P, KT, 256], F32, mem)
        scale_b = core.sb("pm_scale", [P, D], F32, mem)
        yT = core.sb("pm_yT", [P, KT, TOK], F32, mem)
        z = core.sb("pm_z", [P, 2, D], F32, mem)
        pn = PostNorm(core, "pm_", mem)
        x_in = [core.sem(f"pm_x_in{s}") for s in range(xs)]
        gain_in = core.sem("pm_gain_in")
        tables_in = core.sem("pm_tables_in")
        weights_in = core.sem("pm_weights_in")
        squared = core.sem("pm_squared")
        ms_shifted = core.sem("pm_ms_shifted")
        rstd_ready = core.sem("pm_rstd_ready")
        normed = core.sem("pm_normed")
        pool_stored = core.sem("pm_pool_stored")
        pooled = core.sem("pm_pooled")
        yT_ready = core.sem("pm_yT_ready")
        z_ready = core.sem("pm_z_ready")
        z_scaled = core.sem("pm_z_scaled")

        def pooled_ps(t):
            return core.banks(2 * (t % 2), 2).rearrange("p (k c) -> p k c", k=KT)

        with nc.Block() as block:
            @block.sync
            def _(sp):
                sp.dma_start(gain_b[:], pre_gain.partition_broadcast(P)).then_inc(gain_in, 16)
                for t in range(NT):
                    if t >= xs:
                        sp.wait_ge(normed, t - xs + 1)
                    for rows, src in token_rows(*x_src, t):
                        sp.dma_start(x[rows, t % xs, :], src).then_inc(x_in[t % xs], 16)
                    if t == 1:
                        sp.dma_start(band[:], tables["pool_band"].rearrange("p (g a c) -> p g a c", g=4, a=3)
                                     ).then_inc(tables_in, 16)
                        sp.dma_start(own[:], tables["pool_own"].rearrange("p (g c) -> p g c", g=4)).then_inc(tables_in, 16)
                        sp.dma_start(ctx[:], tables["pool_ctx"].rearrange("p (g c) -> p g c", g=4)).then_inc(tables_in, 16)
                        sp.dma_start(before[:], state).then_inc(tables_in, 16)
                        sp.dma_start(w[:], pool_w.rearrange("(k p) n -> p k n", p=P)).then_inc(weights_in, 16)
                        sp.dma_start(scale_b[:], pool_scale.partition_broadcast(P)).then_inc(weights_in, 16)
                        sp.dma_start(pn.gain[:], post_gain.partition_broadcast(P)).then_inc(pn.gain_in, 16)
                    if t >= 5:
                        store_residual(sp, pn, x_dst, t - 5)
                    if t >= 3:
                        load_residual(sp, pn, x_src, t - 3)
                for t in range(NT - 3, NT):
                    store_residual(sp, pn, x_dst, t - 2)
                    load_residual(sp, pn, x_src, t)
                for t in range(NT - 2, NT):
                    store_residual(sp, pn, x_dst, t)
                wait_stored(sp, pn)

            @block.gpsimd
            def _(pool):
                for b in range(NB):
                    pool.dma_start(sample_pool[b, 0:CTX - NQ, :],
                                   state[b * CTX + NQ:(b + 1) * CTX, :]).then_inc(pool_stored, 16)
                for t in range(NT):
                    pool.wait_ge(squared, t + 1)
                    root(core, pool, ms, rstd, ms_shifted, rstd_ready, t)
                    if t >= 3:
                        rstd_of_y(core, pool, pn, t - 3)
                pool.wait_ge(normed, NT)
                pool.dma_start(prompt_pool, h[P - CTX:P, PT - 1, :]).then_inc(pool_stored, 16)
                for b in range(NB):
                    r = P - NS + b * NQ
                    pool.dma_start(sample_pool[b, CTX - NQ:CTX, :], h[r:r + NQ, PT, :]).then_inc(pool_stored, 16)
                for t in range(NT - 3, NT):
                    rstd_of_y(core, pool, pn, t)
                pool.wait_ge(pool_stored, 16 * (2 * NB + 1))

            @block.scalar
            def _(act):
                def take_pooled(t):
                    act.wait_ge(pooled, t + 1)
                    c, n = (t * P, P) if t < PT else (SEQ, NS)
                    nc.scalar.activation(yT[:, :, c:c + n], pooled_ps(t)[:, :, 0:n], ACT.Copy).then_inc(yT_ready, 1)

                def square_z(t):
                    act.wait_ge(z_scaled, t + 1)
                    square_of_y(nc, act, pn, z[:, t % 2, :], t)

                for t in range(NT):
                    act.wait_ge(x_in[t % xs], 16 * (t // xs + 1 + (t == PT)))
                    if t >= 1:
                        act.wait_ge(squared, t)
                    nc.scalar.activation(junk[:], x[:, t % xs, :], ACT.Square, scale=1.0 / 32,
                                         accum_out=ms[:, t:t + 1]).then_inc(squared, 1)
                    if t >= 1:
                        take_pooled(t - 1)
                    if t >= 3:
                        square_z(t - 3)
                take_pooled(NT - 1)
                for t in range(NT - 3, NT):
                    square_z(t)

            @block.vector
            def _(dve):
                def scale_z(t):
                    dve.wait_ge(z_ready, t + 1)
                    if t == 0:
                        dve.wait_ge(weights_in, 32)
                    if t >= 2:
                        dve.wait_ge(pn.scaled, t - 1)
                        dve.wait_ge(pn.squared, t - 1)
                    nc.vector.tensor_tensor(z[:, t % 2, :], core.banks(4 + 2 * (t % 2), 2), scale_b[:],
                                            ALU.mult).then_inc(z_scaled, 1)

                for t in range(NT):
                    dve.wait_ge(rstd_ready, t + 1)
                    if t == 0:
                        dve.wait_ge(gain_in, 16)
                    nc.vector.scalar_tensor_tensor(h[:, t, :], x[:, t % xs, :], rstd[:, t:t + 1], gain_b[:],
                                                   ALU.mult, ALU.mult).then_inc(normed, 1)
                    if t >= 2:
                        scale_z(t - 2)
                    if t >= 3:
                        add_normed(nc, dve, pn, z[:, (t - 3) % 2, :], t - 3)
                for t in range(NT - 2, NT):
                    scale_z(t)
                    add_normed(nc, dve, pn, z[:, (t - 1) % 2, :], t - 1)
                add_normed(nc, dve, pn, z[:, (NT - 1) % 2, :], NT - 1)

            @block.tensor
            def _(pe):
                def mix(t):
                    pe.wait_ge(yT_ready, t + 1)
                    if t == 0:
                        pe.wait_ge(weights_in, 32)
                    if t >= 2:
                        pe.wait_ge(z_scaled, t - 1)
                    c = tile_start(t)
                    for g in range(4):
                        for k in range(2):
                            last = nc.tensor.matmul(core.banks(4 + 2 * (t % 2), 2)[:, g * 256:(g + 1) * 256],
                                                    yT[:, 2 * g + k, c:c + P], w[:, 2 * g + k, :],
                                                    start=(k == 0), stop=(k == 1))
                    last.then_inc(z_ready, 1)

                pe.wait_ge(tables_in, 64)
                for t in range(NT):
                    pe.wait_ge(normed, t + 1)
                    if t >= 2:
                        pe.wait_ge(yT_ready, t - 1)
                    for f in range(KT):
                        fc, g = slice(f * P, (f + 1) * P), f // 2
                        if t == 0:
                            parts = [(h[:, 0, fc], band[:, g, 0, :])]
                        elif t < PT:
                            parts = [(h[:, t, fc], band[:, g, 1, :]), (h[:, t - 1, fc], band[:, g, 2, :])]
                        else:
                            parts = [(h[:, t, fc], own[:, g, :]), (before[:, fc], ctx[:, g, :])]
                        n = P if t < PT else NS
                        for j, (lhs, rhs) in enumerate(parts):
                            last = nc.tensor.matmul(pooled_ps(t)[:, f, 0:n], lhs, rhs, start=(j == 0),
                                                    stop=(j == len(parts) - 1))
                    last.then_inc(pooled, 1)
                    if t >= 1:
                        mix(t - 1)
                mix(NT - 1)


def build(nc, ins, tables, outs, scratch):
    xp, xs = ins["x_prompt"], ins["x_sample"]
    gains = ins["norm_g"]
    x1, x2, x3, o_rows = (scratch[n] for n in ("x1", "x2", "x3", "o_rows"))
    halves = lambda x: (x[0:SEQ, :], x[SEQ:TOK, :])
    with ExitStack() as ctx:
        core = Core(nc, ctx)
        start(core, tables)
        core.end_stage()
        with ExitStack() as mem:
            qT = core.sb("qT", [P, KT, TOK], F32, mem)
            kaT = core.sb("kaT", [P, TOK], F32, mem)
            kbT = core.sb("kbT", [P, NH // 2, TOK], F32, mem)
            v = core.sb("v", [P, NT, P + NH * HD], F32, mem)
            with ExitStack() as inner:
                xT_hi = core.sb("a_xT_hi", [P, KT, TOK], F32R, inner)
                xT_lo = core.sb("a_xT_lo", [P, KT, TOK], F32R, inner)
                prepare(core, "a_", xp, xs, gains[0], xT_hi, xT_lo)
                core.end_stage()
                in_project(core, ins["attn_w_in"], xT_hi, xT_lo, qT, kaT, kbT, v, outs)
                core.end_stage()
            prompt_attention(core, qT, kaT, kbT, v, tables["prompt_bias"], ins["attn_sinks"], o_rows)
            core.end_stage()
            sample_attention(core, qT, kaT, kbT, v, {n: ins["cache_" + n] for n in ("a_k", "a_v", "b_k", "b_v")},
                             ins["attn_sinks"], tables["sample_bias"], tables["own_bias"])
            core.end_stage()
        out_project(core, o_rows, ins["attn_w_out"], (xp, xs), halves(x1), gains[1])
        core.end_stage()
        for layer, src, dst in ((0, halves(x1), halves(x2)), (1, halves(x3), (outs["y_prompt"], outs["y_sample"]))):
            if layer == 1:
                pool_mix(core, halves(x2), src, ins["state_pool"], ins["pool_w"], ins["pool_scale"], gains[4], gains[5],
                         tables, outs["prompt_pool"], outs["sample_pool"])
                core.end_stage()
            tag = f"m{layer}_"
            with ExitStack() as mem:
                y = core.sb(tag + "y", [P, NT, D], F32, mem)
                with ExitStack() as inner:
                    xT_hi = core.sb(tag + "xT_hi", [P, KT, TOK], F32R, inner)
                    xT_lo = core.sb(tag + "xT_lo", [P, KT, TOK], F32R, inner)
                    prepare(core, tag + "pre_", *src, gains[4 * layer + 2], xT_hi, xT_lo)
                    core.end_stage()
                    mlp(core, tag, xT_hi, xT_lo, ins["mlp_w1"][layer], ins["mlp_w2"][layer], y)
                    core.end_stage()
                finish_mlp(core, tag, y, src, dst, gains[4 * layer + 3])
                core.end_stage()


def kernel(**inputs):
    import concourse.bacc as bacc
    from concourse.bass_utils import run_bass_kernel_spmd

    nc = bacc.Bacc("TRN2", target_bir_lowering=False, num_devices=1)
    shapes = {
        "x_prompt": (SEQ, D), "x_sample": (NS, D),
        "cache_a_k": (NB, P, P), "cache_a_v": (NB, P, P),
        "cache_b_k": (NB, PAST, NH * HD), "cache_b_v": (NB, PAST, NH * HD),
        "state_pool": (NB * CTX, D), "norm_g": (8, D), "attn_w_in": (D, 2304), "attn_w_out": (D, D),
        "attn_sinks": (NH,), "pool_w": (D, 256), "pool_scale": (D,),
        "mlp_w1": (2, D, DFF), "mlp_w2": (2, DFF, D),
    }
    arrays, ins, tables, outs, scratch = {}, {}, {}, {}, {}
    for name, shape in shapes.items():
        arrays[name] = np.ascontiguousarray(np.asarray(inputs[name]).reshape(shape))
        ins[name] = nc.dram_tensor(name, shape, F32, kind="ExternalInput").ap()
    for name, table in shape_constants().items():
        arrays["table_" + name] = table
        tables[name] = nc.dram_tensor("table_" + name, table.shape, F32, kind="ExternalInput").ap()
    results = {
        "y_prompt": ((SEQ, D), (1, SEQ, D)), "y_sample": ((NS, D), (NB, NQ, D)),
        "prompt_a_k": ((P, P), (1, 1, P, 2, HD)), "prompt_a_v": ((P, P), (1, 1, P, 2, HD)),
        "prompt_b_k": ((SEQ, 512), (1, 1, SEQ, NH, HD)), "prompt_b_v": ((SEQ, 512), (1, 1, SEQ, NH, HD)),
        "prompt_pool": ((CTX, D), (1, 1, CTX, D)),
        "sample_a_k": ((NS, P), (1, NB, NQ, 2, HD)), "sample_a_v": ((NS, P), (1, NB, NQ, 2, HD)),
        "sample_b_k": ((NS, 512), (1, NB, NQ, NH, HD)), "sample_b_v": ((NS, 512), (1, NB, NQ, NH, HD)),
        "sample_pool": ((NB, CTX, D), (1, NB, CTX, D)),
    }
    for name, (shape, _) in results.items():
        outs[name] = nc.dram_tensor("out_" + name, shape, F32, kind="ExternalOutput").ap()
    for name, rows in (("x1", TOK), ("x2", TOK), ("x3", TOK), ("o_rows", SEQ)):
        scratch[name] = nc.dram_tensor("scratch_" + name, (rows, D), F32, kind="Internal").ap()
    build(nc, ins, tables, outs, scratch)
    r = run_bass_kernel_spmd(nc, [arrays], core_ids=[0])
    return tuple(r.results[0]["out_" + name].reshape(shape) for name, (_, shape) in results.items())
```

```python
from contextlib import ExitStack

import numpy as np

import concourse.bass as bass
from concourse import mybir

F32 = mybir.dt.float32
F32R = mybir.dt.float32r
ALU = mybir.AluOpType
ACT = mybir.ActivationFunctionType
AX = mybir.AxisListType

P = 128
D = 1024
KT = D // P
SEQ = 1024
NB = 8
NQ = 8
NS = NB * NQ
TOK = SEQ + NS
PT = SEQ // P
NT = PT + 1
TOKEN_CHUNKS = ((0, 384), (384, 384), (768, 320))
HD = 64
NH = 8
WINDOW_A = 128
PAST = 2048
DFF = 4 * D
FFB = 4
NBLK = DFF // (FFB * P)
CTX = 15
POOL_W = (2, 4, 8, 16)
EPS = 1e-6
NEG = -1e30
BRANCHES = ((128, 1), (512, 4), (2048, 16))
FAR = PAST - 512
FAR_TILES = FAR // 2 // P
NEAR_TILES = 512 // P
CT = FAR_TILES + NEAR_TILES


def tile_start(t):
    return t * P if t < PT else TOK - P


def new_columns(t):
    return (slice(t * P, (t + 1) * P), slice(0, P)) if t < PT else (slice(SEQ, TOK), slice(P - NS, P))


def slope(n):
    return 2.0 ** (-8.0 * (n + 1) / 16)


def branch_bias(dist, n):
    count = sum(((dist >= 0) & (dist <= w) & (dist % d == 0)).astype(np.float64) for w, d in BRANCHES)
    return np.where(count > 0, np.log(np.maximum(count, 1)) - slope(n) * dist, NEG)


def window_bias(dist, n):
    return np.where((dist >= 0) & (dist <= WINDOW_A), -slope(n) * dist, NEG)


def shape_constants():
    q = np.arange(P)[:, None]
    prompt_a = np.stack([window_bias(P + q - np.arange(2 * P), h) for h in range(NH)], 1)
    prompt_b = np.stack([branch_bias(SEQ - P + q - np.arange(SEQ), NH + h) for h in range(NH)], 1)
    prompt = np.concatenate([np.maximum(x * 8, NEG).reshape(P, -1) for x in (prompt_a, prompt_b)], 1)

    rows = np.empty((CT, P), np.int64)
    p = np.arange(P)
    for t in range(FAR_TILES):
        rows[t] = 16 * (16 * t + p // 8) + p % 8
    for t in range(NEAR_TILES):
        rows[FAR_TILES + t] = FAR + t * P + p
    sample_b = np.zeros((P, CT * P + NQ))
    sample_a = np.zeros((NH * NQ, P + NQ))
    new = np.arange(NQ)
    for h in range(NH):
        for i in range(NQ):
            sample_b[32 * (h // 2) + NQ * (h % 2) + i] = np.concatenate(
                [branch_bias(PAST + i - rows.ravel(), NH + h), branch_bias(i - new, NH + h)])
            sample_a[NQ * h + i] = np.concatenate([window_bias(P + i - p, h), window_bias(i - new, h)])
    pool = np.zeros((P, 4, 3, P), np.float32)
    pool_own = np.zeros((P, 4, NS), np.float32)
    pool_ctx = np.zeros((NB * CTX, 4, NS), np.float32)
    for g, w in enumerate(POOL_W):
        for j in range(P):
            for k in range(max(0, j - w + 1), j + 1):
                pool[k, g, 0, j] += 1.0 / min(w, j + 1)
            for k in range(j - w + 1, j + 1):
                if k >= 0:
                    pool[k, g, 1, j] += 1.0 / w
                else:
                    pool[P + k, g, 2, j] += 1.0 / w
            pool[j, g, 0, j] -= 1
            pool[j, g, 1, j] -= 1
        for b in range(NB):
            for i in range(NQ):
                for k in range(i - w + 1, i + 1):
                    if k >= 0:
                        pool_own[P - NS + b * NQ + k, g, b * NQ + i] += 1.0 / w
                    else:
                        pool_ctx[b * CTX + CTX + k, g, b * NQ + i] += 1.0 / w
                pool_own[P - NS + b * NQ + i, g, b * NQ + i] -= 1
    return {
        "identity": np.eye(P, dtype=np.float32),
        "prompt_bias": prompt.astype(np.float32),
        "sample_bias_b": np.maximum(sample_b * 8, NEG).astype(np.float32),
        "sample_bias_a": np.maximum(sample_a * 8, NEG).astype(np.float32),
        "pool_band": pool.reshape(P, -1),
        "pool_own": pool_own.reshape(P, -1),
        "pool_ctx": pool_ctx.reshape(NB * CTX, -1),
    }


class Core:

    def __init__(self, nc, ctx):
        self.nc, self.ctx = nc, ctx
        self.stage_sems = []
        self.ps = ctx.enter_context(nc.psum_tensor("ps", [P, 8, 512], F32))
        self.identity = self.sb("identity", [P, P])
        self.ones = self.sb("ones", [P, P])
        self.minus_half = self.sb("minus_half", [P, 1])
        self.sample_oT = self.sb("sample_oT", [P, KT, NS])

    def sb(self, name, shape, dt=F32, ctx=None):
        return (ctx or self.ctx).enter_context(self.nc.sbuf_tensor(name, shape, dt))

    def sem(self, name):
        self.stage_sems.append(self.nc.alloc_semaphore(name=name))
        return self.stage_sems[-1]

    def end_stage(self):
        self.nc.clear_and_free_semaphores(self.stage_sems)
        self.stage_sems = []
        self.nc.all_engine_barrier()

    def banks(self, first, n, width=512):
        return self.ps[:, first:first + n, :].rearrange("p a b -> p (a b)")[:, 0:n * 512 if width == 512 else width]


def token_rows(prompt, sample, t):
    if t < PT:
        return [(slice(0, P), prompt[t * P:(t + 1) * P, :])]
    return [(slice(0, P - NS), prompt[SEQ - (P - NS):SEQ, :]), (slice(P - NS, P), sample[0:NS, :])]


def stored_rows(prompt, sample, t):
    return token_rows(prompt, sample, t) if t < PT else token_rows(prompt, sample, t)[1:]


def start(core, constants):
    nc = core.nc
    const_in = core.sem("const_in")
    with nc.Block() as block:
        @block.sync
        def _(sp):
            sp.dma_start(core.identity[:], constants["identity"]).then_inc(const_in, 16)
            sp.wait_ge(const_in, 16)

        @block.vector
        def _(dve):
            nc.vector.memset(core.ones[:], 1.0)
            nc.vector.memset(core.minus_half[:], -0.5)


def root(core, pool, ms, rstd, shifted, ready, t):
    nc = core.nc
    col = slice(t, t + 1)
    nc.gpsimd.tensor_scalar(ms[:, col], ms[:, col], EPS, None, ALU.add).then_inc(shifted, 1)
    pool.wait_ge(shifted, t + 1)
    nc.gpsimd.tensor_tensor(rstd[:, col], ms[:, col], core.minus_half[:], ALU.pow).then_inc(ready, 1)


def prepare(core, tag, x_prompt, x_sample, gain, xT_hi, xT_lo):
    nc = core.nc
    xs = 3
    with ExitStack() as mem:
        x = core.sb(tag + "x", [P, xs, D], F32, mem)
        xn = core.sb(tag + "xn", [P, 2, D], F32, mem)
        gain_b = core.sb(tag + "gain", [P, D], F32, mem)
        junk = core.sb(tag + "junk", [P, D], F32, mem)
        ms = core.sb(tag + "ms", [P, NT], F32, mem)
        rstd = core.sb(tag + "rstd", [P, NT], F32, mem)
        x_in = [core.sem(f"{tag}x_in{s}") for s in range(xs)]
        gain_in = core.sem(tag + "gain_in")
        squared = core.sem(tag + "squared")
        ms_shifted = core.sem(tag + "ms_shifted")
        rstd_ready = core.sem(tag + "rstd_ready")
        normed = core.sem(tag + "normed")
        turned = core.sem(tag + "turned")
        hi_done = core.sem(tag + "hi_done")
        lo_done = core.sem(tag + "lo_done")
        turned_ps = [core.banks(2 * i, 2).rearrange("p (k c) -> p k c", k=KT) for i in range(2)]

        with nc.Block() as block:
            @block.sync
            def _(sp):
                sp.dma_start(gain_b[:], gain.partition_broadcast(P)).then_inc(gain_in, 16)
                for t in range(NT):
                    if t >= xs:
                        sp.wait_ge(normed, t - xs + 1)
                    for rows, src in token_rows(x_prompt, x_sample, t):
                        sp.dma_start(x[rows, t % xs, :], src).then_inc(x_in[t % xs], 16)

            @block.scalar
            def _(act):
                def take_hi(t):
                    act.wait_ge(turned, t + 1)
                    c, new = new_columns(t)
                    nc.scalar.activation(xT_hi[:, :, c], turned_ps[t % 2][:, :, new], ACT.Copy).then_inc(hi_done, 1)

                for t in range(NT):
                    act.wait_ge(x_in[t % xs], 16 * (t // xs + 1 + (t == PT)))
                    if t >= 1:
                        act.wait_ge(squared, t)
                    nc.scalar.activation(junk[:], x[:, t % xs, :], ACT.Square, scale=1.0 / 32,
                                         accum_out=ms[:, t:t + 1]).then_inc(squared, 1)
                    if t >= 1:
                        take_hi(t - 1)
                take_hi(NT - 1)

            @block.gpsimd
            def _(pool):
                for t in range(NT):
                    pool.wait_ge(squared, t + 1)
                    root(core, pool, ms, rstd, ms_shifted, rstd_ready, t)

            @block.vector
            def _(dve):
                def take_lo(t):
                    dve.wait_ge(hi_done, t + 1)
                    c, new = new_columns(t)
                    nc.vector.tensor_tensor(xT_lo[:, :, c], turned_ps[t % 2][:, :, new],
                                            xT_hi[:, :, c].bitcast(F32), ALU.subtract).then_inc(lo_done, 1)

                for t in range(NT):
                    dve.wait_ge(rstd_ready, t + 1)
                    if t == 0:
                        dve.wait_ge(gain_in, 16)
                    if t >= 2:
                        dve.wait_ge(turned, t - 1)
                    nc.vector.scalar_tensor_tensor(xn[:, t % 2, :], x[:, t % xs, :], rstd[:, t:t + 1], gain_b[:],
                                                   ALU.mult, ALU.mult).then_inc(normed, 1)
                    if t >= 1:
                        take_lo(t - 1)
                take_lo(NT - 1)

            @block.tensor
            def _(pe):
                for t in range(NT):
                    pe.wait_ge(normed, t + 1)
                    if t >= 2:
                        pe.wait_ge(lo_done, t - 1)
                    for k in range(KT):
                        last = nc.tensor.transpose(turned_ps[t % 2][:, k, :], xn[:, t % 2, k * P:(k + 1) * P],
                                                   core.identity[:])
                    last.then_inc(turned, 1)


def in_project(core, w_in, xT_hi, xT_lo, qT, kaT, kbT, v, outs):
    nc = core.nc
    W = 256
    chunks = [4, 5, 6, 7, 8, 0, 1, 2, 3]
    NKV, NK = 5, 3
    w_rows = w_in.rearrange("(k p) n -> p k n", p=P)
    with ExitStack() as mem:
        raw = core.sb("in_raw", [P, 2, KT, W], F32, mem)
        w_hi = core.sb("in_w_hi", [P, 2, KT, W], F32R, mem)
        w_lo = core.sb("in_w_lo", [P, 2, KT, W], F32R, mem)
        ks = 3
        k_rows = core.sb("k_rows", [P, ks, W], F32, mem)
        raw_in = [core.sem(f"in_raw_in{s}") for s in range(2)]
        hi_done = core.sem("in_hi_done")
        lo_done = core.sem("in_lo_done")
        kv_ready = core.sem("in_kv_ready")
        kv_taken = core.sem("in_kv_taken")
        k_stored = [core.sem(f"in_k_stored{s}") for s in range(ks)]
        k_turned = core.sem("in_k_turned")
        kT_taken = core.sem("in_kT_taken")
        q_ready = core.sem("in_q_ready")
        q_taken = core.sem("in_q_taken")
        v_stored = core.sem("in_v_stored")

        def k_store(n, t):
            rows = slice(0, P) if t < PT else slice(P - NS, P)
            if n == 0:
                if t < PT - 1:
                    return None
                return (outs["prompt_a_k"] if t < PT else outs["sample_a_k"])[:, :], rows, slice(0, P)
            c = (n - 1) * W
            dst = outs["prompt_b_k"][t * P:(t + 1) * P, c:c + W] if t < PT else outs["sample_b_k"][:, c:c + W]
            return dst, rows, slice(0, W)

        stored_before = {}
        count = [0] * ks
        for i in range(NK * NT):
            stored_before[i] = count[i % ks]
            count[i % ks] += k_store(i // NT, i % NT) is not None

        arrived = [16 * sum(4 if chunks[j] < 2 else 1 for j in range(n % 2, n + 1, 2)) for n in range(len(chunks))]

        with nc.Block() as block:
            @block.sync
            def _(sp):
                for n, c in enumerate(chunks):
                    if n >= 2:
                        sp.wait_ge(lo_done, n - 1)
                    if c >= 2:
                        sp.dma_start(raw[:, n % 2], w_rows[:, :, c * W:(c + 1) * W]).then_inc(raw_in[n % 2], 16)
                        continue
                    for j in range(2):
                        for half in range(2):
                            src = half * W + (2 * c + j) * HD
                            dst = (2 * j + half) * HD
                            sp.dma_start(raw[:, n % 2, :, dst:dst + HD],
                                         w_rows[:, :, src:src + HD]).then_inc(raw_in[n % 2], 16)

            @block.gpsimd
            def _(pool):
                for i in range(NK * NT):
                    n, t = divmod(i, NT)
                    if (piece := k_store(n, t)) is not None:
                        dst, rows, cols = piece
                        pool.wait_ge(kv_taken, i + 1)
                        pool.dma_start(dst, k_rows[rows, i % ks, cols]).then_inc(k_stored[i % ks], 16)
                pool.wait_ge(kv_taken, NKV * NT)
                pool.dma_start(outs["prompt_b_v"].rearrange("(t p) n -> p t n", p=P),
                               v[:, 0:PT, P:]).then_inc(v_stored, 16)
                pool.dma_start(outs["prompt_a_v"], v[:, PT - 1, 0:P]).then_inc(v_stored, 16)
                pool.dma_start(outs["sample_b_v"], v[P - NS:P, PT, P:]).then_inc(v_stored, 16)
                pool.dma_start(outs["sample_a_v"], v[P - NS:P, PT, 0:P]).then_inc(v_stored, 16)
                pool.wait_ge(v_stored, 64)
                for s in range(ks):
                    pool.wait_ge(k_stored[s], 16 * count[s])

            @block.scalar
            def _(act):
                def split(n):
                    act.wait_ge(raw_in[n % 2], arrived[n])
                    if 2 <= n < NKV + 2:
                        act.wait_ge(kv_ready, NT * (n - 1))
                    elif n >= NKV + 2:
                        act.wait_ge(q_ready, 2 * (n - 1 - NKV))
                    nc.scalar.activation(w_hi[:, n % 2], raw[:, n % 2], ACT.Copy).then_inc(hi_done, 1)

                split(0)
                split(1)
                for n in range(NKV):
                    for t in range(NT):
                        i = n * NT + t
                        act.wait_ge(kv_ready, i + 1)
                        got = core.ps[:, 6 + i % 2, 0:W]
                        if n < NK:
                            if i >= ks:
                                act.wait_ge(k_turned, i - ks + 1)
                                if stored_before[i]:
                                    act.wait_ge(k_stored[i % ks], 16 * stored_before[i])
                            op = nc.scalar.activation(k_rows[:, i % ks, :], got, ACT.Copy)
                            if n == 0:
                                op = nc.scalar.activation(v[:, t, 0:P], got[:, P:W], ACT.Copy)
                        else:
                            c = P + (n - NK) * W
                            op = nc.scalar.activation(v[:, t, c:c + W], got, ACT.Copy)
                        op.then_inc(kv_taken, 1)
                    if n + 2 < len(chunks):
                        split(n + 2)
                for m in range(KT):
                    act.wait_ge(q_ready, m + 1)
                    for j, (c, w) in enumerate(TOKEN_CHUNKS):
                        op = nc.scalar.activation(qT[:, m, c:c + w], core.ps[:, 3 * (m % 2) + j, 0:w], ACT.Copy)
                    op.then_inc(q_taken, 1)
                    n = NKV + m // 2 + 2
                    if m % 2 == 1 and n < len(chunks):
                        split(n)

            @block.vector
            def _(dve):
                def lo(n):
                    dve.wait_ge(hi_done, n + 1)
                    nc.vector.tensor_tensor(w_lo[:, n % 2], raw[:, n % 2], w_hi[:, n % 2].bitcast(F32),
                                            ALU.subtract).then_inc(lo_done, 1)

                lo(0)
                lo(1)
                for n in range(NK):
                    for t in range(NT):
                        i = n * NT + t
                        dve.wait_ge(k_turned, i + 1)
                        c, new = new_columns(t)
                        if n == 0:
                            op = nc.vector.tensor_copy(kaT[:, c], core.ps[:, i % 2, new])
                        else:
                            j = 2 * (n - 1)
                            op = nc.vector.tensor_copy(kbT[:, j:j + 2, c], core.ps[:, i % 2, 0:W].rearrange(
                                "p (j c) -> p j c", j=2)[:, :, new])
                        op.then_inc(kT_taken, 1)
                    lo(n + 2)
                for n in range(NK + 2, len(chunks)):
                    lo(n)

            @block.tensor
            def _(pe):
                def turn(i):
                    n = i // NT
                    pe.wait_ge(kv_taken, i + 1)
                    if i >= 2:
                        pe.wait_ge(kT_taken, i - 1)
                    for j in range(1 if n == 0 else 2):
                        last = nc.tensor.transpose(core.ps[:, i % 2, j * P:(j + 1) * P],
                                                   k_rows[:, i % ks, j * P:(j + 1) * P], core.identity[:])
                    last.then_inc(k_turned, 1)

                for n in range(NKV):
                    pe.wait_ge(lo_done, n + 1)
                    for t in range(NT):
                        i = n * NT + t
                        if i >= 2:
                            pe.wait_ge(kv_taken, i - 1)
                        c = tile_start(t)
                        for k in range(KT):
                            for a, b in ((xT_hi, w_hi), (xT_hi, w_lo), (xT_lo, w_hi)):
                                last = nc.tensor.matmul(core.ps[:, 6 + i % 2, 0:W], a[:, k, c:c + P], b[:, n % 2, k, :],
                                                        start=(k == 0 and b is w_hi and a is xT_hi),
                                                        stop=(k == KT - 1 and a is xT_lo))
                        last.then_inc(kv_ready, 1)
                        if 1 <= i <= NK * NT:
                            turn(i - 1)
                for m in range(KT):
                    n = NKV + m // 2
                    pe.wait_ge(lo_done, n + 1)
                    if m == 0:
                        pe.wait_ge(kT_taken, NK * NT)
                    if m >= 2:
                        pe.wait_ge(q_taken, m - 1)
                    for k in range(KT):
                        for a, b in ((w_hi, xT_hi), (w_hi, xT_lo), (w_lo, xT_hi)):
                            lhs = a[:, n % 2, k, (m % 2) * P:(m % 2 + 1) * P]
                            for j, (c, w) in enumerate(TOKEN_CHUNKS):
                                last = nc.tensor.matmul(core.ps[:, 3 * (m % 2) + j, 0:w], lhs, b[:, k, c:c + w],
                                                        start=(k == 0 and a is w_hi and b is xT_hi),
                                                        stop=(k == KT - 1 and a is w_lo))
                    last.then_inc(q_ready, 1)


def prompt_attention(core, qT, kaT, kbT, v, prompt_bias, sinks, o_rows):
    nc = core.nc
    SB = 4
    LAG = 3
    WA, WB = 2 * P, SEQ
    with ExitStack() as mem:
        bias = core.sb("pa_bias", [P, NH * (WA + WB)], F32, mem)
        bias_a = bias[:, 0:NH * WA].rearrange("p (h c) -> p h c", h=NH)
        bias_b = bias[:, NH * WA:].rearrange("p (h c) -> p h c", h=NH)
        sink_b = core.sb("pa_sink", [P, NH], F32, mem)
        s = core.sb("pa_s", [P, SB, SEQ], F32, mem)
        pT = core.sb("pa_pT", [P, 2, 4 * P], F32, mem)
        o = core.sb("pa_o", [P, 2, D], F32, mem)
        m = core.sb("pa_m", [P, PT, 2 * NH], F32, mem)
        neg_m = core.sb("pa_neg_m", [P, PT, 2 * NH], F32, mem)
        den = core.sb("pa_den", [P, PT, 2 * NH], F32, mem)
        e_sink = core.sb("pa_e_sink", [P, PT, NH], F32, mem)
        rden = core.sb("pa_rden", [P, PT, 2 * NH], F32, mem)
        tables_in = core.sem("pa_tables_in")
        scored = core.sem("pa_scored")
        biased = core.sem("pa_biased")
        negated = core.sem("pa_negated")
        exped = core.sem("pa_exped")
        turned = core.sem("pa_turned")
        copied = [core.sem("pa_copied_act"), core.sem("pa_copied_dve")]
        multiplied = core.sem("pa_multiplied")
        sink_shifted = core.sem("pa_sink_shifted")
        sink_exped = core.sem("pa_sink_exped")
        den_ready = core.sem("pa_den_ready")
        rden_ready = core.sem("pa_rden_ready")
        o_ready = core.sem("pa_o_ready")
        o_stored = [core.sem(f"pa_o_stored{x}") for x in range(2)]

        units = [(i, h) for i in range(PT) for h in range(2 * NH)]
        U = len(units)

        def first_tile(u):
            i, h = units[u]
            return 0 if h >= NH else max(0, i - 1)

        def n_tiles(u):
            return units[u][0] + 1 - first_tile(u)

        groups = [(u, g, min(4, n_tiles(u) - g)) for u in range(U) for g in range(0, n_tiles(u), 4)]
        first_group = {}
        for n, (u, _, _) in enumerate(groups):
            first_group.setdefault(u, n)
        last_group = {u: n for n, (u, _, _) in enumerate(groups)}

        def score_ps(u):
            return core.banks(2 * (u % 2), 2)[:, 0:n_tiles(u) * P]

        def copies_before(n, which):
            return (n - which) // 2 + 1

        with nc.Block() as block:
            @block.sync
            def _(sp):
                sp.dma_start(bias[:], prompt_bias).then_inc(tables_in, 16)
                sp.dma_start(sink_b[:], sinks.partition_broadcast(P)).then_inc(tables_in, 16)
                for i in range(PT):
                    sp.wait_ge(o_ready, 2 * (i + 1))
                    sp.dma_start(o_rows[i * P:(i + 1) * P, :], o[:, i % 2, :]).then_inc(o_stored[i % 2], 16)
                for x in range(2):
                    sp.wait_ge(o_stored[x], 16 * (PT // 2))

            @block.scalar
            def _(act):
                def copy(n):
                    u, _, k = groups[n]
                    act.wait_ge(turned, n + 1)
                    if n >= 2:
                        act.wait_ge(multiplied, n - 1)
                    nc.scalar.activation(pT[:, n % 2, 0:k * P], core.ps[:, 4 + n % 2, 0:k * P],
                                         ACT.Copy).then_inc(copied[0], 1)

                for step in range(U + LAG):
                    if step < U:
                        u = step
                        i, h = units[u]
                        act.wait_ge(negated, u + 1)
                        row = s[:, u % SB, 0:n_tiles(u) * P]
                        nc.scalar.activation(row, row, ACT.Exp, bias=neg_m[:, i, h:h + 1],
                                             accum_out=den[:, i, h:h + 1]).then_inc(exped, 1)
                        if h == 2 * NH - 1:
                            act.wait_ge(sink_shifted, i + 1)
                            nc.scalar.activation(e_sink[:, i], e_sink[:, i], ACT.Exp).then_inc(sink_exped, 1)
                    if step >= LAG:
                        for n in range(first_group[step - LAG], last_group[step - LAG] + 1):
                            if n % 2 == 0:
                                copy(n)

            @block.vector
            def _(dve):
                dve.wait_ge(tables_in, 32)
                for step in range(U + LAG + 1):
                    if step < U:
                        u = step
                        i, h = units[u]
                        w = n_tiles(u) * P
                        dve.wait_ge(scored, u + 1)
                        if u >= SB:
                            dve.wait_ge(turned, last_group[u - SB] + 1)
                        if h < NH:
                            table, least = bias_a[:, h, WA - w:WA], sink_b[:, h:h + 1]
                        else:
                            table, least = bias_b[:, h - NH, WB - w:WB], NEG
                        nc.vector.tensor_tensor_reduce(s[:, u % SB, 0:w], score_ps(u), table, 0.125, least,
                                                       ALU.add, ALU.max, m[:, i, h:h + 1]).then_inc(biased, 1)
                        dve.wait_ge(biased, u + 1)
                        nc.vector.tensor_scalar(neg_m[:, i, h:h + 1], m[:, i, h:h + 1], -1.0, None,
                                                ALU.mult).then_inc(negated, 1)
                        if h == 2 * NH - 1:
                            nc.vector.tensor_tensor(e_sink[:, i], sink_b[:], m[:, i, 0:NH],
                                                    ALU.subtract).then_inc(sink_shifted, 1)
                    if LAG <= step < U + LAG:
                        for n in range(first_group[step - LAG], last_group[step - LAG] + 1):
                            if n % 2 == 1:
                                dve.wait_ge(turned, n + 1)
                                if n >= 2:
                                    dve.wait_ge(multiplied, n - 1)
                                k = groups[n][2]
                                nc.vector.tensor_copy(pT[:, n % 2, 0:k * P],
                                                      core.ps[:, 4 + n % 2, 0:k * P]).then_inc(copied[1], 1)
                    if step >= LAG + 1 and units[step - LAG - 1][1] == 2 * NH - 1:
                        u = step - LAG - 1
                        i = units[u][0]
                        dve.wait_ge(sink_exped, i + 1)
                        dve.wait_ge(exped, u + 1)
                        nc.vector.tensor_tensor(den[:, i, 0:NH], den[:, i, 0:NH], e_sink[:, i],
                                                ALU.add).then_inc(den_ready, 1)
                        dve.wait_ge(den_ready, i + 1)
                        nc.vector.reciprocal(rden[:, i], den[:, i]).then_inc(rden_ready, 1)
                        dve.wait_ge(rden_ready, i + 1)
                        dve.wait_ge(multiplied, last_group[u] + 1)
                        if i >= 2:
                            dve.wait_ge(o_stored[i % 2], 16 * (i // 2))
                        r_a = rden[:, i, 0:NH].rearrange("p (s j) -> p j s", s=2).unsqueeze(3)
                        nc.vector.tensor_tensor(
                            o[:, i % 2, 0:NH * HD].rearrange("p (j s d) -> p j s d", j=4, s=2),
                            core.ps[:, 6, :].rearrange("p (j s d) -> p j s d", j=4, s=2),
                            r_a.to_broadcast([P, 4, 2, HD]), ALU.mult).then_inc(o_ready, 1)
                        r_b = rden[:, i, NH:].unsqueeze(2)
                        nc.vector.tensor_tensor(
                            o[:, i % 2, NH * HD:].rearrange("p (h d) -> p h d", h=NH),
                            core.ps[:, 7, :].rearrange("p (h d) -> p h d", h=NH),
                            r_b.to_broadcast([P, NH, HD]), ALU.mult).then_inc(o_ready, 1)

            @block.tensor
            def _(pe):
                def scores(u):
                    i, h = units[u]
                    if u >= 2:
                        pe.wait_ge(biased, u - 1)
                    j, half = (h % 4, h // 4) if h < NH else (h // 2, h % 2)
                    rows = slice(half * HD, (half + 1) * HD)
                    kT = kaT[rows, :] if h < NH else kbT[rows, j - 4, :]
                    w, k0 = n_tiles(u) * P, first_tile(u) * P
                    for c in range(0, w, 512):
                        e = min(w, c + 512)
                        last = nc.tensor.matmul(score_ps(u)[:, c:e], qT[rows, j, i * P:(i + 1) * P],
                                                kT[:, k0 + c:k0 + e], start=True, stop=True)
                    last.then_inc(scored, 1)

                def turn(n):
                    u, g, k = groups[n]
                    if g == 0:
                        pe.wait_ge(exped, u + 1)
                    if n >= 2:
                        pe.wait_ge(copied[n % 2], copies_before(n - 2, n % 2))
                    for t in range(k):
                        last = nc.tensor.transpose(core.ps[:, 4 + n % 2, t * P:(t + 1) * P],
                                                   s[:, u % SB, (g + t) * P:(g + t + 1) * P], core.identity[:])
                    last.then_inc(turned, 1)

                def multiply(n):
                    u, g, k = groups[n]
                    i, h = units[u]
                    if g == 0 and h % NH == 0 and i >= 1:
                        pe.wait_ge(o_ready, 2 * i)
                    pe.wait_ge(copied[n % 2], copies_before(n, n % 2))
                    col = (h % 4) * P + (h // 4) * HD if h < NH else (h - NH) * HD
                    vc = (h // 4) * HD if h < NH else P + (h - NH) * HD
                    for t in range(k):
                        kt = first_tile(u) + g + t
                        last = nc.tensor.matmul(core.ps[:, 6 + h // NH, col:col + HD], pT[:, n % 2, t * P:(t + 1) * P],
                                                v[:, kt, vc:vc + HD], start=(g + t == 0), stop=(g + t == n_tiles(u) - 1))
                    last.then_inc(multiplied, 1)

                for step in range(U + LAG):
                    if step < U:
                        scores(step)
                    if step >= LAG:
                        for n in range(first_group[step - LAG], last_group[step - LAG] + 1):
                            turn(n)
                            if n >= 1:
                                multiply(n - 1)
                multiply(len(groups) - 1)


def sample_attention(core, qT, kaT, kbT, v, cache, sinks, bias_b, bias_a):
    nc = core.nc
    HQ = NH * NQ
    PAIRS = NH // 2
    W = CT * P
    OWN = W + P
    RING = 3
    with ExitStack() as mem:
        kb = core.sb("sa_kb", [P, CT, 512], F32, mem)
        vb = core.sb("sa_vb", [P, 2, CT, 512], F32, mem)
        ka = core.sb("sa_ka", [P, 2, P], F32, mem)
        va = core.sb("sa_va", [P, 2, P], F32, mem)
        kT = core.sb("sa_kT", [P, CT, PAIRS, P], F32, mem)
        kT_a = core.sb("sa_kT_a", [P, P], F32, mem)
        q_b = core.sb("sa_q_b", [P, NB, PAIRS, 32], F32, mem)
        q_a = core.sb("sa_q_a", [P, NB, HQ], F32, mem)
        table_b = core.sb("sa_table_b", [P, W + NQ], F32, mem)
        table_a = core.sb("sa_table_a", [HQ, P + NQ], F32, mem)
        sink = core.sb("sa_sink", [HQ, 1], F32, mem)
        pb = core.sb("sa_pb", [P, 2, OWN], F32, mem)
        pa = core.sb("sa_pa", [HQ, 2, 2 * P], F32, mem)
        pT = core.sb("sa_pT", [P, CT + 1, P], F32, mem)
        pT_a = core.sb("sa_pT_a", [P, 2, HQ], F32, mem)
        m_cache = core.sb("sa_m_cache", [P, NB, 2], F32, mem)
        m = core.sb("sa_m", [P, NB, 2], F32, mem)
        neg_m = core.sb("sa_neg_m", [P, NB, 2], F32, mem)
        den = core.sb("sa_den", [P, NB, 5], F32, mem)
        den_sum = core.sb("sa_den_sum", [P, NB, 2], F32, mem)
        rden = core.sb("sa_rden", [P, NB, 2], F32, mem)
        o = core.sb("sa_o", [P, 2 * P], F32, mem)

        kb_in = [core.sem(f"sa_kb_in{t}") for t in range(CT)]
        ka_in = [core.sem(f"sa_ka_in{x}") for x in range(2)]
        v_in = [core.sem(f"sa_v_in{x}") for x in range(2)]
        tables_in = core.sem("sa_tables_in")
        cleared = core.sem("sa_cleared")
        q_ready = core.sem("sa_q_ready")
        own_cleared = core.sem("sa_own_cleared")
        keys_turned = core.sem("sa_keys_turned")
        copied = [core.sem("sa_copied_act"), core.sem("sa_copied_dve")]
        scored = core.sem("sa_scored")
        cache_biased = core.sem("sa_cache_biased")
        biased = core.sem("sa_biased")
        negated = core.sem("sa_negated")
        exped = core.sem("sa_exped")
        den_ready = core.sem("sa_den_ready")
        rden_ready = core.sem("sa_rden_ready")
        normed = core.sem("sa_normed")
        probs_turned = core.sem("sa_probs_turned")
        multiplied = core.sem("sa_multiplied")
        o_copied = core.sem("sa_o_copied")
        o_turned = core.sem("sa_o_turned")
        o_taken = core.sem("sa_o_taken")

        KG = CT + 1
        PG = [(0, 4), (4, 4), (8, 3), (None, 2)]
        order = []
        for b in range(NB + 1):
            if b < NB:
                order += [("key", b, t) for t in range(KG)]
            if b >= 1:
                order += [("prob", b - 1, g) for g in range(len(PG))]
        at = {x: n for n, x in enumerate(order)}

        def bank(n):
            return n % RING

        def copied_by(n):
            return copied[n % 2], n // 2 + 1

        def copy_entry(copy, n):
            kind, b, x = order[n]
            if kind == "key" and x < CT:
                return copy(kT[:, x], core.ps[:, bank(n), :].rearrange("p (c k) -> p c k", c=PAIRS))
            if kind == "key":
                return copy(kT_a[:], core.ps[:, bank(n), 0:P])
            first, count = PG[x]
            if first is None:
                return copy(pT_a[:], core.ps[:, bank(n), 0:2 * HQ].rearrange("p (t r) -> p t r", t=2))
            return copy(pT[:, first:first + count, :],
                        core.ps[:, bank(n), 0:count * P].rearrange("p (t r) -> p t r", t=count))

        def wait_for_entry(eng, n):
            kind, b, x = order[n]
            if kind == "key":
                eng.wait_ge(keys_turned, KG * b + x + 1)
                if b >= 1:
                    eng.wait_ge(scored, b)
            else:
                eng.wait_ge(probs_turned, len(PG) * b + x + 1)
                if b >= 1:
                    eng.wait_ge(multiplied, b)

        score_b = core.banks(4, 3)
        score_a = core.ps[0:HQ, 7, 0:P + NQ]

        with nc.Block() as block:
            @block.sync
            def _(sp):
                sp.dma_start(ka[:, 0, :], cache["a_k"][0]).then_inc(ka_in[0], 16)
                for b in range(NB):
                    far = cache["b_k"][b].rearrange("(t m s) c -> t m s c", m=16, s=16)
                    for t in range(CT):
                        if b >= 1:
                            sp.wait_ge(keys_turned, KG * (b - 1) + t + 1)
                        src = far[t, :, 0:8, :] if t < FAR_TILES else \
                            cache["b_k"][b, FAR + (t - FAR_TILES) * P:FAR + (t - FAR_TILES + 1) * P, :]
                        sp.dma_start(kb[:, t, :], src).then_inc(kb_in[t], 16)
                    if b == 0:
                        sp.dma_start(table_b[:], bias_b).then_inc(tables_in, 16)
                        sp.dma_start(table_a[:], bias_a).then_inc(tables_in, 16)
                        for h in range(NH):
                            sp.dma_start(sink[h * NQ:(h + 1) * NQ, :],
                                         sinks[h:h + 1].partition_broadcast(NQ)).then_inc(tables_in, 16)
                    if b >= 2:
                        sp.wait_ge(multiplied, b - 1)
                    far = cache["b_v"][b].rearrange("(t m s) c -> t m s c", m=16, s=16)
                    for t in range(FAR_TILES):
                        sp.dma_start(vb[:, b % 2, t, :], far[t, :, 0:8, :]).then_inc(v_in[b % 2], 16)
                    sp.dma_start(vb[:, b % 2, FAR_TILES:CT, :],
                                 cache["b_v"][b, FAR:PAST, :].rearrange("(t p) c -> p t c", p=P)).then_inc(v_in[b % 2], 16)
                    sp.dma_start(va[:, b % 2, :], cache["a_v"][b]).then_inc(v_in[b % 2], 16)
                    if b + 1 < NB:
                        if b >= 1:
                            sp.wait_ge(keys_turned, KG * b)
                        sp.dma_start(ka[:, (b + 1) % 2, :], cache["a_k"][b + 1]).then_inc(ka_in[(b + 1) % 2], 16)

            @block.gpsimd
            def _(pool):
                for b in range(NB):
                    if b >= 2:
                        pool.wait_ge(probs_turned, len(PG) * (b - 1))
                    nc.gpsimd.memset(pb[:, b % 2, W:OWN], 0.0)
                    nc.gpsimd.memset(pa[:, b % 2, P:2 * P], 0.0).then_inc(own_cleared, 1)

            @block.scalar
            def _(act):
                def copies(kind, b, count):
                    for x in range(count):
                        n = at[kind, b, x]
                        if n % 2 == 0:
                            wait_for_entry(act, n)
                            copy_entry(lambda out, in_: nc.scalar.activation(out, in_, ACT.Copy), n).then_inc(copied[0], 1)

                def exps(b):
                    act.wait_ge(negated, b + 1)
                    own = slice(W + P - NS + b * NQ, W + P - NS + (b + 1) * NQ)
                    own_a = slice(own.start - W + P, own.stop - W + P)
                    x = b % 2
                    nb, na = neg_m[:, b, 0:1], neg_m[0:HQ, b, 1:2]
                    nc.scalar.activation(pb[:, x, 0:W], pb[:, x, 0:W], ACT.Exp, bias=nb, accum_out=den[:, b, 0:1])
                    nc.scalar.activation(pb[:, x, own], pb[:, x, own], ACT.Exp, bias=nb, accum_out=den[:, b, 2:3])
                    nc.scalar.activation(pa[:, x, 0:P], pa[:, x, 0:P], ACT.Exp, bias=na, accum_out=den[0:HQ, b, 1:2])
                    nc.scalar.activation(pa[:, x, own_a], pa[:, x, own_a], ACT.Exp, bias=na, accum_out=den[0:HQ, b, 3:4])
                    nc.scalar.activation(den[0:HQ, b, 4:5], sink[:], ACT.Exp, bias=na).then_inc(exped, 1)

                for b in range(NB + 1):
                    if b < NB:
                        copies("key", b, KG)
                    if b >= 1:
                        copies("prob", b - 1, len(PG))
                    if b < NB:
                        exps(b)

            @block.vector
            def _(dve):
                def copies(kind, b, count):
                    for x in range(count):
                        n = at[kind, b, x]
                        if n % 2 == 1:
                            wait_for_entry(dve, n)
                            copy_entry(nc.vector.tensor_copy, n).then_inc(copied[1], 1)

                def softmax(b):
                    x = b % 2
                    own = slice(W + P - NS + b * NQ, W + P - NS + (b + 1) * NQ)
                    own_a = slice(own.start - W + P, own.stop - W + P)
                    dve.wait_ge(scored, b + 1)
                    dve.wait_ge(own_cleared, b + 1)
                    if b >= 2:
                        dve.wait_ge(probs_turned, len(PG) * (b - 1))
                    nc.vector.tensor_tensor_reduce(pb[:, x, 0:W], score_b[:, 0:W], table_b[:, 0:W], 0.125, NEG,
                                                   ALU.add, ALU.max, m_cache[:, b, 0:1]).then_inc(cache_biased, 1)
                    nc.vector.tensor_tensor_reduce(pa[:, x, 0:P], score_a[:, 0:P], table_a[:, 0:P], 0.125, sink[:, 0:1],
                                                   ALU.add, ALU.max, m_cache[0:HQ, b, 1:2]).then_inc(cache_biased, 1)
                    dve.wait_ge(cache_biased, 2 * (b + 1))
                    nc.vector.tensor_tensor_reduce(pb[:, x, own], score_b[:, W:W + NQ], table_b[:, W:W + NQ], 0.125,
                                                   m_cache[:, b, 0:1], ALU.add, ALU.max, m[:, b, 0:1]).then_inc(biased, 1)
                    nc.vector.tensor_tensor_reduce(pa[:, x, own_a], score_a[:, P:P + NQ], table_a[:, P:P + NQ], 0.125,
                                                   m_cache[0:HQ, b, 1:2], ALU.add, ALU.max,
                                                   m[0:HQ, b, 1:2]).then_inc(biased, 1)
                    dve.wait_ge(biased, 2 * (b + 1))
                    nc.vector.tensor_scalar(neg_m[:, b], m[:, b], -1.0, None, ALU.mult).then_inc(negated, 1)

                def normalise(b):
                    x = b % 2
                    dve.wait_ge(exped, b + 1)
                    nc.vector.tensor_tensor(den_sum[:, b], den[:, b, 0:2], den[:, b, 2:4], ALU.add).then_inc(den_ready, 1)
                    dve.wait_ge(den_ready, 2 * b + 1)
                    nc.vector.tensor_tensor(den_sum[0:HQ, b, 1:2], den_sum[0:HQ, b, 1:2], den[0:HQ, b, 4:5],
                                            ALU.add).then_inc(den_ready, 1)
                    dve.wait_ge(den_ready, 2 * b + 2)
                    nc.vector.reciprocal(rden[:, b], den_sum[:, b]).then_inc(rden_ready, 1)
                    dve.wait_ge(rden_ready, b + 1)
                    nc.vector.tensor_scalar(pb[:, x, :], pb[:, x, :], rden[:, b, 0:1], None, ALU.mult)
                    nc.vector.tensor_scalar(pa[:, x, :], pa[:, x, :], rden[0:HQ, b, 1:2], None,
                                            ALU.mult).then_inc(normed, 1)

                def o_copy(b):
                    dve.wait_ge(multiplied, b + 1)
                    if b >= 1:
                        dve.wait_ge(o_turned, b)
                    nc.vector.tensor_copy(o[:, 0:P], core.ps[:, 3, 0:P])
                    nc.vector.tensor_copy(o[0:HQ, P:2 * P], core.ps[0:HQ, 3, P:2 * P]).then_inc(o_copied, 1)

                def o_take(b):
                    dve.wait_ge(o_turned, b + 1)
                    for half in range(2):
                        rows = slice(half * HD, (half + 1) * HD)
                        out = core.sample_oT[rows, :, b * NQ:(b + 1) * NQ]
                        got_b = core.ps[rows, 3, 2 * P:3 * P].rearrange("p (c x) -> p c x", c=PAIRS)
                        got_a = core.ps[rows, 3, 3 * P:3 * P + HQ].rearrange("p (s j i) -> p s j i", s=2, j=PAIRS)
                        nc.vector.tensor_copy(out[:, PAIRS:, :], got_b[:, :, half * NQ:(half + 1) * NQ])
                        last = nc.vector.tensor_copy(out[:, 0:PAIRS, :], got_a[:, half])
                    last.then_inc(o_taken, 1)

                for tile in (q_b, q_a, m, den, m_cache):
                    nc.vector.memset(tile[:], 0.0 if tile in (q_b, q_a) else 1.0).then_inc(cleared, 1)
                dve.wait_ge(cleared, 5)
                for half in range(2):
                    rows = slice(half * HD, (half + 1) * HD)
                    for j in range(PAIRS):
                        c = half * HQ // 2 + j * NQ
                        nc.vector.tensor_copy(q_a[rows, :, c:c + NQ],
                                              qT[rows, j, SEQ:TOK].rearrange("p (b i) -> p b i", b=NB))
                        nc.vector.tensor_copy(q_b[rows, :, j, half * NQ:(half + 1) * NQ],
                                              qT[rows, PAIRS + j, SEQ:TOK].rearrange("p (b i) -> p b i", b=NB)
                                              ).then_inc(q_ready, 1)
                for b in range(NB + 2):
                    if b < NB:
                        copies("key", b, KG)
                    if b >= 2:
                        o_take(b - 2)
                    if 1 <= b <= NB:
                        copies("prob", b - 1, len(PG))
                    if b < NB:
                        if b == 0:
                            dve.wait_ge(tables_in, 16 * (2 + NH))
                        softmax(b)
                    if 1 <= b <= NB:
                        o_copy(b - 1)
                    if b < NB:
                        normalise(b)

            @block.tensor
            def _(pe):
                def bank_free(n):
                    if n >= RING:
                        pe.wait_ge(*copied_by(n - RING))

                def turn_keys(b):
                    for t in range(KG):
                        n = at["key", b, t]
                        bank_free(n)
                        if t < CT:
                            pe.wait_ge(kb_in[t], 16 * (b + 1))
                            for c in range(PAIRS):
                                last = nc.tensor.transpose(core.ps[:, bank(n), c * P:(c + 1) * P],
                                                           kb[:, t, c * P:(c + 1) * P], core.identity[:])
                        else:
                            pe.wait_ge(ka_in[b % 2], 16 * (b // 2 + 1))
                            last = nc.tensor.transpose(core.ps[:, bank(n), 0:P], ka[:, b % 2, :], core.identity[:])
                        last.then_inc(keys_turned, 1)

                def score(b):
                    for n in (at["key", b, KG - 1], at["key", b, KG - 2]):
                        pe.wait_ge(*copied_by(n))
                    if b >= 1:
                        pe.wait_ge(biased, 2 * b)
                    own = slice(SEQ + b * NQ, SEQ + (b + 1) * NQ)
                    for t in range(0, CT, 4):
                        e = min(CT, t + 4)
                        for c in range(PAIRS):
                            nc.tensor.matmul(score_b[32 * c:32 * c + 32, t * P:e * P], q_b[:, b, c, :], kT[:, t:e, c, :],
                                             start=True, stop=True)
                    for c in range(PAIRS):
                        nc.tensor.matmul(score_b[32 * c:32 * c + 32, W:W + NQ], q_b[:, b, c, :], kbT[:, c, own],
                                         start=True, stop=True)
                    nc.tensor.matmul(score_a[:, 0:P], q_a[:, b, :], kT_a[:], start=True, stop=True)
                    nc.tensor.matmul(score_a[:, P:P + NQ], q_a[:, b, :], kaT[:, own], start=True,
                                     stop=True).then_inc(scored, 1)

                def turn_probs(b):
                    pe.wait_ge(normed, b + 1)
                    for g, (first, count) in enumerate(PG):
                        n = at["prob", b, g]
                        bank_free(n)
                        for x in range(count):
                            if first is None:
                                last = nc.tensor.transpose(core.ps[:, bank(n), x * HQ:(x + 1) * HQ],
                                                           pa[:, b % 2, x * P:(x + 1) * P], core.identity[0:HQ, 0:HQ])
                            else:
                                last = nc.tensor.transpose(core.ps[:, bank(n), x * P:(x + 1) * P],
                                                           pb[:, b % 2, (first + x) * P:(first + x + 1) * P],
                                                           core.identity[:])
                        last.then_inc(probs_turned, 1)

                def multiply(b):
                    pe.wait_ge(v_in[b % 2], 16 * (FAR_TILES + 2) * (b // 2 + 1))
                    if b >= 1:
                        pe.wait_ge(o_taken, b)
                    for g in range(len(PG)):
                        pe.wait_ge(*copied_by(at["prob", b, g]))
                    nc.tensor.matmul(core.ps[0:HQ, 3, P:2 * P], pT_a[:, 0, :], va[:, b % 2, :], start=True, stop=False)
                    nc.tensor.matmul(core.ps[0:HQ, 3, P:2 * P], pT_a[:, 1, :], v[:, PT, 0:P], start=False, stop=True)
                    for t in range(CT + 1):
                        for c in range(PAIRS):
                            rhs = vb[:, b % 2, t, c * P:(c + 1) * P] if t < CT else v[:, PT, P + c * P:P + (c + 1) * P]
                            last = nc.tensor.matmul(core.ps[32 * c:32 * c + 32, 3, 0:P], pT[:, t, 32 * c:32 * c + 32],
                                                    rhs, start=(t == 0), stop=(t == CT))
                    last.then_inc(multiplied, 1)

                def turn_outputs(b):
                    pe.wait_ge(o_copied, b + 1)
                    nc.tensor.transpose(core.ps[:, 3, 2 * P:3 * P], o[:, 0:P], core.identity[:])
                    nc.tensor.transpose(core.ps[:, 3, 3 * P:3 * P + HQ], o[0:HQ, P:2 * P],
                                        core.identity[0:HQ, 0:HQ]).then_inc(o_turned, 1)

                pe.wait_ge(q_ready, 2 * PAIRS)
                for b in range(NB + 2):
                    if b < NB:
                        turn_keys(b)
                    if b >= 2:
                        turn_outputs(b - 2)
                    if b < NB:
                        score(b)
                    if 1 <= b <= NB:
                        turn_probs(b - 1)
                        multiply(b - 1)


class PostNorm:

    def __init__(self, core, tag, mem):
        self.x = core.sb(tag + "res", [P, 2, D], F32, mem)
        self.yn = core.sb(tag + "yn", [P, D], F32, mem)
        self.gain = core.sb(tag + "post_gain", [P, D], F32, mem)
        self.junk = core.sb(tag + "post_junk", [P, D], F32, mem)
        self.ms = core.sb(tag + "post_ms", [P, NT], F32, mem)
        self.rstd = core.sb(tag + "post_rstd", [P, NT], F32, mem)
        self.gain_in = core.sem(tag + "post_gain_in")
        self.x_in = [core.sem(f"{tag}res_in{s}") for s in range(2)]
        self.squared = core.sem(tag + "post_squared")
        self.ms_shifted = core.sem(tag + "post_ms_shifted")
        self.rstd_ready = core.sem(tag + "post_rstd_ready")
        self.scaled = core.sem(tag + "post_scaled")
        self.added = core.sem(tag + "post_added")
        self.stored = [core.sem(f"{tag}post_stored{s}") for s in range(2)]


def load_residual(sp, pn, src, t):
    if t >= 2:
        sp.wait_ge(pn.stored[t % 2], 16 * (t // 2))
    for rows, piece in token_rows(*src, t):
        sp.dma_start(pn.x[rows, t % 2, :], piece).then_inc(pn.x_in[t % 2], 16)


def store_residual(sp, pn, dst, t):
    sp.wait_ge(pn.added, t + 1)
    for rows, piece in stored_rows(*dst, t):
        sp.dma_start(piece, pn.x[rows, t % 2, :]).then_inc(pn.stored[t % 2], 16)


def square_of_y(nc, act, pn, y, t):
    if t >= 1:
        act.wait_ge(pn.squared, t)
    nc.scalar.activation(pn.junk[:], y, ACT.Square, scale=1.0 / 32,
                         accum_out=pn.ms[:, t:t + 1]).then_inc(pn.squared, 1)


def rstd_of_y(core, pool, pn, t):
    pool.wait_ge(pn.squared, t + 1)
    root(core, pool, pn.ms, pn.rstd, pn.ms_shifted, pn.rstd_ready, t)


def add_normed(nc, dve, pn, y, t):
    if t == 0:
        dve.wait_ge(pn.gain_in, 16)
    dve.wait_ge(pn.rstd_ready, t + 1)
    if t >= 1:
        dve.wait_ge(pn.added, t)
    nc.vector.scalar_tensor_tensor(pn.yn[:], y, pn.rstd[:, t:t + 1], pn.gain[:], ALU.mult, ALU.mult).then_inc(pn.scaled, 1)
    dve.wait_ge(pn.scaled, t + 1)
    dve.wait_ge(pn.x_in[t % 2], 16 * (t // 2 + 1 + (t == PT)))
    nc.vector.tensor_tensor(pn.x[:, t % 2, :], pn.x[:, t % 2, :], pn.yn[:], ALU.add).then_inc(pn.added, 1)


def wait_stored(sp, pn):
    sp.wait_ge(pn.stored[0], 16 * (PT // 2 + 1))
    sp.wait_ge(pn.stored[1], 16 * (PT // 2))


def out_project(core, o_rows, w_out, x_src, x_dst, gain):
    nc = core.nc
    with ExitStack() as mem:
        oT_hi = core.sb("oT_hi", [P, KT, TOK], F32R, mem)
        oT_lo = core.sb("oT_lo", [P, KT, TOK], F32R, mem)
        w_hi = core.sb("out_w_hi", [P, KT, D], F32R, mem)
        w_lo = core.sb("out_w_lo", [P, KT, D], F32R, mem)
        raws = 2
        raw = core.sb("out_raw", [P, raws, D], F32, mem)
        o = core.sb("out_o", [P, 2, D], F32, mem)
        pn = PostNorm(core, "out_", mem)
        raw_in = [core.sem(f"out_raw_in{s}") for s in range(raws)]
        o_in = [core.sem(f"out_o_in{s}") for s in range(2)]
        w_hi_done = core.sem("out_w_hi_done")
        w_lo_done = core.sem("out_w_lo_done")
        turned = core.sem("out_turned")
        o_hi_done = core.sem("out_o_hi_done")
        o_lo_done = core.sem("out_o_lo_done")
        y_ready = core.sem("out_y_ready")
        turned_ps = [core.banks(2 * i, 2).rearrange("p (k c) -> p k c", k=KT) for i in range(2)]

        def w_pieces(k):
            if k >= KT // 2:
                return [(slice(0, P), w_out[k * P:(k + 1) * P, :])]
            return [(slice(h * HD, (h + 1) * HD), w_out[(k + 4 * h) * HD:(k + 4 * h + 1) * HD, :]) for h in range(2)]

        raw_arrived = [16 * sum(len(w_pieces(j)) for j in range(k % raws, k + 1, raws)) for k in range(KT)]

        def y_of(t):
            return core.banks(4 + 2 * (t % 2), 2)

        with nc.Block() as block:
            @block.sync
            def _(sp):
                for t in range(PT):
                    if t >= 2:
                        sp.wait_ge(turned, t - 1)
                    sp.dma_start(o[:, t % 2, :], o_rows[t * P:(t + 1) * P, :]).then_inc(o_in[t % 2], 16)
                    if t >= raws:
                        sp.wait_ge(w_lo_done, t - raws + 1)
                    for rows, src in w_pieces(t):
                        sp.dma_start(raw[rows, t % raws, :], src).then_inc(raw_in[t % raws], 16)
                sp.dma_start(pn.gain[:], gain.partition_broadcast(P)).then_inc(pn.gain_in, 16)
                for t in range(NT):
                    load_residual(sp, pn, x_src, t)
                    if t >= 1:
                        store_residual(sp, pn, x_dst, t - 1)
                store_residual(sp, pn, x_dst, NT - 1)
                wait_stored(sp, pn)

            @block.scalar
            def _(act):
                nc.scalar.activation(oT_hi[:, :, SEQ:TOK], core.sample_oT[:], ACT.Copy).then_inc(o_hi_done, 1)
                for t in range(PT):
                    act.wait_ge(raw_in[t % raws], raw_arrived[t])
                    nc.scalar.activation(w_hi[:, t, :], raw[:, t % raws, :], ACT.Copy).then_inc(w_hi_done, 1)
                    act.wait_ge(turned, t + 1)
                    nc.scalar.activation(oT_hi[:, :, t * P:(t + 1) * P], turned_ps[t % 2],
                                         ACT.Copy).then_inc(o_hi_done, 1)
                for t in range(NT):
                    act.wait_ge(y_ready, t + 1)
                    square_of_y(nc, act, pn, y_of(t), t)

            @block.gpsimd
            def _(pool):
                for t in range(NT):
                    rstd_of_y(core, pool, pn, t)

            @block.vector
            def _(dve):
                dve.wait_ge(o_hi_done, 1)
                nc.vector.tensor_tensor(oT_lo[:, :, SEQ:TOK], core.sample_oT[:], oT_hi[:, :, SEQ:TOK].bitcast(F32),
                                        ALU.subtract).then_inc(o_lo_done, 1)
                for t in range(PT):
                    dve.wait_ge(w_hi_done, t + 1)
                    nc.vector.tensor_tensor(w_lo[:, t, :], raw[:, t % raws, :], w_hi[:, t, :].bitcast(F32),
                                            ALU.subtract).then_inc(w_lo_done, 1)
                    dve.wait_ge(o_hi_done, t + 2)
                    c = slice(t * P, (t + 1) * P)
                    nc.vector.tensor_tensor(oT_lo[:, :, c], turned_ps[t % 2], oT_hi[:, :, c].bitcast(F32),
                                            ALU.subtract).then_inc(o_lo_done, 1)
                for t in range(NT):
                    add_normed(nc, dve, pn, y_of(t), t)

            @block.tensor
            def _(pe):
                for t in range(PT):
                    pe.wait_ge(o_in[t % 2], 16 * (t // 2 + 1))
                    if t >= 2:
                        pe.wait_ge(o_lo_done, t)
                    for k in range(KT):
                        last = nc.tensor.transpose(turned_ps[t % 2][:, k, :], o[:, t % 2, k * P:(k + 1) * P],
                                                   core.identity[:])
                    last.then_inc(turned, 1)
                pe.wait_ge(w_lo_done, KT)
                pe.wait_ge(o_lo_done, NT)
                for t in range(NT):
                    if t >= 2:
                        pe.wait_ge(pn.scaled, t - 1)
                    c = tile_start(t)
                    for k in range(KT):
                        for a, b in ((oT_hi, w_hi), (oT_hi, w_lo), (oT_lo, w_hi)):
                            for n in range(2):
                                last = nc.tensor.matmul(core.ps[:, 4 + 2 * (t % 2) + n, :], a[:, k, c:c + P],
                                                        b[:, k, n * 512:(n + 1) * 512],
                                                        start=(k == 0 and a is oT_hi and b is w_hi),
                                                        stop=(k == KT - 1 and a is oT_lo))
                    last.then_inc(y_ready, 1)


def mlp(core, tag, xT_hi, xT_lo, w1, w2, y):
    nc = core.nc
    w1_rows = w1.rearrange("(k p) n -> p k n", p=P)
    with ExitStack() as mem:
        h_hi = core.sb(tag + "h_hi", [P, FFB, TOK], F32R, mem)
        h_lo = core.sb(tag + "h_lo", [P, FFB, TOK], F32R, mem)
        w2_hi = core.sb(tag + "w2_hi", [P, FFB, D], F32R, mem)
        w2_lo = core.sb(tag + "w2_lo", [P, FFB, D], F32R, mem)
        relu = core.sb(tag + "relu", [P, 2, 384], F32, mem)
        square = core.sb(tag + "square", [P, 2, 384], F32, mem)
        w1_hi = core.sb(tag + "w1_hi", [P, 2, KT, P], F32R, mem)
        w1_lo = core.sb(tag + "w1_lo", [P, 2, KT, P], F32R, mem)
        raw = core.sb(tag + "raw", [P, 2, D], F32, mem)
        raw_in = [core.sem(f"{tag}raw_in{s}") for s in range(2)]
        hi_done = core.sem(tag + "hi_done")
        lo_done = core.sem(tag + "lo_done")
        up_ready = core.sem(tag + "up_ready")
        relu_done = core.sem(tag + "relu_done")
        square_hi = core.sem(tag + "square_hi")
        squared = core.sem(tag + "squared")
        h_ready = core.sem(tag + "h_ready")
        part_ready = core.sem(tag + "part_ready")
        part_added = core.sem(tag + "part_added")
        y_zero = core.sem(tag + "y_zero")
        PARTS = 2 * NT

        def tile_source(b, n, ahead=0):
            if n in (3, 4, 5, 6):
                return w2[bass.ds((b + ahead) * (FFB * P) + (n - 3) * P, P), :]
            i = 3 if n == 7 else n
            return w1_rows[:, :, bass.ds((b + ahead) * (FFB * P) + i * P, P)]

        def raw_view(n):
            r = raw[:, n % 2, :]
            return r if n in (3, 4, 5, 6) else r.rearrange("p (k c) -> p k c", k=KT)

        def split_into(n):
            if n in (3, 4, 5, 6):
                return w2_hi[:, n - 3, :], w2_lo[:, n - 3, :]
            i = 3 if n == 7 else n
            return w1_hi[:, i % 2], w1_lo[:, i % 2]

        with nc.Block() as block:
            @block.sync
            def _(sp):
                def load(b, n, ahead=0, first=False):
                    if not first:
                        sp.wait_ge(lo_done, b * 8 + (8 * ahead + n - 1))
                    sp.dma_start(raw_view(n), tile_source(b, n, ahead)).then_inc(raw_in[n % 2], 16)

                load(0, 0, first=True)
                load(0, 1, first=True)
                for b in range(NBLK):
                    for n in range(2, 8):
                        load(b, n)
                    if b < NBLK - 1:
                        load(b, 0, 1)
                        load(b, 1, 1)

            @block.scalar
            def _(act):
                def split(b, n, ahead=0, first=False):
                    m = 8 * ahead + n
                    act.wait_ge(raw_in[n % 2], b * 64 + 16 * (m // 2 + 1))
                    if n in (3, 4, 5, 6):
                        if not first:
                            act.wait_ge(part_ready, b * PARTS)
                    elif not first:
                        i = 4 * ahead + (3 if n == 7 else n)
                        act.wait_ge(up_ready, b * 4 + (i - 1))
                    nc.scalar.activation(split_into(n)[0], raw_view(n), ACT.Copy).then_inc(hi_done, 1)

                def hidden(b, i, first=False):
                    act.wait_ge(up_ready, b * 4 + (i + 1))
                    if i == 0 and not first:
                        act.wait_ge(part_ready, b * PARTS)
                    for j, (c, w) in enumerate(TOKEN_CHUNKS):
                        n = 3 * i + j
                        if not (first and n < 2):
                            act.wait_ge(squared, b * 12 + (n - 1))
                        nc.scalar.activation(relu[:, n % 2, 0:w], core.ps[:, 3 * (i % 2) + j, 0:w],
                                             ACT.Relu).then_inc(relu_done, 1)
                        act.wait_ge(relu_done, b * 12 + (n + 1))
                        nc.scalar.activation(h_hi[:, i, c:c + w], relu[:, n % 2, 0:w], ACT.Square).then_inc(square_hi, 1)

                def steps(b, last=False, first=False):
                    hidden(b, 0, first)
                    split(b, 2)
                    for n in (3, 4, 5, 6):
                        split(b, n, first=first)
                    split(b, 7)
                    hidden(b, 1)
                    if not last:
                        split(b, 0, 1)
                    hidden(b, 2)
                    if not last:
                        split(b, 1, 1)
                    hidden(b, 3)

                split(0, 0, first=True)
                split(0, 1, first=True)
                steps(0, first=True)
                with act.Fori(1, NBLK - 1) as b:
                    steps(b)
                steps(NBLK - 1, last=True)

            @block.vector
            def _(dve):
                def split(b, n, ahead=0):
                    dve.wait_ge(hi_done, b * 8 + (8 * ahead + n + 1))
                    hi, lo = split_into(n)
                    nc.vector.tensor_tensor(lo, raw_view(n), hi.bitcast(F32), ALU.subtract).then_inc(lo_done, 1)

                def hidden(b, i):
                    for j, (c, w) in enumerate(TOKEN_CHUNKS):
                        n = 3 * i + j
                        dve.wait_ge(relu_done, b * 12 + (n + 1))
                        nc.vector.tensor_tensor(square[:, n % 2, 0:w], relu[:, n % 2, 0:w], relu[:, n % 2, 0:w],
                                                ALU.mult).then_inc(squared, 1)
                        dve.wait_ge(squared, b * 12 + (n + 1))
                        dve.wait_ge(square_hi, b * 12 + (n + 1))
                        nc.vector.tensor_tensor(h_lo[:, i, c:c + w], square[:, n % 2, 0:w],
                                                h_hi[:, i, c:c + w].bitcast(F32), ALU.subtract).then_inc(h_ready, 1)

                def steps(b, last=False):
                    hidden(b, 0)
                    for n in range(2, 8):
                        split(b, n)
                    hidden(b, 1)
                    if not last:
                        split(b, 0, 1)
                    hidden(b, 2)
                    if not last:
                        split(b, 1, 1)
                    hidden(b, 3)
                    for n in range(PARTS):
                        dve.wait_ge(part_ready, b * PARTS + (n + 1))
                        part = y[:, n // 2, (n % 2) * 512:(n % 2 + 1) * 512]
                        nc.vector.tensor_tensor(part, part, core.ps[:, 6 + n % 2, :], ALU.add).then_inc(part_added, 1)

                nc.vector.memset(y[:], 0.0).then_inc(y_zero, 1)
                split(0, 0)
                split(0, 1)
                dve.wait_ge(y_zero, 1)
                with dve.Fori(0, NBLK - 1) as b:
                    steps(b)
                steps(NBLK - 1, last=True)

            @block.tensor
            def _(pe):
                def up(b, i, ahead=0, first=False):
                    pe.wait_ge(lo_done, b * 8 + (8 * ahead + (8 if i == 3 else i + 1)))
                    if not first:
                        pe.wait_ge(relu_done, b * 12 + (3 * (4 * ahead + i) - 3))
                    for k in range(KT):
                        for a, x in ((w1_hi, xT_hi), (w1_hi, xT_lo), (w1_lo, xT_hi)):
                            for j, (c, w) in enumerate(TOKEN_CHUNKS):
                                mm = nc.tensor.matmul(core.ps[:, 3 * (i % 2) + j, 0:w], a[:, i % 2, k, :],
                                                      x[:, k, c:c + w],
                                                      start=(k == 0 and a is w1_hi and x is xT_hi),
                                                      stop=(k == KT - 1 and a is w1_lo))
                    mm.then_inc(up_ready, 1)

                def down(b, first=False):
                    pe.wait_ge(lo_done, b * 8 + 7)
                    pe.wait_ge(h_ready, b * 12 + 12)
                    for n in range(PARTS):
                        t, half = n // 2, n % 2
                        if not (first and n < 2):
                            pe.wait_ge(part_added, b * PARTS + (n - 1))
                        s = tile_start(t)
                        for k in range(FFB):
                            for a, w in ((h_hi, w2_hi), (h_hi, w2_lo), (h_lo, w2_hi)):
                                mm = nc.tensor.matmul(core.ps[:, 6 + half, :], a[:, k, s:s + P],
                                                      w[:, k, half * 512:(half + 1) * 512],
                                                      start=(k == 0 and a is h_hi and w is w2_hi),
                                                      stop=(k == FFB - 1 and a is h_lo))
                        mm.then_inc(part_ready, 1)

                up(0, 0, first=True)
                up(0, 1, first=True)
                for i in (2, 3):
                    up(0, i)
                up(0, 0, 1)
                down(0, first=True)
                with pe.Fori(1, NBLK - 1) as b:
                    for i in (1, 2, 3):
                        up(b, i)
                    up(b, 0, 1)
                    down(b)
                for i in (1, 2, 3):
                    up(NBLK - 1, i)
                down(NBLK - 1)


def finish_mlp(core, tag, y, x_src, x_dst, gain):
    nc = core.nc
    with ExitStack() as mem:
        pn = PostNorm(core, tag, mem)
        with nc.Block() as block:
            @block.sync
            def _(sp):
                sp.dma_start(pn.gain[:], gain.partition_broadcast(P)).then_inc(pn.gain_in, 16)
                for t in range(NT):
                    load_residual(sp, pn, x_src, t)
                    if t >= 1:
                        store_residual(sp, pn, x_dst, t - 1)
                store_residual(sp, pn, x_dst, NT - 1)
                wait_stored(sp, pn)

            @block.scalar
            def _(act):
                for t in range(NT):
                    square_of_y(nc, act, pn, y[:, t, :], t)

            @block.gpsimd
            def _(pool):
                for t in range(NT):
                    rstd_of_y(core, pool, pn, t)

            @block.vector
            def _(dve):
                for t in range(NT):
                    add_normed(nc, dve, pn, y[:, t, :], t)


def pool_mix(core, x_src, x_dst, state, pool_w, pool_scale, pre_gain, post_gain, tables, prompt_pool, sample_pool):
    nc = core.nc
    xs = 3
    with ExitStack() as mem:
        x = core.sb("pm_x", [P, xs, D], F32, mem)
        gain_b = core.sb("pm_gain", [P, D], F32, mem)
        junk = core.sb("pm_junk", [P, D], F32, mem)
        ms = core.sb("pm_ms", [P, NT], F32, mem)
        rstd = core.sb("pm_rstd", [P, NT], F32, mem)
        h = core.sb("pm_h", [P, NT, D], F32, mem)
        before = core.sb("pm_before", [NB * CTX, D], F32, mem)
        band = core.sb("pm_band", [P, 4, 3, P], F32, mem)
        own = core.sb("pm_own", [P, 4, NS], F32, mem)
        ctx = core.sb("pm_ctx", [NB * CTX, 4, NS], F32, mem)
        w = core.sb("pm_w", [P, KT, 256], F32, mem)
        scale_b = core.sb("pm_scale", [P, D], F32, mem)
        yT = core.sb("pm_yT", [P, KT, TOK], F32, mem)
        z = core.sb("pm_z", [P, 2, D], F32, mem)
        pn = PostNorm(core, "pm_", mem)
        x_in = [core.sem(f"pm_x_in{s}") for s in range(xs)]
        gain_in = core.sem("pm_gain_in")
        tables_in = core.sem("pm_tables_in")
        weights_in = core.sem("pm_weights_in")
        squared = core.sem("pm_squared")
        ms_shifted = core.sem("pm_ms_shifted")
        rstd_ready = core.sem("pm_rstd_ready")
        normed = core.sem("pm_normed")
        pool_stored = core.sem("pm_pool_stored")
        pooled = core.sem("pm_pooled")
        yT_ready = core.sem("pm_yT_ready")
        z_ready = core.sem("pm_z_ready")
        z_scaled = core.sem("pm_z_scaled")

        def pooled_ps(t):
            return core.banks(2 * (t % 2), 2).rearrange("p (k c) -> p k c", k=KT)

        with nc.Block() as block:
            @block.sync
            def _(sp):
                sp.dma_start(gain_b[:], pre_gain.partition_broadcast(P)).then_inc(gain_in, 16)
                for t in range(NT):
                    if t >= xs:
                        sp.wait_ge(normed, t - xs + 1)
                    for rows, src in token_rows(*x_src, t):
                        sp.dma_start(x[rows, t % xs, :], src).then_inc(x_in[t % xs], 16)
                    if t == 1:
                        sp.dma_start(band[:], tables["pool_band"].rearrange("p (g a c) -> p g a c", g=4, a=3)
                                     ).then_inc(tables_in, 16)
                        sp.dma_start(own[:], tables["pool_own"].rearrange("p (g c) -> p g c", g=4)).then_inc(tables_in, 16)
                        sp.dma_start(ctx[:], tables["pool_ctx"].rearrange("p (g c) -> p g c", g=4)).then_inc(tables_in, 16)
                        sp.dma_start(before[:], state).then_inc(tables_in, 16)
                        sp.dma_start(w[:], pool_w.rearrange("(k p) n -> p k n", p=P)).then_inc(weights_in, 16)
                        sp.dma_start(scale_b[:], pool_scale.partition_broadcast(P)).then_inc(weights_in, 16)
                        sp.dma_start(pn.gain[:], post_gain.partition_broadcast(P)).then_inc(pn.gain_in, 16)
                    if t >= 5:
                        store_residual(sp, pn, x_dst, t - 5)
                    if t >= 3:
                        load_residual(sp, pn, x_src, t - 3)
                for t in range(NT - 3, NT):
                    store_residual(sp, pn, x_dst, t - 2)
                    load_residual(sp, pn, x_src, t)
                for t in range(NT - 2, NT):
                    store_residual(sp, pn, x_dst, t)
                wait_stored(sp, pn)

            @block.gpsimd
            def _(pool):
                for b in range(NB):
                    pool.dma_start(sample_pool[b, 0:CTX - NQ, :],
                                   state[b * CTX + NQ:(b + 1) * CTX, :]).then_inc(pool_stored, 16)
                for t in range(NT):
                    pool.wait_ge(squared, t + 1)
                    root(core, pool, ms, rstd, ms_shifted, rstd_ready, t)
                    if t >= 3:
                        rstd_of_y(core, pool, pn, t - 3)
                pool.wait_ge(normed, NT)
                pool.dma_start(prompt_pool, h[P - CTX:P, PT - 1, :]).then_inc(pool_stored, 16)
                for b in range(NB):
                    r = P - NS + b * NQ
                    pool.dma_start(sample_pool[b, CTX - NQ:CTX, :], h[r:r + NQ, PT, :]).then_inc(pool_stored, 16)
                for t in range(NT - 3, NT):
                    rstd_of_y(core, pool, pn, t)
                pool.wait_ge(pool_stored, 16 * (2 * NB + 1))

            @block.scalar
            def _(act):
                def take_pooled(t):
                    act.wait_ge(pooled, t + 1)
                    c, n = (t * P, P) if t < PT else (SEQ, NS)
                    nc.scalar.activation(yT[:, :, c:c + n], pooled_ps(t)[:, :, 0:n], ACT.Copy).then_inc(yT_ready, 1)

                def square_z(t):
                    act.wait_ge(z_scaled, t + 1)
                    square_of_y(nc, act, pn, z[:, t % 2, :], t)

                for t in range(NT):
                    act.wait_ge(x_in[t % xs], 16 * (t // xs + 1 + (t == PT)))
                    if t >= 1:
                        act.wait_ge(squared, t)
                    nc.scalar.activation(junk[:], x[:, t % xs, :], ACT.Square, scale=1.0 / 32,
                                         accum_out=ms[:, t:t + 1]).then_inc(squared, 1)
                    if t >= 1:
                        take_pooled(t - 1)
                    if t >= 3:
                        square_z(t - 3)
                take_pooled(NT - 1)
                for t in range(NT - 3, NT):
                    square_z(t)

            @block.vector
            def _(dve):
                def scale_z(t):
                    dve.wait_ge(z_ready, t + 1)
                    if t == 0:
                        dve.wait_ge(weights_in, 32)
                    if t >= 2:
                        dve.wait_ge(pn.scaled, t - 1)
                        dve.wait_ge(pn.squared, t - 1)
                    nc.vector.tensor_tensor(z[:, t % 2, :], core.banks(4 + 2 * (t % 2), 2), scale_b[:],
                                            ALU.mult).then_inc(z_scaled, 1)

                for t in range(NT):
                    dve.wait_ge(rstd_ready, t + 1)
                    if t == 0:
                        dve.wait_ge(gain_in, 16)
                    nc.vector.scalar_tensor_tensor(h[:, t, :], x[:, t % xs, :], rstd[:, t:t + 1], gain_b[:],
                                                   ALU.mult, ALU.mult).then_inc(normed, 1)
                    if t >= 2:
                        scale_z(t - 2)
                    if t >= 3:
                        add_normed(nc, dve, pn, z[:, (t - 3) % 2, :], t - 3)
                for t in range(NT - 2, NT):
                    scale_z(t)
                    add_normed(nc, dve, pn, z[:, (t - 1) % 2, :], t - 1)
                add_normed(nc, dve, pn, z[:, (NT - 1) % 2, :], NT - 1)

            @block.tensor
            def _(pe):
                def mix(t):
                    pe.wait_ge(yT_ready, t + 1)
                    if t == 0:
                        pe.wait_ge(weights_in, 32)
                    if t >= 2:
                        pe.wait_ge(z_scaled, t - 1)
                    c = tile_start(t)
                    for g in range(4):
                        for k in range(2):
                            last = nc.tensor.matmul(core.banks(4 + 2 * (t % 2), 2)[:, g * 256:(g + 1) * 256],
                                                    yT[:, 2 * g + k, c:c + P], w[:, 2 * g + k, :],
                                                    start=(k == 0), stop=(k == 1))
                    last.then_inc(z_ready, 1)

                pe.wait_ge(tables_in, 64)
                for t in range(NT):
                    pe.wait_ge(normed, t + 1)
                    if t >= 2:
                        pe.wait_ge(yT_ready, t - 1)
                    for f in range(KT):
                        fc, g = slice(f * P, (f + 1) * P), f // 2
                        if t == 0:
                            parts = [(h[:, 0, fc], band[:, g, 0, :])]
                        elif t < PT:
                            parts = [(h[:, t, fc], band[:, g, 1, :]), (h[:, t - 1, fc], band[:, g, 2, :])]
                        else:
                            parts = [(h[:, t, fc], own[:, g, :]), (before[:, fc], ctx[:, g, :])]
                        n = P if t < PT else NS
                        for j, (lhs, rhs) in enumerate(parts):
                            last = nc.tensor.matmul(pooled_ps(t)[:, f, 0:n], lhs, rhs, start=(j == 0),
                                                    stop=(j == len(parts) - 1))
                    last.then_inc(pooled, 1)
                    if t >= 1:
                        mix(t - 1)
                mix(NT - 1)


def build(nc, ins, tables, outs, scratch):
    xp, xs = ins["x_prompt"], ins["x_sample"]
    gains = ins["norm_g"]
    x1, x2, x3, o_rows = (scratch[n] for n in ("x1", "x2", "x3", "o_rows"))
    halves = lambda x: (x[0:SEQ, :], x[SEQ:TOK, :])
    with ExitStack() as ctx:
        core = Core(nc, ctx)
        start(core, tables)
        core.end_stage()
        with ExitStack() as mem:
            qT = core.sb("qT", [P, KT, TOK], F32, mem)
            kaT = core.sb("kaT", [P, TOK], F32, mem)
            kbT = core.sb("kbT", [P, NH // 2, TOK], F32, mem)
            v = core.sb("v", [P, NT, P + NH * HD], F32, mem)
            with ExitStack() as inner:
                xT_hi = core.sb("a_xT_hi", [P, KT, TOK], F32R, inner)
                xT_lo = core.sb("a_xT_lo", [P, KT, TOK], F32R, inner)
                prepare(core, "a_", xp, xs, gains[0], xT_hi, xT_lo)
                core.end_stage()
                in_project(core, ins["attn_w_in"], xT_hi, xT_lo, qT, kaT, kbT, v, outs)
                core.end_stage()
            prompt_attention(core, qT, kaT, kbT, v, tables["prompt_bias"], ins["attn_sinks"], o_rows)
            core.end_stage()
            sample_attention(core, qT, kaT, kbT, v, {n: ins["cache_" + n] for n in ("a_k", "a_v", "b_k", "b_v")},
                             ins["attn_sinks"], tables["sample_bias_b"], tables["sample_bias_a"])
            core.end_stage()
        out_project(core, o_rows, ins["attn_w_out"], (xp, xs), halves(x1), gains[1])
        core.end_stage()
        for layer, src, dst in ((0, halves(x1), halves(x2)), (1, halves(x3), (outs["y_prompt"], outs["y_sample"]))):
            if layer == 1:
                pool_mix(core, halves(x2), src, ins["state_pool"], ins["pool_w"], ins["pool_scale"], gains[4], gains[5],
                         tables, outs["prompt_pool"], outs["sample_pool"])
                core.end_stage()
            tag = f"m{layer}_"
            with ExitStack() as mem:
                y = core.sb(tag + "y", [P, NT, D], F32, mem)
                with ExitStack() as inner:
                    xT_hi = core.sb(tag + "xT_hi", [P, KT, TOK], F32R, inner)
                    xT_lo = core.sb(tag + "xT_lo", [P, KT, TOK], F32R, inner)
                    prepare(core, tag + "pre_", *src, gains[4 * layer + 2], xT_hi, xT_lo)
                    core.end_stage()
                    mlp(core, tag, xT_hi, xT_lo, ins["mlp_w1"][layer], ins["mlp_w2"][layer], y)
                    core.end_stage()
                finish_mlp(core, tag, y, src, dst, gains[4 * layer + 3])
                core.end_stage()


def kernel(**inputs):
    import concourse.bacc as bacc
    from concourse.bass_utils import run_bass_kernel_spmd

    nc = bacc.Bacc("TRN2", target_bir_lowering=False, num_devices=1)
    shapes = {
        "x_prompt": (SEQ, D), "x_sample": (NS, D),
        "cache_a_k": (NB, P, P), "cache_a_v": (NB, P, P),
        "cache_b_k": (NB, PAST, NH * HD), "cache_b_v": (NB, PAST, NH * HD),
        "state_pool": (NB * CTX, D), "norm_g": (8, D), "attn_w_in": (D, 2304), "attn_w_out": (D, D),
        "attn_sinks": (NH,), "pool_w": (D, 256), "pool_scale": (D,),
        "mlp_w1": (2, D, DFF), "mlp_w2": (2, DFF, D),
    }
    arrays, ins, tables, outs, scratch = {}, {}, {}, {}, {}
    for name, shape in shapes.items():
        arrays[name] = np.ascontiguousarray(np.asarray(inputs[name]).reshape(shape))
        ins[name] = nc.dram_tensor(name, shape, F32, kind="ExternalInput").ap()
    for name, table in shape_constants().items():
        arrays["table_" + name] = table
        tables[name] = nc.dram_tensor("table_" + name, table.shape, F32, kind="ExternalInput").ap()
    results = {
        "y_prompt": ((SEQ, D), (1, SEQ, D)), "y_sample": ((NS, D), (NB, NQ, D)),
        "prompt_a_k": ((P, P), (1, 1, P, 2, HD)), "prompt_a_v": ((P, P), (1, 1, P, 2, HD)),
        "prompt_b_k": ((SEQ, 512), (1, 1, SEQ, NH, HD)), "prompt_b_v": ((SEQ, 512), (1, 1, SEQ, NH, HD)),
        "prompt_pool": ((CTX, D), (1, 1, CTX, D)),
        "sample_a_k": ((NS, P), (1, NB, NQ, 2, HD)), "sample_a_v": ((NS, P), (1, NB, NQ, 2, HD)),
        "sample_b_k": ((NS, 512), (1, NB, NQ, NH, HD)), "sample_b_v": ((NS, 512), (1, NB, NQ, NH, HD)),
        "sample_pool": ((NB, CTX, D), (1, NB, CTX, D)),
    }
    for name, (shape, _) in results.items():
        outs[name] = nc.dram_tensor("out_" + name, shape, F32, kind="ExternalOutput").ap()
    for name, rows in (("x1", TOK), ("x2", TOK), ("x3", TOK), ("o_rows", SEQ)):
        scratch[name] = nc.dram_tensor("scratch_" + name, (rows, D), F32, kind="Internal").ap()
    build(nc, ins, tables, outs, scratch)
    r = run_bass_kernel_spmd(nc, [arrays], core_ids=[0])
    return tuple(r.results[0]["out_" + name].reshape(shape) for name, (_, shape) in results.items())
```

```python
from contextlib import ExitStack

import numpy as np

import concourse.bass as bass
from concourse import mybir

F32 = mybir.dt.float32
F32R = mybir.dt.float32r
ALU = mybir.AluOpType
ACT = mybir.ActivationFunctionType
AX = mybir.AxisListType

P = 128
D = 1024
KT = D // P
SEQ = 1024
NB = 8
NQ = 8
NS = NB * NQ
TOK = SEQ + NS
PT = SEQ // P
NT = PT + 1
TOKEN_CHUNKS = ((0, 384), (384, 384), (768, 320))
HD = 64
NH = 8
WINDOW_A = 128
PAST = 2048
DFF = 4 * D
FFB = 4
NBLK = DFF // (FFB * P)
CTX = 15
POOL_W = (2, 4, 8, 16)
EPS = 1e-6
NEG = -1e30
BRANCHES = ((128, 1), (512, 4), (2048, 16))
FAR = PAST - 512
FAR_TILES = FAR // 2 // P
NEAR_TILES = 512 // P
CT = FAR_TILES + NEAR_TILES


def tile_start(t):
    return t * P if t < PT else TOK - P


def new_columns(t):
    return (slice(t * P, (t + 1) * P), slice(0, P)) if t < PT else (slice(SEQ, TOK), slice(P - NS, P))


def slope(n):
    return 2.0 ** (-8.0 * (n + 1) / 16)


def branch_bias(dist, n):
    count = sum(((dist >= 0) & (dist <= w) & (dist % d == 0)).astype(np.float64) for w, d in BRANCHES)
    return np.where(count > 0, np.log(np.maximum(count, 1)) - slope(n) * dist, NEG)


def window_bias(dist, n):
    return np.where((dist >= 0) & (dist <= WINDOW_A), -slope(n) * dist, NEG)


def shape_constants():
    q = np.arange(P)[:, None]
    prompt_a = np.stack([window_bias(P + q - np.arange(2 * P), h) for h in range(NH)], 1)
    prompt_b = np.stack([branch_bias(SEQ - P + q - np.arange(SEQ), NH + h) for h in range(NH)], 1)
    prompt = np.concatenate([np.maximum(x * 8, NEG).reshape(P, -1) for x in (prompt_a, prompt_b)], 1)

    rows = np.empty((CT, P), np.int64)
    p = np.arange(P)
    for t in range(FAR_TILES):
        rows[t] = 16 * (16 * t + p // 8) + p % 8
    for t in range(NEAR_TILES):
        rows[FAR_TILES + t] = FAR + t * P + p
    sample_b = np.zeros((P, CT * P + NQ))
    sample_a = np.zeros((NH * NQ, P + NQ))
    new = np.arange(NQ)
    for h in range(NH):
        for i in range(NQ):
            sample_b[32 * (h // 2) + NQ * (h % 2) + i] = np.concatenate(
                [branch_bias(PAST + i - rows.ravel(), NH + h), branch_bias(i - new, NH + h)])
            sample_a[NQ * h + i] = np.concatenate([window_bias(P + i - p, h), window_bias(i - new, h)])
    pool = np.zeros((P, 4, 3, P), np.float32)
    pool_own = np.zeros((P, 4, NS), np.float32)
    pool_ctx = np.zeros((NB * CTX, 4, NS), np.float32)
    for g, w in enumerate(POOL_W):
        for j in range(P):
            for k in range(max(0, j - w + 1), j + 1):
                pool[k, g, 0, j] += 1.0 / min(w, j + 1)
            for k in range(j - w + 1, j + 1):
                if k >= 0:
                    pool[k, g, 1, j] += 1.0 / w
                else:
                    pool[P + k, g, 2, j] += 1.0 / w
            pool[j, g, 0, j] -= 1
            pool[j, g, 1, j] -= 1
        for b in range(NB):
            for i in range(NQ):
                for k in range(i - w + 1, i + 1):
                    if k >= 0:
                        pool_own[P - NS + b * NQ + k, g, b * NQ + i] += 1.0 / w
                    else:
                        pool_ctx[b * CTX + CTX + k, g, b * NQ + i] += 1.0 / w
                pool_own[P - NS + b * NQ + i, g, b * NQ + i] -= 1
    return {
        "identity": np.eye(P, dtype=np.float32),
        "prompt_bias": prompt.astype(np.float32),
        "sample_bias_b": np.maximum(sample_b * 8, NEG).astype(np.float32),
        "sample_bias_a": np.maximum(sample_a * 8, NEG).astype(np.float32),
        "pool_band": pool.reshape(P, -1),
        "pool_own": pool_own.reshape(P, -1),
        "pool_ctx": pool_ctx.reshape(NB * CTX, -1),
    }


class Core:

    def __init__(self, nc, ctx):
        self.nc, self.ctx = nc, ctx
        self.stage_sems = []
        self.ps = ctx.enter_context(nc.psum_tensor("ps", [P, 8, 512], F32))
        self.identity = self.sb("identity", [P, P])
        self.minus_half = self.sb("minus_half", [P, 1])
        self.stats = self.sb("stats", [P, 4, NT])
        self.next_stat = 0

    def sb(self, name, shape, dt=F32, ctx=None, side=None):
        return (ctx or self.ctx).enter_context(self.nc.sbuf_tensor(name, shape, dt, side=side))

    def sem(self, name):
        self.stage_sems.append(self.nc.alloc_semaphore(name=name))
        return self.stage_sems[-1]

    def end_stage(self):
        self.nc.clear_and_free_semaphores(self.stage_sems)
        self.stage_sems = []
        self.next_stat = 0
        self.nc.all_engine_barrier()

    def stat(self):
        self.next_stat += 1
        return self.stats[:, self.next_stat - 1, :]

    def banks(self, first, n, width=512):
        return self.ps[:, first:first + n, :].rearrange("p a b -> p (a b)")[:, 0:n * 512 if width == 512 else width]

    def feature_banks(self, first):
        return self.banks(first, 2).rearrange("p (k c) -> p k c", k=KT)


def token_rows(prompt, sample, t):
    if t < PT:
        return [(slice(0, P), prompt[t * P:(t + 1) * P, :])]
    return [(slice(0, P - NS), prompt[SEQ - (P - NS):SEQ, :]), (slice(P - NS, P), sample[0:NS, :])]


def stored_rows(prompt, sample, t):
    return token_rows(prompt, sample, t) if t < PT else token_rows(prompt, sample, t)[1:]


def start(core, constants):
    nc = core.nc
    const_in = core.sem("const_in")
    with nc.Block() as block:
        @block.sync
        def _(sp):
            sp.dma_start(core.identity[:], constants["identity"]).then_inc(const_in, 16)
            sp.wait_ge(const_in, 16)

        @block.vector
        def _(dve):
            nc.vector.memset(core.minus_half[:], -0.5)


def root(core, pool, ms, rstd, shifted, ready, t):
    nc = core.nc
    col = slice(t, t + 1)
    nc.gpsimd.tensor_scalar(ms[:, col], ms[:, col], EPS, None, ALU.add).then_inc(shifted, 1)
    pool.wait_ge(shifted, t + 1)
    nc.gpsimd.tensor_tensor(rstd[:, col], ms[:, col], core.minus_half[:], ALU.pow).then_inc(ready, 1)


class PostNorm:

    def __init__(self, core, tag, slots, gain, junk):
        self.slots, self.gain, self.junk = slots, gain, junk
        self.ms, self.rstd = core.stat(), core.stat()
        self.gain_in = core.sem(tag + "post_gain_in")
        self.x_in = [core.sem(f"{tag}res_in{s}") for s in range(len(slots))]
        self.squared = core.sem(tag + "post_squared")
        self.ms_shifted = core.sem(tag + "post_ms_shifted")
        self.rstd_ready = core.sem(tag + "post_rstd_ready")
        self.scaled = core.sem(tag + "post_scaled")
        self.added = core.sem(tag + "post_added")
        self.stored = [core.sem(f"{tag}post_stored{s}") for s in range(len(slots))]

    def x(self, t):
        return self.slots[t % len(self.slots)]

    def load(self, sp, src, t, pre=None):
        n = len(self.slots)
        if t >= n:
            sp.wait_ge(self.stored[t % n], 16 * (t // n))
            if pre:
                sp.wait_ge(pre.normed, t - n + 1)
        for rows, piece in token_rows(*src, t):
            sp.dma_start(self.x(t)[rows, :], piece).then_inc(self.x_in[t % n], 16)

    def store(self, sp, dst, t):
        sp.wait_ge(self.added, t + 1)
        for rows, piece in stored_rows(*dst, t):
            sp.dma_start(piece, self.x(t)[rows, :]).then_inc(self.stored[t % len(self.slots)], 16)

    def wait_stored(self, sp):
        n = len(self.slots)
        for s in range(n):
            sp.wait_ge(self.stored[s], 16 * len(range(s, NT, n)))

    def square(self, nc, act, y, t):
        if t >= 1:
            act.wait_ge(self.squared, t)
        nc.scalar.activation(self.junk, y, ACT.Square, scale=1.0 / 32,
                             accum_out=self.ms[:, t:t + 1]).then_inc(self.squared, 1)

    def root(self, core, pool, t):
        pool.wait_ge(self.squared, t + 1)
        root(core, pool, self.ms, self.rstd, self.ms_shifted, self.rstd_ready, t)

    def scale(self, nc, dve, y, out, t):
        if t == 0:
            dve.wait_ge(self.gain_in, 16)
        dve.wait_ge(self.rstd_ready, t + 1)
        nc.vector.scalar_tensor_tensor(out, y, self.rstd[:, t:t + 1], self.gain, ALU.mult, ALU.mult).then_inc(self.scaled, 1)

    def add(self, nc, dve, yn, t):
        n = len(self.slots)
        dve.wait_ge(self.scaled, t + 1)
        dve.wait_ge(self.x_in[t % n], 16 * (t // n + 1 + (t == PT)))
        nc.vector.tensor_tensor(self.x(t), self.x(t), yn, ALU.add).then_inc(self.added, 1)


class PreNorm:

    def __init__(self, core, tag, gain, junk):
        self.gain, self.junk = gain, junk
        self.ms, self.rstd = core.stat(), core.stat()
        self.gain_in = core.sem(tag + "gain_in")
        self.squared = core.sem(tag + "squared")
        self.ms_shifted = core.sem(tag + "ms_shifted")
        self.rstd_ready = core.sem(tag + "rstd_ready")
        self.normed = core.sem(tag + "normed")

    def square(self, nc, act, x, t):
        if t >= 1:
            act.wait_ge(self.squared, t)
        nc.scalar.activation(self.junk, x, ACT.Square, scale=1.0 / 32,
                             accum_out=self.ms[:, t:t + 1]).then_inc(self.squared, 1)

    def root(self, core, pool, t):
        pool.wait_ge(self.squared, t + 1)
        root(core, pool, self.ms, self.rstd, self.ms_shifted, self.rstd_ready, t)

    def scale(self, nc, dve, x, out, t):
        if t == 0:
            dve.wait_ge(self.gain_in, 16)
        dve.wait_ge(self.rstd_ready, t + 1)
        nc.vector.scalar_tensor_tensor(out, x, self.rstd[:, t:t + 1], self.gain, ALU.mult, ALU.mult).then_inc(self.normed, 1)


class Turned:

    def __init__(self, core, tag, xn, ps, xT_hi, xT_lo):
        self.xn, self.ps, self.xT_hi, self.xT_lo = xn, ps, xT_hi, xT_lo
        self.turned = core.sem(tag + "turned")
        self.hi_done = core.sem(tag + "hi_done")
        self.lo_done = core.sem(tag + "lo_done")

    def wait_slot(self, dve, t):
        if t >= 2:
            dve.wait_ge(self.turned, t - 1)

    def turn(self, core, pe, pre, t):
        pe.wait_ge(pre.normed, t + 1)
        n = len(self.ps)
        if t >= n:
            pe.wait_ge(self.lo_done, t - n + 1)
        for k in range(KT):
            last = core.nc.tensor.transpose(self.ps[t % n][:, k, :], self.xn[:, t % 2, k * P:(k + 1) * P],
                                            core.identity[:])
        last.then_inc(self.turned, 1)

    def take_hi(self, nc, act, t):
        act.wait_ge(self.turned, t + 1)
        c, new = new_columns(t)
        nc.scalar.activation(self.xT_hi[:, :, c], self.ps[t % len(self.ps)][:, :, new], ACT.Copy).then_inc(self.hi_done, 1)

    def take_lo(self, nc, dve, t):
        dve.wait_ge(self.hi_done, t + 1)
        c, new = new_columns(t)
        nc.vector.tensor_tensor(self.xT_lo[:, :, c], self.ps[t % len(self.ps)][:, :, new],
                                self.xT_hi[:, :, c].bitcast(F32), ALU.subtract).then_inc(self.lo_done, 1)




def in_project(core, x_src, gain, w_in, xT_hi, xT_lo, qT, kaT, kbT, v, outs):
    nc = core.nc
    W = 256
    chunks = [4, 5, 6, 7, 8, 0, 1, 2, 3]
    NKV, NK = 5, 3
    w_rows = w_in.rearrange("(k p) n -> p k n", p=P)
    with ExitStack() as mem:
        raw = core.sb("in_raw", [P, 2, KT, W], F32, mem)
        w_hi = core.sb("in_w_hi", [P, 2, KT, W], F32R, mem)
        w_lo = core.sb("in_w_lo", [P, 2, KT, W], F32R, mem)
        ks = 3
        k_rows = core.sb("k_rows", [P, ks, W], F32, mem)
        xs = 3
        x = qT[:, 0:xs, 0:D]
        xn = qT[:, xs:xs + 2, 0:D]
        x_in = [core.sem(f"in_x_in{s}") for s in range(xs)]
        pre = PreNorm(core, "in_pre_", qT[:, xs + 2, 0:D], qT[:, xs + 3, 0:D])
        tn = Turned(core, "in_x_", xn, [core.feature_banks(2 + 2 * i) for i in range(2)], xT_hi, xT_lo)
        raw_in = [core.sem(f"in_raw_in{s}") for s in range(2)]
        hi_done = core.sem("in_hi_done")
        lo_done = core.sem("in_lo_done")
        kv_ready = core.sem("in_kv_ready")
        kv_taken = core.sem("in_kv_taken")
        k_stored = [core.sem(f"in_k_stored{s}") for s in range(ks)]
        k_turned = core.sem("in_k_turned")
        kT_taken = core.sem("in_kT_taken")
        q_ready = core.sem("in_q_ready")
        q_taken = core.sem("in_q_taken")
        v_stored = core.sem("in_v_stored")

        def k_store(n, t):
            rows = slice(0, P) if t < PT else slice(P - NS, P)
            if n == 0:
                if t < PT - 1:
                    return None
                return (outs["prompt_a_k"] if t < PT else outs["sample_a_k"])[:, :], rows, slice(0, P)
            c = (n - 1) * W
            dst = outs["prompt_b_k"][t * P:(t + 1) * P, c:c + W] if t < PT else outs["sample_b_k"][:, c:c + W]
            return dst, rows, slice(0, W)

        stored_before = {}
        count = [0] * ks
        for i in range(NK * NT):
            stored_before[i] = count[i % ks]
            count[i % ks] += k_store(i // NT, i % NT) is not None

        arrived = [16 * sum(4 if chunks[j] < 2 else 1 for j in range(n % 2, n + 1, 2)) for n in range(len(chunks))]

        with nc.Block() as block:
            @block.sync
            def _(sp):
                def load_x(t):
                    if t >= xs:
                        sp.wait_ge(pre.normed, t - xs + 1)
                    for rows, src in token_rows(*x_src, t):
                        sp.dma_start(x[rows, t % xs, :], src).then_inc(x_in[t % xs], 16)

                load_x(0)
                sp.dma_start(pre.gain, gain.partition_broadcast(P)).then_inc(pre.gain_in, 16)
                for n, c in enumerate(chunks):
                    if n == 1:
                        load_x(1)
                        load_x(2)
                    if n == 2:
                        for t in range(xs, NT):
                            load_x(t)
                    if n >= 2:
                        sp.wait_ge(lo_done, n - 1)
                    if c >= 2:
                        sp.dma_start(raw[:, n % 2], w_rows[:, :, c * W:(c + 1) * W]).then_inc(raw_in[n % 2], 16)
                        continue
                    for j in range(2):
                        for half in range(2):
                            src = half * W + (2 * c + j) * HD
                            dst = (2 * j + half) * HD
                            sp.dma_start(raw[:, n % 2, :, dst:dst + HD],
                                         w_rows[:, :, src:src + HD]).then_inc(raw_in[n % 2], 16)

            @block.gpsimd
            def _(pool):
                pre.root(core, pool, 0)
                pre.root(core, pool, 1)
                for i in range(NK * NT):
                    n, t = divmod(i, NT)
                    if i + 2 < NT:
                        pre.root(core, pool, i + 2)
                    if (piece := k_store(n, t)) is not None:
                        dst, rows, cols = piece
                        pool.wait_ge(kv_taken, i + 1)
                        pool.dma_start(dst, k_rows[rows, i % ks, cols]).then_inc(k_stored[i % ks], 16)
                pool.wait_ge(kv_taken, NKV * NT)
                pool.dma_start(outs["prompt_b_v"].rearrange("(t p) n -> p t n", p=P),
                               v[:, 0:PT, P:]).then_inc(v_stored, 16)
                pool.dma_start(outs["prompt_a_v"], v[:, PT - 1, 0:P]).then_inc(v_stored, 16)
                pool.dma_start(outs["sample_b_v"], v[P - NS:P, PT, P:]).then_inc(v_stored, 16)
                pool.dma_start(outs["sample_a_v"], v[P - NS:P, PT, 0:P]).then_inc(v_stored, 16)
                pool.wait_ge(v_stored, 64)
                for s in range(ks):
                    pool.wait_ge(k_stored[s], 16 * count[s])

            @block.scalar
            def _(act):
                def split(n):
                    act.wait_ge(raw_in[n % 2], arrived[n])
                    if 2 <= n < NKV + 2:
                        act.wait_ge(kv_ready, NT * (n - 1))
                    elif n >= NKV + 2:
                        act.wait_ge(q_ready, 2 * (n - 1 - NKV))
                    nc.scalar.activation(w_hi[:, n % 2], raw[:, n % 2], ACT.Copy).then_inc(hi_done, 1)

                def square(t):
                    act.wait_ge(x_in[t % xs], 16 * (t // xs + 1 + (t == PT)))
                    pre.square(nc, act, x[:, t % xs, :], t)

                square(0)
                split(0)
                square(1)
                tn.take_hi(nc, act, 0)
                for n in range(NKV):
                    for t in range(NT):
                        i = n * NT + t
                        if i + 2 < NT:
                            square(i + 2)
                        if i + 1 < NT:
                            tn.take_hi(nc, act, i + 1)
                        if i == 4:
                            split(1)
                        act.wait_ge(kv_ready, i + 1)
                        got = core.ps[:, 6 + i % 2, 0:W]
                        if n < NK:
                            if i >= ks:
                                act.wait_ge(k_turned, i - ks + 1)
                                if stored_before[i]:
                                    act.wait_ge(k_stored[i % ks], 16 * stored_before[i])
                            op = nc.scalar.activation(k_rows[:, i % ks, :], got, ACT.Copy)
                            if n == 0:
                                op = nc.scalar.activation(v[:, t, 0:P], got[:, P:W], ACT.Copy)
                        else:
                            c = P + (n - NK) * W
                            op = nc.scalar.activation(v[:, t, c:c + W], got, ACT.Copy)
                        op.then_inc(kv_taken, 1)
                    if n + 2 < len(chunks):
                        split(n + 2)
                for m in range(KT):
                    act.wait_ge(q_ready, m + 1)
                    for j, (c, w) in enumerate(TOKEN_CHUNKS):
                        op = nc.scalar.activation(qT[:, m, c:c + w], core.ps[:, 3 * (m % 2) + j, 0:w], ACT.Copy)
                    op.then_inc(q_taken, 1)
                    n = NKV + m // 2 + 2
                    if m % 2 == 1 and n < len(chunks):
                        split(n)

            @block.vector
            def _(dve):
                def lo(n):
                    dve.wait_ge(hi_done, n + 1)
                    nc.vector.tensor_tensor(w_lo[:, n % 2], raw[:, n % 2], w_hi[:, n % 2].bitcast(F32),
                                            ALU.subtract).then_inc(lo_done, 1)

                def norm(t):
                    tn.wait_slot(dve, t)
                    pre.scale(nc, dve, x[:, t % xs, :], xn[:, t % 2, :], t)

                norm(0)
                norm(1)
                lo(0)
                tn.take_lo(nc, dve, 0)
                def take_keys(i):
                    n, t = divmod(i, NT)
                    dve.wait_ge(k_turned, i + 1)
                    c, new = new_columns(t)
                    if n == 0:
                        op = nc.vector.tensor_copy(kaT[:, c], core.ps[:, i % 2, new])
                    else:
                        j = 2 * (n - 1)
                        op = nc.vector.tensor_copy(kbT[:, j:j + 2, c], core.ps[:, i % 2, 0:W].rearrange(
                            "p (j c) -> p j c", j=2)[:, :, new])
                    op.then_inc(kT_taken, 1)

                for i in range(NT):
                    if i + 2 < NT:
                        norm(i + 2)
                    if i + 1 < NT:
                        tn.take_lo(nc, dve, i + 1)
                    if i == 4:
                        lo(1)
                    if i >= 1:
                        take_keys(i - 1)
                take_keys(NT - 1)
                for n in range(NK):
                    if n >= 1:
                        for t in range(NT):
                            take_keys(n * NT + t)
                    lo(n + 2)
                for n in range(NK + 2, len(chunks)):
                    lo(n)

            @block.tensor
            def _(pe):
                def turn(i):
                    n = i // NT
                    pe.wait_ge(kv_taken, i + 1)
                    if i >= 2:
                        pe.wait_ge(kT_taken, i - 1)
                    for j in range(1 if n == 0 else 2):
                        last = nc.tensor.transpose(core.ps[:, i % 2, j * P:(j + 1) * P],
                                                   k_rows[:, i % ks, j * P:(j + 1) * P], core.identity[:])
                    last.then_inc(k_turned, 1)

                tn.turn(core, pe, pre, 0)
                tn.turn(core, pe, pre, 1)
                for n in range(NKV):
                    pe.wait_ge(lo_done, n + 1)
                    for t in range(NT):
                        i = n * NT + t
                        if n == 0:
                            pe.wait_ge(tn.lo_done, t + 1)
                            if t >= 1 and t + 1 < NT:
                                tn.turn(core, pe, pre, t + 1)
                        if i >= 2:
                            pe.wait_ge(kv_taken, i - 1)
                        c = tile_start(t)
                        for k in range(KT):
                            for a, b in ((xT_hi, w_hi), (xT_hi, w_lo), (xT_lo, w_hi)):
                                last = nc.tensor.matmul(core.ps[:, 6 + i % 2, 0:W], a[:, k, c:c + P], b[:, n % 2, k, :],
                                                        start=(k == 0 and b is w_hi and a is xT_hi),
                                                        stop=(k == KT - 1 and a is xT_lo))
                        last.then_inc(kv_ready, 1)
                        if 1 <= i <= NK * NT:
                            turn(i - 1)
                for m in range(KT):
                    n = NKV + m // 2
                    pe.wait_ge(lo_done, n + 1)
                    if m == 0:
                        pe.wait_ge(kT_taken, NK * NT)
                    if m >= 2:
                        pe.wait_ge(q_taken, m - 1)
                    for k in range(KT):
                        for a, b in ((w_hi, xT_hi), (w_hi, xT_lo), (w_lo, xT_hi)):
                            lhs = a[:, n % 2, k, (m % 2) * P:(m % 2 + 1) * P]
                            for j, (c, w) in enumerate(TOKEN_CHUNKS):
                                last = nc.tensor.matmul(core.ps[:, 3 * (m % 2) + j, 0:w], lhs, b[:, k, c:c + w],
                                                        start=(k == 0 and a is w_hi and b is xT_hi),
                                                        stop=(k == KT - 1 and a is w_lo))
                    last.then_inc(q_ready, 1)


def prompt_attention(core, qT, kaT, kbT, v, prompt_bias, sinks):
    nc = core.nc
    SB = 7
    LAG = 5
    WA, WB = 2 * P, SEQ
    HEADS = 2 * NH
    with ExitStack() as mem:
        bias = core.sb("pa_bias", [P, NH * (WA + WB)], F32, mem)
        bias_a = bias[:, 0:NH * WA].rearrange("p (h c) -> p h c", h=NH)
        bias_b = bias[:, NH * WA:].rearrange("p (h c) -> p h c", h=NH)
        sink_b = core.sb("pa_sink", [P, NH], F32, mem)
        neg_sink = core.sb("pa_neg_sink", [P, NH], F32, mem)
        k_hi, k_lo = (core.sb(name, [P, 1 + NH // 2, SEQ], F32R, mem) for name in ("pa_k_hi", "pa_k_lo"))
        q_hi = core.sb("pa_q_hi", [P, HEADS, P], F32R, mem)
        q_lo = core.sb("pa_q_lo", [P, HEADS, P], F32R, mem)
        probs = core.sb("pa_probs", [P, SB, SEQ], F32, mem)
        pT = core.sb("pa_pT", [P, 2, 4 * P], F32, mem)
        least = core.sb("pa_least", [P, PT, HEADS], F32, mem)
        den = core.sb("pa_den", [P, PT, HEADS], F32, mem)
        rden = den
        tables_in = [core.sem(f"pa_tables_in{x}") for x in range(3)]
        sink_ready = core.sem("pa_sink_ready")
        q_cleared = core.sem("pa_q_cleared")
        hi_done = core.sem("pa_hi_done")
        lo_done = core.sem("pa_lo_done")
        scored = core.sem("pa_scored")
        biased = core.sem("pa_biased")
        exped = core.sem("pa_exped")
        rden_ready = core.sem("pa_rden_ready")
        normed = core.sem("pa_normed")
        turned = core.sem("pa_turned")
        copied = [core.sem("pa_copied_act"), core.sem("pa_copied_dve")]
        multiplied = core.sem("pa_multiplied")
        o_taken = core.sem("pa_o_taken")

        U = PT * HEADS
        zeros = probs[:, 0, 0:P]
        zeros_by_head = zeros.unsqueeze(1).to_broadcast([P, HEADS, P])

        def parts_of(u):
            return u // HEADS, u % HEADS // 2, u % 2

        def head(j, half):
            return j + 4 * half if j < 4 else 2 * (j - 4) + half

        def first_tile(u):
            i, j, _ = parts_of(u)
            return 0 if j >= 4 else max(0, i - 1)

        def n_tiles(u):
            return u // HEADS + 1 - first_tile(u)

        groups = [(u, g, min(2, n_tiles(u) - g)) for u in range(0, U, 2) for g in range(0, n_tiles(u), 2)]
        of_pair = {}
        for n, (u, _, _) in enumerate(groups):
            of_pair.setdefault(u, []).append(n)

        def groups_at(step):
            u = step - LAG
            mine = of_pair.get(u - u % 2, [])
            cut = (len(mine) + 1) // 2
            return mine[cut:] if u % 2 else mine[:cut]

        STEPS = U + LAG

        def turned_after(u):
            return of_pair[u - u % 2][-1] + 1

        def score_chunks(u):
            w = n_tiles(u) * P
            left = w if w <= 512 else 384 if w <= 768 else 512
            chunks = [(512 - left, 0, left)]
            if w > left:
                chunks.append((512, left, w - left))
            return chunks

        def score_ps(u):
            c, _, _ = score_chunks(u)[0]
            return core.banks(2 * (u % 2), 2)[:, c:c + n_tiles(u) * P]

        copier = [int(n % 2 == 1 and u % HEADS >= NH) for n, (u, _, _) in enumerate(groups)]

        def wait_for_copy(n):
            nc.tensor.wait_ge(copied[copier[n]], copier[:n + 1].count(copier[n]))

        def split_pieces(step):
            i, at = step // HEADS, step % HEADS
            if step < 0:
                return [0, 1, 2]
            if at == NH + 1 and i + 1 < PT:
                return [3 * (i + 1), 3 * (i + 1) + 1]
            return [3 * i + 2] if at == 1 and 0 < i < PT else []

        def piece_views(n):
            i, kind = divmod(n, 3)
            c = slice(i * P, (i + 1) * P)
            if kind == 0:
                return [(kaT[:, c], k_hi[:, 0, c], k_lo[:, 0, c]), (kbT[:, :, c], k_hi[:, 1:, c], k_lo[:, 1:, c])]
            views = []
            for half in range(2):
                rows = slice(half * HD, (half + 1) * HD)
                pairs = slice(4 * (kind - 1), 4 * kind)
                hi, lo = (x[rows].rearrange("p (j s) c -> p j s c", s=2)[:, pairs, half, :] for x in (q_hi, q_lo))
                views.append((qT[rows, pairs, c], hi, lo))
            return views

        def wait_for_scores(eng, n):
            i, kind = divmod(n, 3)
            if kind > 0 and i > 0:
                eng.wait_ge(scored, HEADS * (i - 1) + NH * kind)

        with nc.Block() as block:
            @block.sync
            def _(sp):
                sp.dma_start(bias[:, 0:NH * WA], prompt_bias[:, 0:NH * WA]).then_inc(tables_in[0], 16)
                sp.dma_start(sink_b[:], sinks.partition_broadcast(P)).then_inc(tables_in[0], 16)
                table_b = prompt_bias[:, NH * WA:].rearrange("p (h c) -> p h c", h=NH)
                for x, c in ((1, slice(WB - 2 * P, WB)), (2, slice(0, WB - 2 * P))):
                    sp.dma_start(bias_b[:, :, c], table_b[:, :, c]).then_inc(tables_in[x], 16)

            @block.gpsimd
            def _(pool):
                pool.wait_ge(q_cleared, 3)
                for step in range(-1, U):
                    for n in split_pieces(step):
                        pool.wait_ge(hi_done, 2 * (n + 1))
                        wait_for_scores(pool, n)
                        for x, (src, hi, lo) in enumerate(piece_views(n)):
                            if 2 * n + x > 0:
                                pool.wait_ge(lo_done, 2 * n + x)
                            nc.gpsimd.tensor_tensor(lo, src, hi.bitcast(F32), ALU.subtract).then_inc(lo_done, 1)

            @block.scalar
            def _(act):
                def high_parts(step):
                    for n in split_pieces(step):
                        wait_for_scores(act, n)
                        for x, hi, lo in piece_views(n):
                            nc.scalar.activation(hi, x, ACT.Copy).then_inc(hi_done, 1)

                def copy(n):
                    _, _, k = groups[n]
                    act.wait_ge(turned, n + 1)
                    if n >= 2:
                        act.wait_ge(multiplied, n - 1)
                    nc.scalar.activation(pT[:, n % 2, 0:2 * k * P], core.ps[:, 4 + n % 2, 0:2 * k * P],
                                         ACT.Copy).then_inc(copied[0], 1)

                act.wait_ge(q_cleared, 1)
                nc.scalar.activation(q_lo[:], zeros_by_head, ACT.Copy).then_inc(q_cleared, 1)
                act.wait_ge(q_cleared, 3)
                high_parts(-1)
                for step in range(STEPS):
                    for n in groups_at(step):
                        if copier[n] == 0:
                            copy(n)
                    if step < U:
                        u = step
                        i, j, half = parts_of(u)
                        w = n_tiles(u) * P
                        act.wait_ge(biased, u + 1)
                        d = 2 * j + half
                        row = probs[:, u % SB, 0:w + (j < 4)]
                        nc.scalar.activation(row, row, ACT.Exp, bias=least[:, i, d:d + 1], scale=-1.0,
                                             accum_out=den[:, i, d:d + 1]).then_inc(exped, 1)
                    high_parts(step)

            @block.vector
            def _(dve):
                def take_outputs(u):
                    i, j, _ = parts_of(u)
                    group = j // 4
                    dve.wait_ge(multiplied, turned_after(u))
                    dve.wait_ge(lo_done, 2 * (3 * i + 2 + group))
                    nc.vector.tensor_copy(qT[:, 4 * group:4 * group + 4, i * P:(i + 1) * P],
                                          core.ps[:, 6 + group, :].rearrange("p (j c) -> p j c", j=4)).then_inc(o_taken, 1)

                nc.vector.memset(zeros, 0.0).then_inc(q_cleared, 1)
                dve.wait_ge(q_cleared, 1)
                nc.vector.tensor_copy(q_hi[:], zeros_by_head).then_inc(q_cleared, 1)
                dve.wait_ge(q_cleared, 3)
                dve.wait_ge(tables_in[0], 32)
                nc.vector.tensor_scalar(neg_sink[:], sink_b[:], -1.0, None, ALU.mult).then_inc(sink_ready, 1)
                dve.wait_ge(sink_ready, 1)
                for step in range(STEPS + 1):
                    if step < U:
                        u = step
                        i, j, half = parts_of(u)
                        h = head(j, half)
                        d = 2 * j + half
                        w = n_tiles(u) * P
                        dve.wait_ge(scored, u + 1)
                        if u >= SB:
                            dve.wait_ge(turned, turned_after(u - SB))
                        if j < 4:
                            table, start = bias_a[:, h, WA - w:], neg_sink[:, h:h + 1]
                            nc.vector.tensor_copy(probs[:, u % SB, w:w + 1], start)
                        else:
                            if i in (0, 2) and d == NH:
                                dve.wait_ge(tables_in[1 + i // 2], 16)
                            table, start = bias_b[:, h, WB - w:], -NEG
                        nc.vector.tensor_tensor_reduce(probs[:, u % SB, 0:w], score_ps(u), table, -0.125, start,
                                                       ALU.add, ALU.min, least[:, i, d:d + 1]).then_inc(biased, 1)
                    if 1 <= step <= U:
                        i, d = divmod(step - 1, HEADS)
                        dve.wait_ge(exped, step)
                        nc.vector.reciprocal(rden[:, i, d:d + 1], den[:, i, d:d + 1]).then_inc(rden_ready, 1)
                    for n in groups_at(step):
                        if copier[n] == 1:
                            dve.wait_ge(turned, n + 1)
                            if n >= 2:
                                dve.wait_ge(multiplied, n - 1)
                            k = groups[n][2]
                            nc.vector.tensor_copy(pT[:, n % 2, 0:2 * k * P],
                                                  core.ps[:, 4 + n % 2, 0:2 * k * P]).then_inc(copied[1], 1)
                    if 1 <= step <= U:
                        dve.wait_ge(rden_ready, step)
                        row = probs[:, (step - 1) % SB, 0:n_tiles(step - 1) * P]
                        nc.vector.tensor_scalar(row, row, rden[:, i, d:d + 1], None, ALU.mult).then_inc(normed, 1)
                    u = step - LAG - 2
                    if u >= 0 and u % NH == NH - 1:
                        take_outputs(u)
                take_outputs(U - 1)

            @block.tensor
            def _(pe):
                def scores(u):
                    i, j, half = parts_of(u)
                    if u % NH == 0:
                        pe.wait_ge(lo_done, 2 * (3 * i + 2 + u // NH % 2))
                    if u >= 2:
                        pe.wait_ge(biased, u - 1)
                    k0 = first_tile(u) * P
                    d = 2 * j + half
                    k_high, k_low = (k[:, max(0, j - 3), :] for k in (k_hi, k_lo))
                    for q, k in ((q_hi, k_high), (q_hi, k_low), (q_lo, k_high)):
                        for c, kc, w in score_chunks(u):
                            last = nc.tensor.matmul(core.banks(2 * (u % 2), 2)[:, c:c + w], q[:, d, :],
                                                    k[:, k0 + kc:k0 + kc + w], start=(q is q_hi and k is k_high),
                                                    stop=(q is q_lo))
                    last.then_inc(scored, 1)

                def turn(n):
                    u, g, k = groups[n]
                    if g == 0:
                        pe.wait_ge(normed, u + 2)
                    if n >= 2:
                        wait_for_copy(n - 2)
                    for half in range(2):
                        for t in range(k):
                            c = (half * k + t) * P
                            last = nc.tensor.transpose(core.ps[:, 4 + n % 2, c:c + P],
                                                       probs[:, (u + half) % SB, (g + t) * P:(g + t + 1) * P],
                                                       core.identity[:])
                    last.then_inc(turned, 1)

                def multiply(n):
                    u, g, k = groups[n]
                    i, j, _ = parts_of(u)
                    if g == 0 and j % 4 == 0 and i > 0:
                        pe.wait_ge(o_taken, 2 * i - 1 + j // 4)
                    wait_for_copy(n)
                    for t in range(k):
                        kt = first_tile(u) + g + t
                        for half in range(2):
                            vc = half * HD if j < 4 else P + (2 * (j - 4) + half) * HD
                            c = (half * k + t) * P
                            last = nc.tensor.matmul(core.ps[half * HD:(half + 1) * HD, 6 + j // 4,
                                                            j % 4 * P:(j % 4 + 1) * P],
                                                    v[:, kt, vc:vc + HD], pT[:, n % 2, c:c + P],
                                                    start=(g + t == 0), stop=(g + t == n_tiles(u) - 1))
                    last.then_inc(multiplied, 1)

                for step in range(STEPS):
                    if step < U:
                        scores(step)
                    for n in groups_at(step):
                        turn(n)
                        if n >= 1:
                            multiply(n - 1)
                multiply(len(groups) - 1)


def sample_attention(core, qT, kaT, kbT, v, cache, sinks, bias_b, bias_a):
    nc = core.nc
    HQ = NH * NQ
    PAIRS = NH // 2
    W = CT * P
    OWN = W + P
    RING = 3
    with ExitStack() as mem:
        kb = core.sb("sa_kb", [P, CT, 512], F32, mem)
        vb = core.sb("sa_vb", [P, 2, CT, 512], F32, mem)
        ka = core.sb("sa_ka", [P, 2, P], F32, mem)
        va = core.sb("sa_va", [P, 2, P], F32, mem)
        kT = core.sb("sa_kT", [P, CT, PAIRS, P], F32, mem)
        kT_a = core.sb("sa_kT_a", [P, P], F32, mem)
        q_b = core.sb("sa_q_b", [P, NB, PAIRS, 32], F32, mem)
        q_a = core.sb("sa_q_a", [P, NB, HQ], F32, mem)
        table_b = core.sb("sa_table_b", [P, W + NQ], F32, mem)
        table_a = core.sb("sa_table_a", [HQ, P + NQ], F32, mem)
        sink = core.sb("sa_sink", [HQ, 1], F32, mem)
        pb = core.sb("sa_pb", [P, 2, OWN], F32, mem)
        pa = core.sb("sa_pa", [HQ, 2, 2 * P], F32, mem)
        pT = core.sb("sa_pT", [P, CT + 1, P], F32, mem)
        pT_a = core.sb("sa_pT_a", [P, 2, HQ], F32, mem)
        m_cache = core.sb("sa_m_cache", [P, NB, 2], F32, mem)
        m = core.sb("sa_m", [P, NB, 2], F32, mem)
        neg_m = core.sb("sa_neg_m", [P, NB, 2], F32, mem)
        den = core.sb("sa_den", [P, NB, 5], F32, mem)
        den_sum = core.sb("sa_den_sum", [P, NB, 2], F32, mem)
        rden = core.sb("sa_rden", [P, NB, 2], F32, mem)
        o = core.sb("sa_o", [P, 2 * P], F32, mem)

        kb_in = [core.sem(f"sa_kb_in{t}") for t in range(CT)]
        ka_in = [core.sem(f"sa_ka_in{x}") for x in range(2)]
        v_in = [core.sem(f"sa_v_in{x}") for x in range(2)]
        tables_in = core.sem("sa_tables_in")
        cleared = core.sem("sa_cleared")
        q_ready = core.sem("sa_q_ready")
        own_cleared = core.sem("sa_own_cleared")
        keys_turned = core.sem("sa_keys_turned")
        copied = [core.sem("sa_copied_act"), core.sem("sa_copied_dve")]
        scored = core.sem("sa_scored")
        cache_biased = core.sem("sa_cache_biased")
        biased = core.sem("sa_biased")
        negated = core.sem("sa_negated")
        exped = core.sem("sa_exped")
        den_ready = core.sem("sa_den_ready")
        rden_ready = core.sem("sa_rden_ready")
        normed = core.sem("sa_normed")
        probs_turned = core.sem("sa_probs_turned")
        multiplied = core.sem("sa_multiplied")
        o_copied = core.sem("sa_o_copied")
        o_turned = core.sem("sa_o_turned")
        o_taken = core.sem("sa_o_taken")

        KG = CT + 1
        PG = [(0, 4), (4, 4), (8, 3), (None, 2)]
        order = []
        for b in range(NB + 1):
            if b < NB:
                order += [("key", b, t) for t in range(KG)]
            if b >= 1:
                order += [("prob", b - 1, g) for g in range(len(PG))]
        at = {x: n for n, x in enumerate(order)}

        def bank(n):
            return n % RING

        def copied_by(n):
            return copied[n % 2], n // 2 + 1

        def copy_entry(copy, n):
            kind, b, x = order[n]
            if kind == "key" and x < CT:
                return copy(kT[:, x], core.ps[:, bank(n), :].rearrange("p (c k) -> p c k", c=PAIRS))
            if kind == "key":
                return copy(kT_a[:], core.ps[:, bank(n), 0:P])
            first, count = PG[x]
            if first is None:
                return copy(pT_a[:], core.ps[:, bank(n), 0:2 * HQ].rearrange("p (t r) -> p t r", t=2))
            return copy(pT[:, first:first + count, :],
                        core.ps[:, bank(n), 0:count * P].rearrange("p (t r) -> p t r", t=count))

        def wait_for_entry(eng, n):
            kind, b, x = order[n]
            if kind == "key":
                eng.wait_ge(keys_turned, KG * b + x + 1)
                if b >= 1:
                    eng.wait_ge(scored, b)
            else:
                eng.wait_ge(probs_turned, len(PG) * b + x + 1)
                if b >= 1:
                    eng.wait_ge(multiplied, b)

        score_b = core.banks(4, 3)
        score_a = core.ps[0:HQ, 7, 0:P + NQ]

        with nc.Block() as block:
            @block.sync
            def _(sp):
                def load_keys(b):
                    if b >= 2:
                        sp.wait_ge(keys_turned, KG * (b - 1))
                    sp.dma_start(ka[:, b % 2, :], cache["a_k"][b]).then_inc(ka_in[b % 2], 16)
                    far = cache["b_k"][b].rearrange("(t m s) c -> t m s c", m=16, s=16)
                    for t in range(CT):
                        if b >= 1:
                            sp.wait_ge(keys_turned, KG * (b - 1) + t + 1)
                        src = far[t, :, 0:8, :] if t < FAR_TILES else \
                            cache["b_k"][b, FAR + (t - FAR_TILES) * P:FAR + (t - FAR_TILES + 1) * P, :]
                        sp.dma_start(kb[:, t, :], src).then_inc(kb_in[t], 16)

                def load_values(b):
                    if b >= 2:
                        sp.wait_ge(multiplied, b - 1)
                    far = cache["b_v"][b].rearrange("(t m s) c -> t m s c", m=16, s=16)
                    for t in range(FAR_TILES):
                        sp.dma_start(vb[:, b % 2, t, :], far[t, :, 0:8, :]).then_inc(v_in[b % 2], 16)
                    sp.dma_start(vb[:, b % 2, FAR_TILES:CT, :],
                                 cache["b_v"][b, FAR:PAST, :].rearrange("(t p) c -> p t c", p=P)).then_inc(v_in[b % 2], 16)
                    sp.dma_start(va[:, b % 2, :], cache["a_v"][b]).then_inc(v_in[b % 2], 16)

                load_keys(0)
                sp.dma_start(table_b[:], bias_b).then_inc(tables_in, 16)
                sp.dma_start(table_a[:], bias_a).then_inc(tables_in, 16)
                for h in range(NH):
                    sp.dma_start(sink[h * NQ:(h + 1) * NQ, :],
                                 sinks[h:h + 1].partition_broadcast(NQ)).then_inc(tables_in, 16)
                for b in range(1, NB):
                    load_keys(b)
                    load_values(b - 1)
                load_values(NB - 1)

            @block.gpsimd
            def _(pool):
                for b in range(NB):
                    if b >= 2:
                        pool.wait_ge(probs_turned, len(PG) * (b - 1))
                    nc.gpsimd.memset(pb[:, b % 2, W:OWN], 0.0)
                    nc.gpsimd.memset(pa[:, b % 2, P:2 * P], 0.0).then_inc(own_cleared, 1)

            @block.scalar
            def _(act):
                def copies(kind, b, count):
                    for x in range(count):
                        n = at[kind, b, x]
                        if n % 2 == 0:
                            wait_for_entry(act, n)
                            copy_entry(lambda out, in_: nc.scalar.activation(out, in_, ACT.Copy), n).then_inc(copied[0], 1)

                def exps(b):
                    act.wait_ge(negated, b + 1)
                    own = slice(W + P - NS + b * NQ, W + P - NS + (b + 1) * NQ)
                    own_a = slice(own.start - W + P, own.stop - W + P)
                    x = b % 2
                    nb, na = neg_m[:, b, 0:1], neg_m[0:HQ, b, 1:2]
                    nc.scalar.activation(pb[:, x, 0:W], pb[:, x, 0:W], ACT.Exp, bias=nb, accum_out=den[:, b, 0:1])
                    nc.scalar.activation(pb[:, x, own], pb[:, x, own], ACT.Exp, bias=nb, accum_out=den[:, b, 2:3])
                    nc.scalar.activation(pa[:, x, 0:P], pa[:, x, 0:P], ACT.Exp, bias=na, accum_out=den[0:HQ, b, 1:2])
                    nc.scalar.activation(pa[:, x, own_a], pa[:, x, own_a], ACT.Exp, bias=na, accum_out=den[0:HQ, b, 3:4])
                    nc.scalar.activation(den[0:HQ, b, 4:5], sink[:], ACT.Exp, bias=na).then_inc(exped, 1)

                for b in range(NB + 1):
                    if b < NB:
                        copies("key", b, KG)
                    if b >= 1:
                        copies("prob", b - 1, len(PG))
                    if b < NB:
                        exps(b)

            @block.vector
            def _(dve):
                def copies(kind, b, count):
                    for x in range(count):
                        n = at[kind, b, x]
                        if n % 2 == 1:
                            wait_for_entry(dve, n)
                            copy_entry(nc.vector.tensor_copy, n).then_inc(copied[1], 1)

                def softmax(b):
                    x = b % 2
                    own = slice(W + P - NS + b * NQ, W + P - NS + (b + 1) * NQ)
                    own_a = slice(own.start - W + P, own.stop - W + P)
                    dve.wait_ge(scored, b + 1)
                    dve.wait_ge(own_cleared, b + 1)
                    if b >= 2:
                        dve.wait_ge(probs_turned, len(PG) * (b - 1))
                    nc.vector.tensor_tensor_reduce(pb[:, x, 0:W], score_b[:, 0:W], table_b[:, 0:W], 0.125, NEG,
                                                   ALU.add, ALU.max, m_cache[:, b, 0:1]).then_inc(cache_biased, 1)
                    nc.vector.tensor_tensor_reduce(pa[:, x, 0:P], score_a[:, 0:P], table_a[:, 0:P], 0.125, sink[:, 0:1],
                                                   ALU.add, ALU.max, m_cache[0:HQ, b, 1:2]).then_inc(cache_biased, 1)
                    dve.wait_ge(cache_biased, 2 * (b + 1))
                    nc.vector.tensor_tensor_reduce(pb[:, x, own], score_b[:, W:W + NQ], table_b[:, W:W + NQ], 0.125,
                                                   m_cache[:, b, 0:1], ALU.add, ALU.max, m[:, b, 0:1]).then_inc(biased, 1)
                    nc.vector.tensor_tensor_reduce(pa[:, x, own_a], score_a[:, P:P + NQ], table_a[:, P:P + NQ], 0.125,
                                                   m_cache[0:HQ, b, 1:2], ALU.add, ALU.max,
                                                   m[0:HQ, b, 1:2]).then_inc(biased, 1)
                    dve.wait_ge(biased, 2 * (b + 1))
                    nc.vector.tensor_scalar(neg_m[:, b], m[:, b], -1.0, None, ALU.mult).then_inc(negated, 1)

                def normalise(b):
                    x = b % 2
                    dve.wait_ge(exped, b + 1)
                    nc.vector.tensor_tensor(den_sum[:, b], den[:, b, 0:2], den[:, b, 2:4], ALU.add).then_inc(den_ready, 1)
                    dve.wait_ge(den_ready, 2 * b + 1)
                    nc.vector.tensor_tensor(den_sum[0:HQ, b, 1:2], den_sum[0:HQ, b, 1:2], den[0:HQ, b, 4:5],
                                            ALU.add).then_inc(den_ready, 1)
                    dve.wait_ge(den_ready, 2 * b + 2)
                    nc.vector.reciprocal(rden[:, b], den_sum[:, b]).then_inc(rden_ready, 1)
                    dve.wait_ge(rden_ready, b + 1)
                    nc.vector.tensor_scalar(pb[:, x, :], pb[:, x, :], rden[:, b, 0:1], None, ALU.mult)
                    nc.vector.tensor_scalar(pa[:, x, :], pa[:, x, :], rden[0:HQ, b, 1:2], None,
                                            ALU.mult).then_inc(normed, 1)

                def o_copy(b):
                    dve.wait_ge(multiplied, b + 1)
                    if b >= 1:
                        dve.wait_ge(o_turned, b)
                    nc.vector.tensor_copy(o[:, 0:P], core.ps[:, 3, 0:P])
                    nc.vector.tensor_copy(o[0:HQ, P:2 * P], core.ps[0:HQ, 3, P:2 * P]).then_inc(o_copied, 1)

                def o_take(b):
                    dve.wait_ge(o_turned, b + 1)
                    for half in range(2):
                        rows = slice(half * HD, (half + 1) * HD)
                        out = qT[rows, :, SEQ + b * NQ:SEQ + (b + 1) * NQ]
                        got_b = core.ps[rows, 3, 2 * P:3 * P].rearrange("p (c x) -> p c x", c=PAIRS)
                        got_a = core.ps[rows, 3, 3 * P:3 * P + HQ].rearrange("p (s j i) -> p s j i", s=2, j=PAIRS)
                        nc.vector.tensor_copy(out[:, PAIRS:, :], got_b[:, :, half * NQ:(half + 1) * NQ])
                        last = nc.vector.tensor_copy(out[:, 0:PAIRS, :], got_a[:, half])
                    last.then_inc(o_taken, 1)

                for tile in (q_b, q_a, m, den, m_cache):
                    nc.vector.memset(tile[:], 0.0 if tile in (q_b, q_a) else 1.0).then_inc(cleared, 1)
                dve.wait_ge(cleared, 5)
                for half in range(2):
                    rows = slice(half * HD, (half + 1) * HD)
                    for j in range(PAIRS):
                        c = half * HQ // 2 + j * NQ
                        nc.vector.tensor_copy(q_a[rows, :, c:c + NQ],
                                              qT[rows, j, SEQ:TOK].rearrange("p (b i) -> p b i", b=NB))
                        nc.vector.tensor_copy(q_b[rows, :, j, half * NQ:(half + 1) * NQ],
                                              qT[rows, PAIRS + j, SEQ:TOK].rearrange("p (b i) -> p b i", b=NB)
                                              ).then_inc(q_ready, 1)
                for b in range(NB + 2):
                    if b < NB:
                        copies("key", b, KG)
                    if b >= 2:
                        o_take(b - 2)
                    if 1 <= b <= NB:
                        copies("prob", b - 1, len(PG))
                    if b < NB:
                        if b == 0:
                            dve.wait_ge(tables_in, 16 * (2 + NH))
                        softmax(b)
                    if 1 <= b <= NB:
                        o_copy(b - 1)
                    if b < NB:
                        normalise(b)

            @block.tensor
            def _(pe):
                def bank_free(n):
                    if n >= RING:
                        pe.wait_ge(*copied_by(n - RING))

                def turn_keys(b):
                    for t in range(KG):
                        n = at["key", b, t]
                        bank_free(n)
                        if t < CT:
                            pe.wait_ge(kb_in[t], 16 * (b + 1))
                            for c in range(PAIRS):
                                last = nc.tensor.transpose(core.ps[:, bank(n), c * P:(c + 1) * P],
                                                           kb[:, t, c * P:(c + 1) * P], core.identity[:])
                        else:
                            pe.wait_ge(ka_in[b % 2], 16 * (b // 2 + 1))
                            last = nc.tensor.transpose(core.ps[:, bank(n), 0:P], ka[:, b % 2, :], core.identity[:])
                        last.then_inc(keys_turned, 1)

                def score(b):
                    for n in (at["key", b, KG - 1], at["key", b, KG - 2]):
                        pe.wait_ge(*copied_by(n))
                    if b >= 1:
                        pe.wait_ge(biased, 2 * b)
                    own = slice(SEQ + b * NQ, SEQ + (b + 1) * NQ)
                    for t in range(0, CT, 4):
                        e = min(CT, t + 4)
                        for c in range(PAIRS):
                            nc.tensor.matmul(score_b[32 * c:32 * c + 32, t * P:e * P], q_b[:, b, c, :], kT[:, t:e, c, :],
                                             start=True, stop=True)
                    for c in range(PAIRS):
                        nc.tensor.matmul(score_b[32 * c:32 * c + 32, W:W + NQ], q_b[:, b, c, :],
                                         kbT[:, c, own],
                                         start=True, stop=True)
                    nc.tensor.matmul(score_a[:, 0:P], q_a[:, b, :], kT_a[:], start=True, stop=True)
                    nc.tensor.matmul(score_a[:, P:P + NQ], q_a[:, b, :], kaT[:, own], start=True,
                                     stop=True).then_inc(scored, 1)

                def turn_probs(b):
                    pe.wait_ge(normed, b + 1)
                    for g, (first, count) in enumerate(PG):
                        n = at["prob", b, g]
                        bank_free(n)
                        for x in range(count):
                            if first is None:
                                last = nc.tensor.transpose(core.ps[:, bank(n), x * HQ:(x + 1) * HQ],
                                                           pa[:, b % 2, x * P:(x + 1) * P], core.identity[0:HQ, 0:HQ])
                            else:
                                last = nc.tensor.transpose(core.ps[:, bank(n), x * P:(x + 1) * P],
                                                           pb[:, b % 2, (first + x) * P:(first + x + 1) * P],
                                                           core.identity[:])
                        last.then_inc(probs_turned, 1)

                def multiply(b):
                    pe.wait_ge(v_in[b % 2], 16 * (FAR_TILES + 2) * (b // 2 + 1))
                    if b >= 1:
                        pe.wait_ge(o_taken, b)
                    for g in range(len(PG)):
                        pe.wait_ge(*copied_by(at["prob", b, g]))
                    nc.tensor.matmul(core.ps[0:HQ, 3, P:2 * P], pT_a[:, 0, :], va[:, b % 2, :], start=True, stop=False)
                    nc.tensor.matmul(core.ps[0:HQ, 3, P:2 * P], pT_a[:, 1, :], v[:, PT, 0:P], start=False, stop=True)
                    for t in range(CT + 1):
                        for c in range(PAIRS):
                            rhs = vb[:, b % 2, t, c * P:(c + 1) * P] if t < CT else v[:, PT, P + c * P:P + (c + 1) * P]
                            last = nc.tensor.matmul(core.ps[32 * c:32 * c + 32, 3, 0:P], pT[:, t, 32 * c:32 * c + 32],
                                                    rhs, start=(t == 0), stop=(t == CT))
                    last.then_inc(multiplied, 1)

                def turn_outputs(b):
                    pe.wait_ge(o_copied, b + 1)
                    nc.tensor.transpose(core.ps[:, 3, 2 * P:3 * P], o[:, 0:P], core.identity[:])
                    nc.tensor.transpose(core.ps[:, 3, 3 * P:3 * P + HQ], o[0:HQ, P:2 * P],
                                        core.identity[0:HQ, 0:HQ]).then_inc(o_turned, 1)

                pe.wait_ge(q_ready, 2 * PAIRS)
                for b in range(NB + 2):
                    if b < NB:
                        turn_keys(b)
                    if b >= 2:
                        turn_outputs(b - 2)
                    if b < NB:
                        score(b)
                    if 1 <= b <= NB:
                        turn_probs(b - 1)
                        multiply(b - 1)


def out_project(core, oT, w_out, x_src, x_dst, post_gain, pre_gain, xT_hi, xT_lo):
    nc = core.nc
    with ExitStack() as mem:
        o_hi = core.sb("out_o_hi", [P, 2, KT, P], F32R, mem)
        o_lo = core.sb("out_o_lo", [P, 2, KT, P], F32R, mem)
        w_hi = core.sb("out_w_hi", [P, KT, D], F32R, mem)
        w_lo = core.sb("out_w_lo", [P, KT, D], F32R, mem)
        rows = core.sb("out_rows", [P, 2, D], F32, mem)
        xn = core.sb("out_xn", [P, 2, D], F32, mem)
        gains = core.sb("out_gains", [P, 2, D], F32, mem)
        pn = PostNorm(core, "out_", [rows[:, s, :] for s in range(2)], gains[:, 0, :], core.banks(2, 2))
        pre = PreNorm(core, "out_pre_", gains[:, 1, :], core.banks(2, 2))
        tn = Turned(core, "out_", xn, [core.feature_banks(0)], xT_hi, xT_lo)
        raw_in = [core.sem(f"out_raw_in{s}") for s in range(2)]
        w_hi_done = core.sem("out_w_hi_done")
        w_lo_done = core.sem("out_w_lo_done")
        o_hi_done = core.sem("out_o_hi_done")
        o_lo_done = core.sem("out_o_lo_done")
        y_ready = core.sem("out_y_ready")

        def w_pieces(k):
            if k >= KT // 2:
                return [(slice(0, P), w_out[k * P:(k + 1) * P, :])]
            return [(slice(h * HD, (h + 1) * HD), w_out[(k + 4 * h) * HD:(k + 4 * h + 1) * HD, :]) for h in range(2)]

        arrived = [16 * sum(len(w_pieces(j)) for j in range(k % 2, k + 1, 2)) for k in range(KT)]

        def y_of(t):
            return core.banks(4 + 2 * (t % 2), 2)

        def o_tile(t):
            return oT[:, :, tile_start(t):tile_start(t) + P]

        with nc.Block() as block:
            @block.sync
            def _(sp):
                for k in range(KT):
                    if k >= 2:
                        sp.wait_ge(w_lo_done, k - 1)
                    for part, src in w_pieces(k):
                        sp.dma_start(rows[part, k % 2, :], src).then_inc(raw_in[k % 2], 16)
                sp.dma_start(pn.gain, post_gain.partition_broadcast(P)).then_inc(pn.gain_in, 16)
                sp.dma_start(pre.gain, pre_gain.partition_broadcast(P)).then_inc(pre.gain_in, 16)
                sp.wait_ge(w_lo_done, KT)
                pn.load(sp, x_src, 0)
                pn.load(sp, x_src, 1)
                for t in range(NT):
                    pn.store(sp, x_dst, t)
                    if t + 2 < NT:
                        pn.load(sp, x_src, t + 2, pre)
                pn.wait_stored(sp)

            @block.scalar
            def _(act):
                def split_o(t):
                    if t >= 2:
                        act.wait_ge(y_ready, t - 1)
                    nc.scalar.activation(o_hi[:, t % 2], o_tile(t), ACT.Copy).then_inc(o_hi_done, 1)

                for k in range(KT):
                    if k < 2:
                        split_o(k)
                    act.wait_ge(raw_in[k % 2], arrived[k])
                    nc.scalar.activation(w_hi[:, k, :], rows[:, k % 2, :], ACT.Copy).then_inc(w_hi_done, 1)
                for t in range(NT):
                    act.wait_ge(y_ready, t + 1)
                    if t + 2 < NT:
                        split_o(t + 2)
                    if t >= 1:
                        act.wait_ge(pre.squared, t)
                    pn.square(nc, act, y_of(t), t)
                    if t >= 1:
                        tn.take_hi(nc, act, t - 1)
                    act.wait_ge(pn.added, t + 1)
                    act.wait_ge(pn.squared, t + 1)
                    pre.square(nc, act, pn.x(t), t)
                tn.take_hi(nc, act, NT - 1)

            @block.gpsimd
            def _(pool):
                for t in range(NT):
                    pn.root(core, pool, t)
                    pre.root(core, pool, t)

            @block.vector
            def _(dve):
                def split_o(t):
                    dve.wait_ge(o_hi_done, t + 1)
                    if t >= 2:
                        dve.wait_ge(y_ready, t - 1)
                    nc.vector.tensor_tensor(o_lo[:, t % 2], o_tile(t), o_hi[:, t % 2].bitcast(F32),
                                            ALU.subtract).then_inc(o_lo_done, 1)

                for k in range(KT):
                    if k < 2:
                        split_o(k)
                    dve.wait_ge(w_hi_done, k + 1)
                    nc.vector.tensor_tensor(w_lo[:, k, :], rows[:, k % 2, :], w_hi[:, k, :].bitcast(F32),
                                            ALU.subtract).then_inc(w_lo_done, 1)
                for t in range(NT):
                    if t + 2 < NT:
                        split_o(t + 2)
                    tn.wait_slot(dve, t)
                    yn = xn[:, t % 2, :]
                    pn.scale(nc, dve, y_of(t), yn, t)
                    pn.add(nc, dve, yn, t)
                    if t >= 1:
                        tn.take_lo(nc, dve, t - 1)
                    dve.wait_ge(pn.added, t + 1)
                    pre.scale(nc, dve, pn.x(t), yn, t)
                tn.take_lo(nc, dve, NT - 1)

            @block.tensor
            def _(pe):
                def multiply(t, k):
                    for a, b in ((o_hi, w_hi), (o_hi, w_lo), (o_lo, w_hi)):
                        for n in range(2):
                            last = nc.tensor.matmul(core.ps[:, 4 + 2 * (t % 2) + n, :], a[:, t % 2, k, :],
                                                    b[:, k, n * 512:(n + 1) * 512],
                                                    start=(k == 0 and a is o_hi and b is w_hi),
                                                    stop=(k == KT - 1 and a is o_lo))
                    if k == KT - 1:
                        last.then_inc(y_ready, 1)

                pe.wait_ge(o_lo_done, 2)
                for k in range(KT):
                    pe.wait_ge(w_lo_done, k + 1)
                    for t in range(2):
                        multiply(t, k)
                for t in range(2, NT):
                    pe.wait_ge(o_lo_done, t + 1)
                    pe.wait_ge(pn.scaled, t - 1)
                    for k in range(KT):
                        multiply(t, k)
                    tn.turn(core, pe, pre, t - 2)
                tn.turn(core, pe, pre, NT - 2)
                tn.turn(core, pe, pre, NT - 1)


def mlp(core, tag, xT_hi, xT_lo, w1, w2, y, x_src, x_dst, post_gain, pre_gain=None):
    nc = core.nc
    w1_rows = w1.rearrange("(k p) n -> p k n", p=P)
    with ExitStack() as mem:
        h_hi = core.sb(tag + "h_hi", [P, FFB, TOK], F32R, mem)
        h_lo = core.sb(tag + "h_lo", [P, FFB, TOK], F32R, mem)
        w2_hi = core.sb(tag + "w2_hi", [P, FFB, D], F32R, mem)
        w2_lo = core.sb(tag + "w2_lo", [P, FFB, D], F32R, mem)
        relu = core.sb(tag + "relu", [P, 2, 384], F32, mem)
        square = core.sb(tag + "square", [P, 2, 384], F32, mem)
        rows = core.sb(tag + "rows", [P, 4, D], F32, mem, side="right")
        offset = nc.sbuf_top
        w1_hi = nc.alloc_sbuf_tensor_at(tag + "w1_hi", [P, 2, KT, P], F32R, offset=offset)
        w1_lo = nc.alloc_sbuf_tensor_at(tag + "w1_lo", [P, 2, KT, P], F32R, offset=offset + 2 * KT * P * 4)
        raw = core.sb(tag + "raw", [P, 2, D], F32, mem)
        raw_in = [core.sem(f"{tag}raw_in{s}") for s in range(2)]
        hi_done = core.sem(tag + "hi_done")
        lo_done = core.sem(tag + "lo_done")
        up_ready = core.sem(tag + "up_ready")
        relu_done = core.sem(tag + "relu_done")
        square_hi = core.sem(tag + "square_hi")
        squared = core.sem(tag + "squared")
        h_ready = core.sem(tag + "h_ready")
        part_ready = core.sem(tag + "part_ready")
        part_added = core.sem(tag + "part_added")
        y_zero = core.sem(tag + "y_zero")
        PARTS = 2 * NT
        pn = PostNorm(core, tag, [rows[:, s, :] for s in range(4)], raw[:, 0, :], core.banks(0, 2))
        pre = PreNorm(core, tag + "next_", raw[:, 1, :], core.banks(2, 2)) if pre_gain is not None else None

        def tile_source(b, n, ahead=0):
            if n in (3, 4, 5, 6):
                return w2[bass.ds((b + ahead) * (FFB * P) + (n - 3) * P, P), :]
            i = 3 if n == 7 else n
            return w1_rows[:, :, bass.ds((b + ahead) * (FFB * P) + i * P, P)]

        def raw_view(n):
            r = raw[:, n % 2, :]
            return r if n in (3, 4, 5, 6) else r.rearrange("p (k c) -> p k c", k=KT)

        def split_into(n):
            if n in (3, 4, 5, 6):
                return w2_hi[:, n - 3, :], w2_lo[:, n - 3, :]
            i = 3 if n == 7 else n
            return w1_hi[:, i % 2], w1_lo[:, i % 2]

        with nc.Block() as block:
            @block.sync
            def _(sp):
                def load(b, n, ahead=0, first=False):
                    if not first:
                        sp.wait_ge(lo_done, b * 8 + (8 * ahead + n - 1))
                    sp.dma_start(raw_view(n), tile_source(b, n, ahead)).then_inc(raw_in[n % 2], 16)

                load(0, 0, first=True)
                load(0, 1, first=True)
                for b in range(NBLK):
                    for n in range(2, 8):
                        load(b, n)
                    if b < NBLK - 1:
                        load(b, 0, 1)
                        load(b, 1, 1)
                sp.wait_ge(lo_done, NBLK * 8)
                sp.dma_start(pn.gain, post_gain.partition_broadcast(P)).then_inc(pn.gain_in, 16)
                if pre:
                    sp.dma_start(pre.gain, pre_gain.partition_broadcast(P)).then_inc(pre.gain_in, 16)
                sp.wait_ge(up_ready, NBLK * 4)
                for t in range(4):
                    pn.load(sp, x_src, t)
                for t in range(NT):
                    pn.store(sp, x_dst, t)
                    if t + 4 < NT:
                        pn.load(sp, x_src, t + 4, pre)
                pn.wait_stored(sp)

            @block.gpsimd
            def _(pool):
                nc.gpsimd.memset(y[:], 0.0).then_inc(y_zero, 1)
                for t in range(NT):
                    pn.root(core, pool, t)
                    if pre and t >= 1:
                        pre.root(core, pool, t - 1)
                if pre:
                    pre.root(core, pool, NT - 1)

            @block.scalar
            def _(act):
                def split(b, n, ahead=0, first=False):
                    m = 8 * ahead + n
                    act.wait_ge(raw_in[n % 2], b * 64 + 16 * (m // 2 + 1))
                    if n in (3, 4, 5, 6):
                        if not first:
                            act.wait_ge(part_ready, b * PARTS)
                    elif not first:
                        i = 4 * ahead + (3 if n == 7 else n)
                        act.wait_ge(up_ready, b * 4 + (i - 1))
                    nc.scalar.activation(split_into(n)[0], raw_view(n), ACT.Copy).then_inc(hi_done, 1)

                def hidden(b, i, first=False):
                    act.wait_ge(up_ready, b * 4 + (i + 1))
                    if i == 0 and not first:
                        act.wait_ge(part_ready, b * PARTS)
                    for j, (c, w) in enumerate(TOKEN_CHUNKS):
                        n = 3 * i + j
                        if not (first and n < 2):
                            act.wait_ge(squared, b * 12 + (n - 1))
                        nc.scalar.activation(relu[:, n % 2, 0:w], core.ps[:, 3 * (i % 2) + j, 0:w],
                                             ACT.Relu).then_inc(relu_done, 1)
                        act.wait_ge(relu_done, b * 12 + (n + 1))
                        nc.scalar.activation(h_hi[:, i, c:c + w], relu[:, n % 2, 0:w], ACT.Square).then_inc(square_hi, 1)

                def steps(b, last=False, first=False):
                    hidden(b, 0, first)
                    split(b, 2)
                    for n in (3, 4, 5, 6):
                        split(b, n, first=first)
                    split(b, 7)
                    hidden(b, 1)
                    if not last:
                        split(b, 0, 1)
                    hidden(b, 2)
                    if not last:
                        split(b, 1, 1)
                    hidden(b, 3)

                split(0, 0, first=True)
                split(0, 1, first=True)
                steps(0, first=True)
                with act.Fori(1, NBLK - 1) as b:
                    steps(b)
                steps(NBLK - 1, last=True)
                act.wait_ge(relu_done, NBLK * 12)
                for t in range(NT):
                    act.wait_ge(part_added, (NBLK - 1) * PARTS + 2 * (t + 1))
                    pn.square(nc, act, y[:, t, :], t)
                    if pre and t >= 1:
                        act.wait_ge(pn.added, t)
                        pre.square(nc, act, pn.x(t - 1), t - 1)
                if pre:
                    act.wait_ge(pn.added, NT)
                    pre.square(nc, act, pn.x(NT - 1), NT - 1)

            @block.vector
            def _(dve):
                def split(b, n, ahead=0):
                    dve.wait_ge(hi_done, b * 8 + (8 * ahead + n + 1))
                    hi, lo = split_into(n)
                    nc.vector.tensor_tensor(lo, raw_view(n), hi.bitcast(F32), ALU.subtract).then_inc(lo_done, 1)

                def hidden(b, i):
                    for j, (c, w) in enumerate(TOKEN_CHUNKS):
                        n = 3 * i + j
                        dve.wait_ge(relu_done, b * 12 + (n + 1))
                        nc.vector.tensor_tensor(square[:, n % 2, 0:w], relu[:, n % 2, 0:w], relu[:, n % 2, 0:w],
                                                ALU.mult).then_inc(squared, 1)
                        dve.wait_ge(squared, b * 12 + (n + 1))
                        dve.wait_ge(square_hi, b * 12 + (n + 1))
                        nc.vector.tensor_tensor(h_lo[:, i, c:c + w], square[:, n % 2, 0:w],
                                                h_hi[:, i, c:c + w].bitcast(F32), ALU.subtract).then_inc(h_ready, 1)

                def steps(b, last=False):
                    hidden(b, 0)
                    for n in range(2, 8):
                        split(b, n)
                    hidden(b, 1)
                    if not last:
                        split(b, 0, 1)
                    hidden(b, 2)
                    if not last:
                        split(b, 1, 1)
                    hidden(b, 3)
                    for n in range(PARTS):
                        dve.wait_ge(part_ready, b * PARTS + (n + 1))
                        part = y[:, n // 2, (n % 2) * 512:(n % 2 + 1) * 512]
                        nc.vector.tensor_tensor(part, part, core.ps[:, 6 + n % 2, :], ALU.add).then_inc(part_added, 1)
                        if last:
                            finish(n)

                def finish(n):
                    t = n // 2 - 1
                    if n % 2 == 0 and 0 <= t < NT:
                        pn.scale(nc, dve, y[:, t, :], y[:, t, :], t)
                    if n % 2 == 1:
                        if 0 <= t < NT:
                            pn.add(nc, dve, y[:, t, :], t)
                        if pre and 0 <= t - 1 < NT:
                            pre.scale(nc, dve, pn.x(t - 1), y[:, t - 1, :], t - 1)

                split(0, 0)
                split(0, 1)
                dve.wait_ge(y_zero, 1)
                with dve.Fori(0, NBLK - 1) as b:
                    steps(b)
                steps(NBLK - 1, last=True)
                for n in range(PARTS, PARTS + 4):
                    finish(n)

            @block.tensor
            def _(pe):
                def up(b, i, ahead=0, first=False):
                    pe.wait_ge(lo_done, b * 8 + (8 * ahead + (8 if i == 3 else i + 1)))
                    if not first:
                        pe.wait_ge(relu_done, b * 12 + (3 * (4 * ahead + i) - 3))
                    for k in range(KT):
                        for a, x in ((w1_hi, xT_hi), (w1_hi, xT_lo), (w1_lo, xT_hi)):
                            for j, (c, w) in enumerate(TOKEN_CHUNKS):
                                mm = nc.tensor.matmul(core.ps[:, 3 * (i % 2) + j, 0:w], a[:, i % 2, k, :],
                                                      x[:, k, c:c + w],
                                                      start=(k == 0 and a is w1_hi and x is xT_hi),
                                                      stop=(k == KT - 1 and a is w1_lo))
                    mm.then_inc(up_ready, 1)

                def down(b, first=False, last=False):
                    pe.wait_ge(lo_done, b * 8 + 7)
                    pe.wait_ge(h_ready, b * 12 + (9 if last else 12))
                    steps = [(n, range(FFB)) for n in range(PARTS)]
                    if last:
                        steps[0:2] = [(n, k) for k in (range(FFB - 1), range(FFB - 1, FFB)) for n in range(2)]
                    for n, tiles in steps:
                        t, half = n // 2, n % 2
                        if not (first and n < 2) and 0 in tiles:
                            pe.wait_ge(part_added, b * PARTS + (n - 1))
                        if last and n == 0 and 0 not in tiles:
                            pe.wait_ge(h_ready, b * 12 + 12)
                        s = tile_start(t)
                        for k in tiles:
                            for a, w in ((h_hi, w2_hi), (h_hi, w2_lo), (h_lo, w2_hi)):
                                mm = nc.tensor.matmul(core.ps[:, 6 + half, :], a[:, k, s:s + P],
                                                      w[:, k, half * 512:(half + 1) * 512],
                                                      start=(k == 0 and a is h_hi and w is w2_hi),
                                                      stop=(k == FFB - 1 and a is h_lo))
                        if FFB - 1 in tiles:
                            mm.then_inc(part_ready, 1)

                up(0, 0, first=True)
                up(0, 1, first=True)
                for i in (2, 3):
                    up(0, i)
                up(0, 0, 1)
                down(0, first=True)
                with pe.Fori(1, NBLK - 1) as b:
                    for i in (1, 2, 3):
                        up(b, i)
                    up(b, 0, 1)
                    down(b)
                for i in (1, 2, 3):
                    up(NBLK - 1, i)
                down(NBLK - 1, last=True)


def pool_mix(core, h, x_src, x_dst, state, pool_w, pool_scale, post_gain, pre_gain, tables, prompt_pool, sample_pool,
             xT_hi, xT_lo):
    nc = core.nc
    with ExitStack() as mem:
        before = core.sb("pm_before", [NB * CTX, D], F32, mem)
        band = core.sb("pm_band", [P, 4, 3, P], F32, mem)
        own = core.sb("pm_own", [P, 4, NS], F32, mem)
        ctx = core.sb("pm_ctx", [NB * CTX, 4, NS], F32, mem)
        w = core.sb("pm_w", [P, KT, 256], F32, mem)
        scale_b = core.sb("pm_scale", [P, D], F32, mem)
        yT = core.sb("pm_yT", [P, KT, TOK], F32, mem)
        z = core.sb("pm_z", [P, 2, D], F32, mem)
        xn = core.sb("pm_xn", [P, 2, D], F32, mem)
        rows = core.sb("pm_rows", [P, 2, D], F32, mem)
        gains = core.sb("pm_gains", [P, 2, D], F32, mem)
        junk = core.sb("pm_junk", [P, D], F32, mem)
        pn = PostNorm(core, "pm_", [rows[:, s, :] for s in range(2)] + [h[:, t, :] for t in range(NT - 2)],
                      gains[:, 0, :], junk[:])
        pre = PreNorm(core, "pm_pre_", gains[:, 1, :], junk[:])
        tn = Turned(core, "pm_", xn, [core.feature_banks(2)], xT_hi, xT_lo)
        band_in = core.sem("pm_band_in")
        tables_in = core.sem("pm_tables_in")
        weights_in = core.sem("pm_weights_in")
        pool_stored = core.sem("pm_pool_stored")
        pooled = core.sem("pm_pooled")
        yT_ready = core.sem("pm_yT_ready")
        z_ready = core.sem("pm_z_ready")
        z_scaled = core.sem("pm_z_scaled")
        pooled_ps = core.feature_banks(0)
        reach = max(POOL_W)

        def z_of(t):
            return core.banks(4 + 2 * (t % 2), 2)

        with nc.Block() as block:
            @block.sync
            def _(sp):
                sp.dma_start(band[:], tables["pool_band"].rearrange("p (g a c) -> p g a c", g=4, a=3)).then_inc(band_in, 16)
                sp.dma_start(w[:], pool_w.rearrange("(k p) n -> p k n", p=P)).then_inc(weights_in, 16)
                sp.dma_start(scale_b[:], pool_scale.partition_broadcast(P)).then_inc(weights_in, 16)
                pn.load(sp, x_src, 0)
                sp.dma_start(pn.gain, post_gain.partition_broadcast(P)).then_inc(pn.gain_in, 16)
                pn.load(sp, x_src, 1)
                sp.dma_start(pre.gain, pre_gain.partition_broadcast(P)).then_inc(pre.gain_in, 16)
                sp.dma_start(own[:], tables["pool_own"].rearrange("p (g c) -> p g c", g=4)).then_inc(tables_in, 16)
                sp.dma_start(ctx[:], tables["pool_ctx"].rearrange("p (g c) -> p g c", g=4)).then_inc(tables_in, 16)
                sp.dma_start(before[:], state).then_inc(tables_in, 16)
                sp.dma_start(prompt_pool, h[P - CTX:P, PT - 1, :]).then_inc(pool_stored, 16)
                for b in range(NB):
                    r = P - NS + b * NQ
                    sp.dma_start(sample_pool[b, CTX - NQ:CTX, :], h[r:r + NQ, PT, :]).then_inc(pool_stored, 16)
                    sp.dma_start(sample_pool[b, 0:CTX - NQ, :],
                                 state[b * CTX + NQ:(b + 1) * CTX, :]).then_inc(pool_stored, 16)
                for t in range(2, NT):
                    sp.wait_ge(pooled, t)
                    pn.load(sp, x_src, t)
                    pn.store(sp, x_dst, t - 2)
                pn.store(sp, x_dst, NT - 2)
                pn.store(sp, x_dst, NT - 1)
                pn.wait_stored(sp)
                sp.wait_ge(pool_stored, 16 * (2 * NB + 1))

            @block.gpsimd
            def _(pool):
                for t in range(NT):
                    pn.root(core, pool, t)
                    if t >= 1:
                        pre.root(core, pool, t - 1)
                pre.root(core, pool, NT - 1)

            @block.scalar
            def _(act):
                def take_pooled(t):
                    act.wait_ge(pooled, t + 1)
                    c, n = (t * P, P) if t < PT else (SEQ, NS)
                    nc.scalar.activation(yT[:, :, c:c + n], pooled_ps[:, :, 0:n], ACT.Copy).then_inc(yT_ready, 1)

                def square_z(t):
                    act.wait_ge(z_scaled, t + 1)
                    if t >= 2:
                        act.wait_ge(pre.squared, t - 1)
                    pn.square(nc, act, z[:, t % 2, :], t)

                def square_x(t):
                    act.wait_ge(pn.added, t + 1)
                    act.wait_ge(pn.squared, min(t + 2, NT))
                    pre.square(nc, act, pn.x(t), t)

                for t in range(NT + 4):
                    if t < NT:
                        take_pooled(t)
                    if 1 <= t <= NT:
                        square_z(t - 1)
                    if 2 <= t <= NT + 1:
                        square_x(t - 2)
                    if 4 <= t:
                        tn.take_hi(nc, act, t - 4)

            @block.vector
            def _(dve):
                def scale_z(t):
                    dve.wait_ge(z_ready, t + 1)
                    if t == 0:
                        dve.wait_ge(weights_in, 32)
                    if t >= 2:
                        dve.wait_ge(pn.added, t - 1)
                    nc.vector.tensor_tensor(z[:, t % 2, :], z_of(t), scale_b[:], ALU.mult).then_inc(z_scaled, 1)

                for t in range(NT + 4):
                    if 4 <= t:
                        tn.take_lo(nc, dve, t - 4)
                    if t < NT:
                        scale_z(t)
                    if 2 <= t <= NT + 1:
                        tn.wait_slot(dve, t - 2)
                        pre.scale(nc, dve, pn.x(t - 2), xn[:, t % 2, :], t - 2)
                    if 1 <= t <= NT:
                        zt = z[:, (t - 1) % 2, :]
                        pn.scale(nc, dve, zt, zt, t - 1)
                        pn.add(nc, dve, zt, t - 1)

            @block.tensor
            def _(pe):
                def mix(t):
                    pe.wait_ge(yT_ready, t + 1)
                    if t == 0:
                        pe.wait_ge(weights_in, 32)
                    if t >= 2:
                        pe.wait_ge(z_scaled, t - 1)
                    c = tile_start(t)
                    for g in range(4):
                        for k in range(2):
                            last = nc.tensor.matmul(z_of(t)[:, g * 256:(g + 1) * 256], yT[:, 2 * g + k, c:c + P],
                                                    w[:, 2 * g + k, :], start=(k == 0), stop=(k == 1))
                    last.then_inc(z_ready, 1)

                def pooling(t):
                    if t >= 1:
                        pe.wait_ge(yT_ready, t)
                    for f in range(KT):
                        fc, g = slice(f * P, (f + 1) * P), f // 2
                        if t == 0:
                            parts = [(h[:, 0, fc], band[:, g, 0, :])]
                        elif t < PT:
                            parts = [(h[:, t, fc], band[:, g, 1, :]), (h[HD:, t - 1, fc], band[HD:, g, 2, 0:reach])]
                        else:
                            parts = [(h[:, t, fc], own[:, g, :]), (before[:, fc], ctx[:, g, :])]
                        for j, (lhs, rhs) in enumerate(parts):
                            last = nc.tensor.matmul(pooled_ps[:, f, 0:rhs.shape[-1]], lhs, rhs, start=(j == 0),
                                                    stop=(j == len(parts) - 1))
                    last.then_inc(pooled, 1)

                pe.wait_ge(band_in, 16)
                for t in range(NT + 4):
                    if t == PT:
                        pe.wait_ge(tables_in, 48)
                    if t < NT:
                        pooling(t)
                    if 1 <= t <= NT:
                        mix(t - 1)
                    if 4 <= t:
                        tn.turn(core, pe, pre, t - 4)


def build(nc, ins, tables, outs, scratch):
    xp, xs = ins["x_prompt"], ins["x_sample"]
    gains = ins["norm_g"]
    x1, x2, x3 = (scratch[n] for n in ("x1", "x2", "x3"))
    halves = lambda x: (x[0:SEQ, :], x[SEQ:TOK, :])
    with ExitStack() as ctx:
        core = Core(nc, ctx)
        start(core, tables)
        core.end_stage()
        with ExitStack() as to_mlp0:
            with ExitStack() as attention:
                qT = core.sb("qT", [P, KT, TOK], F32, attention, side="right")
                with ExitStack() as mem:
                    kaT = core.sb("kaT", [P, TOK], F32, mem)
                    kbT = core.sb("kbT", [P, NH // 2, TOK], F32, mem)
                    v = core.sb("v", [P, NT, P + NH * HD], F32, mem)
                    with ExitStack() as inner:
                        xT_hi, xT_lo = (core.sb(n, [P, KT, TOK], F32R, inner) for n in ("a_xT_hi", "a_xT_lo"))
                        in_project(core, (xp, xs), gains[0], ins["attn_w_in"], xT_hi, xT_lo, qT, kaT, kbT, v, outs)
                        core.end_stage()
                    prompt_attention(core, qT, kaT, kbT, v, tables["prompt_bias"], ins["attn_sinks"])
                    core.end_stage()
                    sample_attention(core, qT, kaT, kbT, v, {n: ins["cache_" + n] for n in ("a_k", "a_v", "b_k", "b_v")},
                                     ins["attn_sinks"], tables["sample_bias_b"], tables["sample_bias_a"])
                    core.end_stage()
                xT_hi, xT_lo = (core.sb(n, [P, KT, TOK], F32R, to_mlp0) for n in ("m0_xT_hi", "m0_xT_lo"))
                out_project(core, qT, ins["attn_w_out"], (xp, xs), halves(x1), gains[1], gains[2], xT_hi, xT_lo)
                core.end_stage()
            y = core.sb("y", [P, NT, D], F32, side="right")
            mlp(core, "m0_", xT_hi, xT_lo, ins["mlp_w1"][0], ins["mlp_w2"][0], y, halves(x1), halves(x2), gains[3], gains[4])
            core.end_stage()
        xT_hi, xT_lo = (core.sb(n, [P, KT, TOK], F32R) for n in ("m1_xT_hi", "m1_xT_lo"))
        pool_mix(core, y, halves(x2), halves(x3), ins["state_pool"], ins["pool_w"], ins["pool_scale"], gains[5], gains[6],
                 tables, outs["prompt_pool"], outs["sample_pool"], xT_hi, xT_lo)
        core.end_stage()
        mlp(core, "m1_", xT_hi, xT_lo, ins["mlp_w1"][1], ins["mlp_w2"][1], y, halves(x3),
            (outs["y_prompt"], outs["y_sample"]), gains[7])
        core.end_stage()


def kernel(**inputs):
    import concourse.bacc as bacc
    from concourse.bass_utils import run_bass_kernel_spmd

    nc = bacc.Bacc("TRN2", target_bir_lowering=False, num_devices=1)
    shapes = {
        "x_prompt": (SEQ, D), "x_sample": (NS, D),
        "cache_a_k": (NB, P, P), "cache_a_v": (NB, P, P),
        "cache_b_k": (NB, PAST, NH * HD), "cache_b_v": (NB, PAST, NH * HD),
        "state_pool": (NB * CTX, D), "norm_g": (8, D), "attn_w_in": (D, 2304), "attn_w_out": (D, D),
        "attn_sinks": (NH,), "pool_w": (D, 256), "pool_scale": (D,),
        "mlp_w1": (2, D, DFF), "mlp_w2": (2, DFF, D),
    }
    arrays, ins, tables, outs, scratch = {}, {}, {}, {}, {}
    for name, shape in shapes.items():
        arrays[name] = np.ascontiguousarray(np.asarray(inputs[name]).reshape(shape))
        ins[name] = nc.dram_tensor(name, shape, F32, kind="ExternalInput").ap()
    for name, table in shape_constants().items():
        arrays["table_" + name] = table
        tables[name] = nc.dram_tensor("table_" + name, table.shape, F32, kind="ExternalInput").ap()
    results = {
        "y_prompt": ((SEQ, D), (1, SEQ, D)), "y_sample": ((NS, D), (NB, NQ, D)),
        "prompt_a_k": ((P, P), (1, 1, P, 2, HD)), "prompt_a_v": ((P, P), (1, 1, P, 2, HD)),
        "prompt_b_k": ((SEQ, 512), (1, 1, SEQ, NH, HD)), "prompt_b_v": ((SEQ, 512), (1, 1, SEQ, NH, HD)),
        "prompt_pool": ((CTX, D), (1, 1, CTX, D)),
        "sample_a_k": ((NS, P), (1, NB, NQ, 2, HD)), "sample_a_v": ((NS, P), (1, NB, NQ, 2, HD)),
        "sample_b_k": ((NS, 512), (1, NB, NQ, NH, HD)), "sample_b_v": ((NS, 512), (1, NB, NQ, NH, HD)),
        "sample_pool": ((NB, CTX, D), (1, NB, CTX, D)),
    }
    for name, (shape, _) in results.items():
        outs[name] = nc.dram_tensor("out_" + name, shape, F32, kind="ExternalOutput").ap()
    for name in ("x1", "x2", "x3"):
        scratch[name] = nc.dram_tensor("scratch_" + name, (TOK, D), F32, kind="Internal").ap()
    build(nc, ins, tables, outs, scratch)
    r = run_bass_kernel_spmd(nc, [arrays], core_ids=[0])
    return tuple(r.results[0]["out_" + name].reshape(shape) for name, (_, shape) in results.items())
```
